# Optimizing a Trainium2 kernel written in Bass

```python
import math
import jax, jax.numpy as jnp
from jax import lax
import numpy as np

D_MODEL = 1024
BATCH = 1
SEQ = 256
DEPTH = 2

GRID_W = 64
CTX_LEN = 256
EPS = 1e-6
ROPE_THETA = 10000.0
Q_BLOCK = 128

D_MIX = D_MODEL
DA_HEADS = 4
DA_QK = 32
DA_V = 2 * DA_QK
DA_WIDTH = DA_HEADS * DA_V
DA_IN = 2 * DA_HEADS * 2 * DA_QK + DA_HEADS * DA_V
SSD_HEADS = 8
SSD_P = 64
SSD_INNER = SSD_HEADS * SSD_P
SSD_GROUPS = 2
SSD_STATE = 64
SSD_CONV = 3
SSD_CHUNK = 128
SSD_CONV_DIM = SSD_INNER + 2 * SSD_GROUPS * SSD_STATE
SSD_IN = SSD_INNER + SSD_CONV_DIM + 2 * SSD_HEADS
MLA_HEADS = 4
MLA_Q_RANK = 256
MLA_KV_RANK = 128
MLA_NOPE = 64
MLA_ROPE = 32
MLA_V = 64
MLA_WIDTH = MLA_HEADS * MLA_V
MLA_IN = MLA_Q_RANK + MLA_KV_RANK + MLA_ROPE
MLA_SCALE = (MLA_NOPE + MLA_ROPE) ** -0.5
IN_WIDTH = DA_IN + SSD_IN + MLA_IN
N_EXPERTS = 16
N_GROUPS = 4
TOP_K = 2
D_EXPERT = 512

kernel_name = 'hybrid_dit_diffattn_ssd_mla_moe'

def rms_norm(x, g):
    xf = x.astype(jnp.float32)
    y = xf * lax.rsqrt(jnp.mean(xf * xf, axis=-1, keepdims=True) + EPS)
    return (y * g.astype(jnp.float32)).astype(x.dtype)

def ada_norm(x, g, shift, scale):
    return rms_norm(x, g) * (1 + scale) + shift

def axial_rope_tables(length, dim):
    rows = length // GRID_W
    row = jnp.repeat(jnp.arange(rows), GRID_W).astype(jnp.float32)
    col = jnp.tile(jnp.arange(GRID_W), rows).astype(jnp.float32)
    n_freq = dim // 4
    inv_freq = ROPE_THETA ** (-jnp.arange(n_freq, dtype=jnp.float32) / n_freq)
    ang = jnp.concatenate([row[:, None] * inv_freq, col[:, None] * inv_freq], axis=-1)
    return jnp.cos(ang), jnp.sin(ang)

def apply_rope(x, cos, sin):
    half = x.shape[-1] // 2
    shape = (1, x.shape[1]) + (1,) * (x.ndim - 3) + (half,)
    cos = cos.reshape(shape)
    sin = sin.reshape(shape)
    xf = x.astype(jnp.float32)
    x1, x2 = xf[..., :half], xf[..., half:]
    return jnp.concatenate([x1 * cos - x2 * sin, x2 * cos + x1 * sin], axis=-1).astype(x.dtype)

def sweep_query_blocks(fn, *qs):
    b, l = qs[0].shape[:2]
    nb = l // Q_BLOCK
    blocks = tuple(jnp.moveaxis(q.reshape((b, nb, Q_BLOCK) + q.shape[2:]), 1, 0) for q in qs)
    out = lax.map(lambda qb: fn(*qb), blocks)
    return jnp.moveaxis(out, 0, 1).reshape((b, l) + out.shape[3:])

def diff_attend(q, k, v, lam):
    s = jnp.einsum('bqhmd,bkhmd->bhmqk', q, k).astype(jnp.float32) * (DA_QK ** -0.5)
    p = jax.nn.softmax(s, axis=-1)
    a = p[:, :, 0] - lam * p[:, :, 1]
    return jnp.einsum('bhqk,bkhv->bqhv', a.astype(v.dtype), v)

def mla_attend(q_nope, q_rope, k_nope, k_rope, v):
    s = (jnp.einsum('bqhd,bkhd->bhqk', q_nope, k_nope)
         + jnp.einsum('bqhr,bkr->bhqk', q_rope, k_rope)).astype(jnp.float32) * MLA_SCALE
    p = jax.nn.softmax(s, axis=-1)
    return jnp.einsum('bhqk,bkhv->bqhv', p.astype(v.dtype), v)

def diff_attention_mixer(p_da, n_ctx, cos, sin, lam_vec, subln_g, lam_init):
    b, t, _ = p_da.shape
    q, k, v = jnp.split(p_da, 3, axis=-1)
    q = q.reshape(b, t, DA_HEADS, 2, DA_QK)
    k = k.reshape(b, t, DA_HEADS, 2, DA_QK)
    v = v.reshape(b, t, DA_HEADS, DA_V)
    lv = lam_vec.astype(jnp.float32)
    lam = jnp.exp(jnp.sum(lv[0] * lv[1])) - jnp.exp(jnp.sum(lv[2] * lv[3])) + lam_init
    q_c, q_x = q[:, :n_ctx], apply_rope(q[:, n_ctx:], cos, sin)
    k_c = k[:, :n_ctx]
    k_all = jnp.concatenate([k_c, apply_rope(k[:, n_ctx:], cos, sin)], axis=1)
    o_c = diff_attend(q_c, k_c, v[:, :n_ctx], lam)
    o_x = sweep_query_blocks(lambda qb: diff_attend(qb, k_all, v, lam), q_x)
    o = rms_norm(jnp.concatenate([o_c, o_x], axis=1), subln_g) * (1.0 - lam_init)
    return o.reshape(b, t, DA_WIDTH)

def depthwise_conv(u, w, bias):
    pad = SSD_CONV // 2
    y = lax.conv_general_dilated(u, w[:, None, :].astype(u.dtype), (1,), [(pad, pad)],
                                 dimension_numbers=('NWC', 'WIO', 'NWC'),
                                 feature_group_count=u.shape[-1])
    return y + bias

def ssd_chunked_scan(xh, dt, a, bm, cm, h0):
    b, l, h, p = xh.shape
    n = bm.shape[-1]
    q = SSD_CHUNK
    nc = l // q
    x_c = xh.reshape(b, nc, q, h, p)
    dt_c = dt.reshape(b, nc, q, h)
    b_c = bm.reshape(b, nc, q, h, n)
    c_c = cm.reshape(b, nc, q, h, n)
    a_cum = jnp.cumsum(dt_c * a, axis=2)
    seg = a_cum[:, :, :, None, :] - a_cum[:, :, None, :, :]
    lower = jnp.tril(jnp.ones((q, q), dtype=bool))[None, None, :, :, None]
    decay = jnp.exp(jnp.where(lower, seg, -jnp.inf))
    scores = jnp.einsum('bcihn,bcjhn->bcijh', c_c, b_c) * decay * dt_c[:, :, None, :, :]
    y_diag = jnp.einsum('bcijh,bcjhp->bcihp', scores, x_c)
    decay_to_end = jnp.exp(a_cum[:, :, -1:, :] - a_cum)
    states = jnp.einsum('bcjhn,bcjh,bcjhp->bchpn', b_c, decay_to_end * dt_c, x_c)
    chunk_decay = jnp.exp(a_cum[:, :, -1, :])

    def step(h_prev, inp):
        st, dec = inp
        return h_prev * dec[:, :, None, None] + st, h_prev

    h_final, h_in = lax.scan(step, h0, (jnp.moveaxis(states, 1, 0), jnp.moveaxis(chunk_decay, 1, 0)))
    h_in = jnp.moveaxis(h_in, 0, 1)
    y_off = jnp.einsum('bcihn,bchpn,bcih->bcihp', c_c, h_in, jnp.exp(a_cum))
    return (y_diag + y_off).reshape(b, l, h, p), h_final

def ssd_bidirectional(xbc, dt, a, d_skip, h0_fwd, h0_bwd):
    b, l, _ = xbc.shape
    u = xbc.astype(jnp.float32)
    rep = SSD_HEADS // SSD_GROUPS
    xh = u[..., :SSD_INNER].reshape(b, l, SSD_HEADS, SSD_P)
    gn = SSD_GROUPS * SSD_STATE
    bm = jnp.repeat(u[..., SSD_INNER:SSD_INNER + gn].reshape(b, l, SSD_GROUPS, SSD_STATE), rep, axis=2)
    cm = jnp.repeat(u[..., SSD_INNER + gn:].reshape(b, l, SSD_GROUPS, SSD_STATE), rep, axis=2)
    flip = lambda arr: jnp.flip(arr, axis=1)
    y_f, h_f = ssd_chunked_scan(xh, dt[:, :, 0], a[0], bm, cm, h0_fwd)
    y_b, h_b = ssd_chunked_scan(flip(xh), flip(dt[:, :, 1]), a[1], flip(bm), flip(cm), h0_bwd)
    y = y_f + flip(y_b) + d_skip.astype(jnp.float32)[:, None] * xh
    return y, h_f, h_b

def ssd_mixer(p_ssd, n_ctx, conv_w, conv_b, dt_bias, a_log, d_skip, norm_g):
    b, t, _ = p_ssd.shape
    z = p_ssd[..., :SSD_INNER]
    xbc = p_ssd[..., SSD_INNER:SSD_INNER + SSD_CONV_DIM]
    dt_raw = p_ssd[..., SSD_INNER + SSD_CONV_DIM:]
    a = -jnp.exp(a_log.astype(jnp.float32))
    dt = jax.nn.softplus(dt_raw.astype(jnp.float32).reshape(b, t, 2, SSD_HEADS) + dt_bias.astype(jnp.float32))
    xbc_c = jax.nn.silu(depthwise_conv(xbc[:, :n_ctx], conv_w, conv_b))
    xbc_x = jax.nn.silu(depthwise_conv(xbc[:, n_ctx:], conv_w, conv_b))
    h_zero = jnp.zeros((b, SSD_HEADS, SSD_P, SSD_STATE), jnp.float32)
    y_c, h_f, h_b = ssd_bidirectional(xbc_c, dt[:, :n_ctx], a, d_skip, h_zero, h_zero)
    y_x, _, _ = ssd_bidirectional(xbc_x, dt[:, n_ctx:], a, d_skip, h_f, h_b)
    y = jnp.concatenate([y_c, y_x], axis=1).reshape(b, t, SSD_INNER).astype(p_ssd.dtype)
    return rms_norm(y * jax.nn.silu(z), norm_g)

def mla_mixer(p_mla, n_ctx, cos, sin, q_norm_g, kv_norm_g, w_uq, w_ukv):
    b, t, _ = p_mla.shape
    cq = p_mla[..., :MLA_Q_RANK]
    ckv = p_mla[..., MLA_Q_RANK:MLA_Q_RANK + MLA_KV_RANK]
    kr = p_mla[..., MLA_Q_RANK + MLA_KV_RANK:]
    q = (rms_norm(cq, q_norm_g) @ w_uq).reshape(b, t, MLA_HEADS, MLA_NOPE + MLA_ROPE)
    kv = (rms_norm(ckv, kv_norm_g) @ w_ukv).reshape(b, t, MLA_HEADS, MLA_NOPE + MLA_V)
    q_nope, q_rope = q[..., :MLA_NOPE], q[..., MLA_NOPE:]
    k_nope, v = kv[..., :MLA_NOPE], kv[..., MLA_NOPE:]
    q_rope_x = apply_rope(q_rope[:, n_ctx:], cos, sin)
    k_rope = jnp.concatenate([kr[:, :n_ctx], apply_rope(kr[:, n_ctx:], cos, sin)], axis=1)
    o_c = mla_attend(q_nope[:, :n_ctx], q_rope[:, :n_ctx], k_nope[:, :n_ctx], k_rope[:, :n_ctx], v[:, :n_ctx])
    o_x = sweep_query_blocks(lambda qn, qr: mla_attend(qn, qr, k_nope, k_rope, v), q_nope[:, n_ctx:], q_rope_x)
    return jnp.concatenate([o_c, o_x], axis=1).reshape(b, t, MLA_WIDTH)

def moe_ffn(h, router_w, router_bias, w_gate, w_up, w_down):
    b, t, _ = h.shape
    per_group = N_EXPERTS // N_GROUPS
    aff = jax.nn.sigmoid((h @ router_w).astype(jnp.float32))
    sel = aff + router_bias.astype(jnp.float32)
    group_score = jnp.sum(lax.top_k(sel.reshape(b, t, N_GROUPS, per_group), 2)[0], axis=-1)
    best = jnp.argmax(group_score, axis=-1)
    in_group = jnp.repeat(jax.nn.one_hot(best, N_GROUPS, dtype=jnp.float32), per_group, axis=-1) > 0
    _, idx = lax.top_k(jnp.where(in_group, sel, -jnp.inf), TOP_K)
    w = jnp.take_along_axis(aff, idx, axis=-1)
    w = w / jnp.sum(w, axis=-1, keepdims=True)
    gates = jnp.einsum('btk,btke->bte', w, jax.nn.one_hot(idx, N_EXPERTS, dtype=jnp.float32)).astype(h.dtype)
    y = jnp.zeros_like(h)
    for e in range(N_EXPERTS):
        he = jax.nn.silu(h @ w_gate[e]) * (h @ w_up[e])
        y = y + gates[..., e:e + 1] * (he @ w_down[e])
    return y

def setup_inputs(seed: int = 0) -> dict:
    key = jax.random.key(seed)
    ks = jax.random.split(key, 32)
    f32 = jnp.float32
    nrm = lambda k, shape, s: jax.random.normal(k, shape, f32) * s
    gain = lambda k, shape: 1.0 + 0.02 * jax.random.normal(k, shape, f32)
    dt = jnp.exp(jax.random.uniform(ks[14], (DEPTH, 2, SSD_HEADS), f32, math.log(1e-3), math.log(1e-1)))
    return {
        'x': nrm(ks[0], (BATCH, SEQ, D_MODEL), 1.0),
        'c': nrm(ks[1], (BATCH, D_MODEL), 1.0),
        'ctx': nrm(ks[2], (BATCH, CTX_LEN, D_MODEL), 1.0),
        'c_ctx': nrm(ks[3], (D_MODEL,), 1.0),
        'norm_mix_g': gain(ks[4], (DEPTH, D_MODEL)),
        'norm_ffn_g': gain(ks[5], (DEPTH, D_MODEL)),
        'w_mod': nrm(ks[6], (DEPTH, D_MODEL, 6 * D_MODEL), 0.5 * D_MODEL ** -0.5),
        'b_mod': nrm(ks[7], (DEPTH, 6 * D_MODEL), 0.02),
        'w_in': nrm(ks[8], (DEPTH, D_MODEL, IN_WIDTH), D_MODEL ** -0.5),
        'w_out': nrm(ks[9], (DEPTH, D_MIX, D_MODEL), D_MIX ** -0.5),
        'da_lambda': nrm(ks[10], (DEPTH, 4, DA_QK), 0.1),
        'da_subln_g': gain(ks[11], (DEPTH, DA_V)),
        'ssd_conv_w': nrm(ks[12], (DEPTH, SSD_CONV, SSD_CONV_DIM), SSD_CONV ** -0.5),
        'ssd_conv_b': nrm(ks[13], (DEPTH, SSD_CONV_DIM), 0.02),
        'ssd_dt_bias': dt + jnp.log(-jnp.expm1(-dt)),
        'ssd_a_log': jnp.log(jax.random.uniform(ks[15], (DEPTH, 2, SSD_HEADS), f32, 1.0, 16.0)),
        'ssd_d': 1.0 + 0.1 * jax.random.normal(ks[16], (DEPTH, SSD_HEADS), f32),
        'ssd_norm_g': gain(ks[17], (DEPTH, SSD_INNER)),
        'mla_q_norm_g': gain(ks[18], (DEPTH, MLA_Q_RANK)),
        'mla_kv_norm_g': gain(ks[19], (DEPTH, MLA_KV_RANK)),
        'mla_w_uq': nrm(ks[20], (DEPTH, MLA_Q_RANK, MLA_HEADS * (MLA_NOPE + MLA_ROPE)), MLA_Q_RANK ** -0.5),
        'mla_w_ukv': nrm(ks[21], (DEPTH, MLA_KV_RANK, MLA_HEADS * (MLA_NOPE + MLA_V)), MLA_KV_RANK ** -0.5),
        'router_w': nrm(ks[22], (D_MODEL, N_EXPERTS), D_MODEL ** -0.5),
        'router_bias': nrm(ks[23], (N_EXPERTS,), 0.01),
        'exp_w_gate': nrm(ks[24], (DEPTH, N_EXPERTS, D_MODEL, D_EXPERT), D_MODEL ** -0.5),
        'exp_w_up': nrm(ks[25], (DEPTH, N_EXPERTS, D_MODEL, D_EXPERT), D_MODEL ** -0.5),
        'exp_w_down': nrm(ks[26], (DEPTH, N_EXPERTS, D_EXPERT, D_MODEL), D_EXPERT ** -0.5),
        'final_norm_g': gain(ks[27], (D_MODEL,)),
    }

def reference(x, c, ctx, c_ctx, norm_mix_g, norm_ffn_g, w_mod, b_mod, w_in, w_out, da_lambda, da_subln_g,
              ssd_conv_w, ssd_conv_b, ssd_dt_bias, ssd_a_log, ssd_d, ssd_norm_g, mla_q_norm_g, mla_kv_norm_g,
              mla_w_uq, mla_w_ukv, router_w, router_bias, exp_w_gate, exp_w_up, exp_w_down, final_norm_g):
    n_ctx = ctx.shape[1]
    n_lat = x.shape[1]
    da_cos, da_sin = axial_rope_tables(n_lat, DA_QK)
    mla_cos, mla_sin = axial_rope_tables(n_lat, MLA_ROPE)
    c_act = jax.nn.silu(c)
    cc_act = jax.nn.silu(c_ctx)
    hx, hc = x, ctx
    for i in range(DEPTH):
        lam_init = 0.8 - 0.6 * math.exp(-0.3 * i)
        mod_x = jnp.split((c_act @ w_mod[i] + b_mod[i])[:, None, :], 6, axis=-1)
        mod_c = jnp.split(cc_act @ w_mod[i] + b_mod[i], 6, axis=-1)
        u = jnp.concatenate([ada_norm(hc, norm_mix_g[i], mod_c[0], mod_c[1]),
                             ada_norm(hx, norm_mix_g[i], mod_x[0], mod_x[1])], axis=1)
        proj = u @ w_in[i]
        o_da = diff_attention_mixer(proj[..., :DA_IN], n_ctx, da_cos, da_sin, da_lambda[i], da_subln_g[i], lam_init)
        o_ssd = ssd_mixer(proj[..., DA_IN:DA_IN + SSD_IN], n_ctx, ssd_conv_w[i], ssd_conv_b[i],
                          ssd_dt_bias[i], ssd_a_log[i], ssd_d[i], ssd_norm_g[i])
        o_mla = mla_mixer(proj[..., DA_IN + SSD_IN:], n_ctx, mla_cos, mla_sin, mla_q_norm_g[i], mla_kv_norm_g[i],
                          mla_w_uq[i], mla_w_ukv[i])
        mix = jnp.concatenate([o_da, o_ssd, o_mla], axis=-1) @ w_out[i]
        hc = hc + mod_c[2] * mix[:, :n_ctx]
        hx = hx + mod_x[2] * mix[:, n_ctx:]
        u_x = ada_norm(hx, norm_ffn_g[i], mod_x[3], mod_x[4])
        if i < DEPTH - 1:
            u_c = ada_norm(hc, norm_ffn_g[i], mod_c[3], mod_c[4])
            y = moe_ffn(jnp.concatenate([u_c, u_x], axis=1), router_w, router_bias,
                        exp_w_gate[i], exp_w_up[i], exp_w_down[i])
            hc = hc + mod_c[5] * y[:, :n_ctx]
            y_x = y[:, n_ctx:]
        else:
            y_x = moe_ffn(u_x, router_w, router_bias, exp_w_gate[i], exp_w_up[i], exp_w_down[i])
        hx = hx + mod_x[5] * y_x
    return rms_norm(hx, final_norm_g)


_drawn_inputs = setup_inputs


def setup_inputs(seed=0):
    import zlib

    import numpy as np

    out = dict(_drawn_inputs(seed))
    spreads = {}
    factors = {'ssd_norm_g': 2.79,
     'mla_q_norm_g': 8.0,
     'mla_kv_norm_g': 8.0,
     'final_norm_g': 9.648,
     'da_subln_g': 6.27}
    for name, (base, spread) in spreads.items():
        noise = np.random.default_rng([zlib.crc32(name.encode()), seed]).standard_normal(out[name].shape)
        drawn = base * np.exp(spread * noise) if base else spread * noise
        out[name] = __import__('jax').numpy.asarray(drawn.astype(out[name].dtype))
    for name, factor in factors.items():
        out[name] = (out[name] * factor).astype(out[name].dtype)
    return out
```

```python
import math
from contextlib import ExitStack

import numpy as np

import concourse.bass as bass
from concourse import mybir

ALU = mybir.AluOpType
ACT = mybir.ActivationFunctionType
F32 = mybir.dt.float32
AX = mybir.AxisListType

P = 128
DM = 1024
KT = DM // P
NCTX, NLAT = 256, 256
T = NCTX + NLAT
TT = T // P
DEPTH = 2
GRID_W = 64
EPS = 1e-6
DA_H, DA_QK, DA_V = 4, 32, 64
SSD_H, SSD_P, SSD_N, SSD_INNER = 8, 64, 64, 512
QR, KVR = 256, 128
NOPE, ROPE = 64, 32
HD = NOPE + ROPE
IN_W = 2480
COL_QK, COL_V, COL_Z, COL_X, COL_BC, COL_DT = 0, 512, 768, 1280, 1792, 2048
NE, NG, DE = 16, 4, 512
DA_SCALE = DA_QK ** -0.5
MLA_SCALE = HD ** -0.5

V_BMOD, V_GMIX, V_GFFN, V_CONVW, V_CONVB, V_QG, V_KVG, V_FING, V_SSDG, V_SUBG, V_CCTX, V_C, NVEC = (
    0, 48, 56, 64, 82, 88, 90, 91, 99, 103, 104, 112, 120)
B_DTB, B_ALOG, B_D, B_LAM, B_RB, NB = 0, 16, 32, 40, 168, 184
C_ID, C_MF, C_MB, C_ROT, C_COS, C_SIN, C_MROT, C_MCOS, C_MSIN, C_PE, C_PG, NCONST = (
    0, 128, 256, 384, 512, 768, 1024, 1152, 1408, 1664, 1680, 1684)

RING = 4
SLOT = 4096
PER_EXPERT = 3
GROUP = 4


def shape_constants():
    c = np.zeros((P, NCONST), np.float32)
    i = np.arange(P)
    c[:, C_ID:C_ID + P] = np.eye(P)
    c[:, C_MF:C_MF + P] = i[:, None] <= i[None, :]
    c[:, C_MB:C_MB + P] = i[:, None] >= i[None, :]
    half = DA_QK // 2
    for m in range(P):
        if m % DA_QK < half:
            c[m + half, C_ROT + m] = -1.0
        else:
            c[m - half, C_ROT + m] = 1.0
    rows = NLAT // GRID_W
    row = np.repeat(np.arange(rows), GRID_W).astype(np.float32)
    col = np.tile(np.arange(GRID_W), rows).astype(np.float32)
    nf = DA_QK // 4
    inv = np.float32(10000.0) ** (-np.arange(nf, dtype=np.float32) / np.float32(nf))
    ang = np.concatenate([row[:, None] * inv, col[:, None] * inv], axis=-1)
    cos, sin = np.cos(ang).T, np.sin(ang).T
    for m in range(P):
        c[m, C_COS:C_COS + NLAT] = cos[m % half]
        c[m, C_SIN:C_SIN + NLAT] = sin[m % half]
    c[:NOPE, C_MCOS:C_MCOS + NLAT] = 1.0
    c[NOPE:HD, C_MCOS:C_MCOS + NLAT] = c[NOPE:HD, C_COS:C_COS + NLAT]
    c[NOPE:HD, C_MSIN:C_MSIN + NLAT] = c[NOPE:HD, C_SIN:C_SIN + NLAT]
    c[NOPE:HD, C_MROT + NOPE:C_MROT + HD] = c[NOPE:HD, C_ROT + NOPE:C_ROT + HD]
    c[:, C_PE:C_PE + NE] = NE - np.arange(NE)
    c[:, C_PG:C_PG + NG] = NG - np.arange(NG)
    return c


def lam_init(layer):
    return 0.8 - 0.6 * math.exp(-0.3 * layer)


def attention_units(layer):
    return [(kind, t, hh, NCTX if P * t < NCTX else T)
            for t in range(0 if layer == 0 else NCTX // P, TT) for kind in ("da", "ml") for hh in range(DA_H)]


def state_steps(layer):
    return [(0, 0, 1), (1, 1, 0), (0, 1, 2), (1, 0, 3), (0, 2, 3), (1, 3, 2)]


class Tally:

    def __init__(self, sem):
        self.sem, self.n = sem, 0

    def by(self, instruction):
        instruction.then_inc(self.sem, 1)
        self.n += 1
        return self.n


def hybrid_dit_kernel(nc, consts, x, c, ctx, c_ctx, norm_mix_g, norm_ffn_g, w_mod, b_mod, w_in, w_out, da_lambda,
                      da_subln_g, ssd_conv_w, ssd_conv_b, ssd_dt_bias, ssd_a_log, ssd_d, ssd_norm_g, mla_q_norm_g,
                      mla_kv_norm_g, mla_w_uq, mla_w_ukv, router_w, router_bias, exp_w_gate, exp_w_up, exp_w_down,
                      final_norm_g, out):
    with ExitStack() as stack:
        def sb(name, *shape):
            return stack.enter_context(nc.sbuf_tensor(name, list(shape), F32))

        sems = {}

        def S(name, layer=None):
            key = name if layer is None else f"{name}_{layer}"
            if key not in sems:
                sems[key] = stack.enter_context(nc.semaphore(key))
            return sems[key]

        cst = sb("cst", P, NCONST)
        ident = cst[:, C_ID:C_ID + P]
        tri = [cst[:, C_MF:C_MF + P], cst[:, C_MB:C_MB + P]]
        ones = sb("ones", P, P)
        ones_mean = sb("ones_mean", P, P)
        h = sb("h", P, KT, T)
        u = sb("u", P, KT, T)
        ring = sb("ring", P, RING, SLOT)
        vecrows = sb("vecrows", P, DEPTH, P)
        vec = sb("vec", P, DEPTH, NVEC)
        bcast = sb("bcast", P, DEPTH, NB)
        cond = sb("cond", P, KT, 32)
        modrow = sb("modrow", P, 512)
        mod = sb("mod", P, DEPTH, 48, 2)
        gain = sb("gain", P, DEPTH, 2, KT, 2)
        wuq = sb("wuq", P, 2, DA_H * HD)
        wukv = sb("wukv", P, 512)
        rw = sb("rw", P, KT, NE)
        rstd = sb("rstd", P, T)
        small = sb("small", P, 64)
        rt = sb("rt", P, 12, TT, NE)
        gates = sb("gates", P, TT, NE)
        arena = sb("arena", P, 21760)

        at = [0]

        def take(n, where=None):
            a = at[0] if where is None else where
            if where is None:
                at[0] += n
            return arena[:, a:a + n]

        xbc = take(6 * T).rearrange("p (m t) -> p m t", t=T)
        v_da = take(TT * 256).rearrange("p (t n) -> p t n", n=256)
        z = take(TT * 512).rearrange("p (t n) -> p t n", n=512)
        qk = take(4 * T).rearrange("p (m t) -> p m t", t=T)
        qm = take(4 * T).rearrange("p (h t) -> p h t", t=T)
        km = take(4 * T).rearrange("p (h t) -> p h t", t=T)
        v_ml = take(TT * 256).rearrange("p (t n) -> p t n", n=256)
        b_tok = take(TT * P).rearrange("p (t n) -> p t n", n=P)
        state = take(2 * TT * 256).rearrange("p (d t n) -> p d t n", d=2, n=256)
        tmp_at = at[0]
        ew = take(2 * 1024).rearrange("p (d h i) -> p d h i", d=2, i=P)
        xdt = take(2 * 512).rearrange("p (d n) -> p d n", d=2)
        gm = take(512).rearrange("p (d g i) -> p d g i", d=2, i=P)
        y_acc = take(512)
        y_two = take(512)
        y_skip = take(512)
        sc = take(64 * 12).rearrange("p (k n) -> p k n", n=64)
        assert at[0] <= 21760, at[0]
        probs = take(2048, tmp_at).rearrange("p (b m k) -> p b m k", b=2, m=2)
        probs_t = take(1024, tmp_at + 2048).rearrange("p (b k q) -> p b k q", b=2, q=P)
        stats = take(4 * 64, tmp_at + 3072).rearrange("p (s u m) -> p s u m", s=4, m=2)
        o_sb = take(512, tmp_at + 3328).rearrange("p (k n) -> p k n", n=256)
        o_sq = take(256, tmp_at + 3840)
        latent = take(3 * T, tmp_at).rearrange("p (m t) -> p m t", t=T)
        latent_sq = take(3 * T, tmp_at + 3 * T).rearrange("p (m t) -> p m t", t=T)
        r_lat = take(2 * T, tmp_at + 6 * T).rearrange("p (m t) -> p m t", t=T)
        rope_tmp = take(256, tmp_at + 8 * T)
        assert tmp_at + 8 * T + 256 <= 21760
        y_tok = take(TT * DM, 0).rearrange("p (t n) -> p t n", n=DM)
        silu_g = take(2 * DE, TT * DM).rearrange("p (b n) -> p b n", b=2)
        hid = take(2 * DE, TT * DM + 2 * DE).rearrange("p (b n) -> p b n", b=2)
        hid_t = take(2 * DE, TT * DM + 4 * DE).rearrange("p (b f t) -> p b f t", b=2, t=P)
        tok = y_tok

        ps = stack.enter_context(nc.psum_tensor("ps", [P, 8, 512], F32))

        chunks = []
        for g in range(3):
            chunks += [("mod", 0, g, k) for k in range(4)]
            if g == 0:
                chunks += [("in", 0, n, 0) for n in ("x", "bcv", "dtm", "qk", "z")]
        chunks += [("mod", 1, g, k) for g in range(3) for k in range(4)]
        chunks += [("out", 0, n, 0) for n in range(2)]
        moe_base = [len(chunks)]
        after = [("in", 1, n, 0) for n in ("x", "bcv", "dtm", "qk", "z")] + [("out", 1, n, 0) for n in range(2)]
        second = len(chunks) + NE * PER_EXPERT
        moe_base.append(second + len(after))
        ring_at = {k: i for i, k in enumerate(chunks)}
        ring_at.update({k: second + i for i, k in enumerate(after)})
        landed = [S(f"ring_landed{s}") for s in range(RING)]
        pairs = [i for k, i in ring_at.items() if k[2] == "bcv"]

        def landed_count(i):
            return 16 * (i // RING + 1 + sum(1 for j in pairs if j <= i and j % RING == i % RING))

        NU = [GROUP * TT, GROUP * 2]
        FIRST_T = [0, 2]
        IN_COLS = {"x": (COL_X, 512), "qk": (COL_QK, 512), "z": (COL_Z, 512), "dtm": (COL_DT, 432)}

        entry = {}
        released = {}
        filled, evacuated = S("bank_filled"), S("bank_evacuated")

        vec_loads, bcast_loads = [], []
        for l in range(DEPTH):
            for row, n, src in ((V_BMOD, 48, b_mod[l].rearrange("(r p) -> r p", p=P)),
                                (V_GMIX, 8, norm_mix_g[l].rearrange("(r p) -> r p", p=P)),
                                (V_GFFN, 8, norm_ffn_g[l].rearrange("(r p) -> r p", p=P)),
                                (V_CONVW, 6, ssd_conv_w[l, 0].rearrange("(r p) -> r p", p=P)),
                                (V_CONVW + 6, 6, ssd_conv_w[l, 1].rearrange("(r p) -> r p", p=P)),
                                (V_CONVW + 12, 6, ssd_conv_w[l, 2].rearrange("(r p) -> r p", p=P)),
                                (V_CONVB, 6, ssd_conv_b[l].rearrange("(r p) -> r p", p=P)),
                                (V_QG, 2, mla_q_norm_g[l].rearrange("(r p) -> r p", p=P)),
                                (V_KVG, 1, mla_kv_norm_g[l].rearrange("(r p) -> r p", p=P)),
                                (V_FING, 8, final_norm_g.rearrange("(r p) -> r p", p=P)),
                                (V_SSDG, 4, ssd_norm_g[l].rearrange("(r p) -> r p", p=P)),
                                (V_CCTX, 8, c_ctx.rearrange("(r p) -> r p", p=P)),
                                (V_C, 8, c[0].rearrange("(r p) -> r p", p=P))):
                vec_loads.append((vecrows[row:row + n, l, :], src))
            for a in range(2):
                vec_loads.append((vecrows[V_SUBG:V_SUBG + 1, l, 64 * a:64 * a + 64],
                                  da_subln_g[l].rearrange("(r p) -> r p", r=1)))
            for at_b, n, src in ((B_DTB, 16, ssd_dt_bias[l].rearrange("a n -> (a n)")),
                                 (B_ALOG, 16, ssd_a_log[l].rearrange("a n -> (a n)")),
                                 (B_D, 8, ssd_d[l]), (B_LAM, 128, da_lambda[l].rearrange("a n -> (a n)")),
                                 (B_RB, 16, router_bias)):
                bcast_loads.append((bcast[:, l, at_b:at_b + n], src.partition_broadcast(P)))
        n_vec_dmas, n_bcast_dmas = len(vec_loads), len(bcast_loads) + 1

        block = stack.enter_context(nc.Block())

        @block.tensor
        def _(pe):
            def wait_chunk(key):
                i = ring_at[key]
                pe.wait_ge(landed[i % RING], landed_count(i))
                return ring[:, i % RING, :]

            def open_bank(name):
                i = len(entry)
                entry[name] = i
                if i >= 2:
                    pe.wait_ge(evacuated, i - 1)
                return ps[:, i % 2, :]

            def close_bank(last):
                last.then_inc(filled, 1)

            def read_back(name):
                pe.wait_ge(evacuated, entry[name] + 1)

            def tr(dst, src):
                n = src.shape[0]
                return nc.tensor.transpose(dst, src, ident[0:n, 0:n])

            def modulation(l, g):
                bank = open_bank(f"mod{l}{g}")
                for kk in range(4):
                    w = wait_chunk(("mod", l, g, kk)).rearrange("p (k n) -> p k n", k=2)
                    for k2 in range(2):
                        k = 2 * kk + k2
                        for j in range(4):
                            last = nc.tensor.matmul(bank[32 * j:32 * j + 32, :], cond[:, k, :],
                                                    w[:, k2, 512 * j:512 * j + 512], start=(k == 0), stop=(k == 7),
                                                    tile_position=(0, 32 * j))
                    if kk < 3:
                        last.then_inc(S("mod_chunk_used"), 1)
                        mod_used[0] += 1
                        released[ring_at[("mod", l, g, kk)]] = (S("mod_chunk_used"), mod_used[0])
                close_bank(last)
                released[ring_at[("mod", l, g, 3)]] = (filled, entry[f"mod{l}{g}"] + 1)
                read_back(f"mod{l}{g}")
                bank = open_bank(f"modT{l}{g}")
                for s in range(4):
                    last = tr(bank[:, P * s:P * s + P], modrow[:, P * s:P * s + P])
                close_bank(last)

            mod_used = [0]

            def mean_square(name, ready, src, n, c0):
                bank = open_bank(name)
                for k in range(n):
                    pe.wait_ge(ready[0], ready[1] + k + 1)
                    last = nc.tensor.matmul(bank[:, 0:T - c0], ones_mean[:, :], src[:, k, c0:T], start=(k == 0),
                                            stop=(k == n - 1))
                close_bank(last)

            def feature_major(name, w, n, c0, ready=None, width=P, row=0):
                bank = open_bank(name)
                for k in range(KT):
                    if ready is not None:
                        pe.wait_ge(ready, 2 * (k + 1))
                    last = nc.tensor.matmul(bank[row:row + width, 0:T - c0], w[:, k, n:n + width], u[:, k, c0:T],
                                            start=(k == 0), stop=(k == KT - 1))
                close_bank(last)

            def token_major(name, w, n, width, tiles):
                bank = open_bank(name)
                for i, t in enumerate(tiles):
                    for k in range(KT):
                        last = nc.tensor.matmul(bank[:, i * width:(i + 1) * width], u[:, k, P * t:P * t + P],
                                                w[:, k, n:n + width], start=(k == 0), stop=(k == KT - 1))
                close_bank(last)

            def in_chunk(l, n):
                width = 432 if n == "dtm" else 512
                w = wait_chunk(("in", l, n, 0))
                return w[:, 0:KT * width].rearrange("p (k n) -> p k n", n=width)

            def free_chunk(key, name):
                released[ring_at[key]] = (filled, entry[name] + 1)

            def project(l):
                first = FIRST_T[l]
                w = in_chunk(l, "x")
                for m in range(4):
                    feature_major(f"xbc{l}{m}", w, P * m, 0, S("u_ready", f"{l}mix") if m == 0 else None)
                free_chunk(("in", l, "x", 0), f"xbc{l}3")
                w = in_chunk(l, "bcv")
                for m in range(2):
                    feature_major(f"xbc{l}{4 + m}", w, P * m, 0)
                for i in range(2):
                    token_major(f"v{l}{i}", w, 256, 256, [2 * i, 2 * i + 1])
                free_chunk(("in", l, "bcv", 0), f"v{l}1")
                w = in_chunk(l, "dtm")
                token_major(f"dt{l}", w, 0, 16, range(TT))
                for m in range(3):
                    feature_major(f"lat{l}{m}", w, 16 + P * m, 0)
                feature_major(f"kr{l}", w, 16 + QR + KVR, 0, width=ROPE, row=NOPE)
                free_chunk(("in", l, "dtm", 0), f"kr{l}")
                w = in_chunk(l, "qk")
                for m in range(4):
                    feature_major(f"qk{l}{m}", w, P * m, 0 if m >= 2 or l == 0 else NCTX)
                free_chunk(("in", l, "qk", 0), f"qk{l}3")
                w = in_chunk(l, "z")
                for t in range(first, TT):
                    token_major(f"z{l}{t}", w, 0, 512, [t])
                free_chunk(("in", l, "z", 0), f"z{l}{TT - 1}")

            def latents_up(l):
                c0 = P * FIRST_T[l]
                mean_square(f"cqms{l}", (S("latent_sq", l), 0), latent_sq, 2, c0)
                mean_square(f"ckvms{l}", (S("latent_sq", l), 2), latent_sq[:, 2:3, :], 1, 0)
                pe.wait_ge(S("wu_landed"), 32 * (l + 1))
                pe.wait_ge(S("latent_normed", l), 3)
                for hh in range(DA_H):
                    bank = open_bank(f"qm{l}{hh}")
                    for m in range(2):
                        last = nc.tensor.matmul(bank[0:HD, 0:T - c0], wuq[:, m, HD * hh:HD * hh + HD],
                                                latent[:, m, c0:T], start=(m == 0), stop=(m == 1))
                    close_bank(last)
                for hh in range(DA_H):
                    bank = open_bank(f"km{l}{hh}")
                    close_bank(nc.tensor.matmul(bank[0:NOPE, :], wukv[:, P * hh:P * hh + NOPE], latent[:, 2, :],
                                                start=True, stop=True))
                wv = wukv[:, :].rearrange("p (h n) -> p h n", n=P)[:, :, NOPE:P]
                for i in range(2):
                    bank = open_bank(f"vm{l}{i}")
                    for j in range(2):
                        t = 2 * i + j
                        last = nc.tensor.matmul(bank[:, 256 * j:256 * j + 256].rearrange("p (h n) -> p h n", h=4),
                                                latent[:, 2, P * t:P * t + P], wv,
                                                start=True, stop=True)
                    close_bank(last)

            def rotate(l):
                for m in range(4):
                    read_back(f"qk{l}{m}")
                    bank = open_bank(f"qkrot{l}{m}")
                    close_bank(nc.tensor.matmul(bank[:, 0:NLAT], cst[:, C_ROT:C_ROT + P], qk[:, m, NCTX:T],
                                                start=True, stop=True))
                for hh in range(DA_H):
                    read_back(f"qm{l}{hh}")
                    bank = open_bank(f"qmrot{l}{hh}")
                    close_bank(nc.tensor.matmul(bank[0:HD, 0:NLAT], cst[0:HD, C_MROT:C_MROT + HD],
                                                qm[0:HD, hh, NCTX:T], start=True, stop=True))
                read_back(f"kr{l}")
                bank = open_bank(f"krrot{l}")
                close_bank(nc.tensor.matmul(bank[NOPE:HD, 0:NLAT],
                                            cst[NOPE:HD, C_ROT + NOPE:C_ROT + HD], km[NOPE:HD, 0, NCTX:T],
                                            start=True, stop=True))

            def scan(l):
                first = FIRST_T[l]
                pe.wait_ge(S("xbc_ready", l), 6)
                for t in range(TT):
                    bank = open_bank(f"xs{l}{t}")
                    for m in range(4):
                        last = tr(bank[:, P * m:P * m + P], xbc[:, m, P * t:P * t + P])
                    close_bank(last)
                bank = open_bank(f"btok{l}")
                for t in range(TT):
                    last = tr(bank[:, P * t:P * t + P], xbc[:, 4, P * t:P * t + P])
                close_bank(last)
                pe.wait_ge(S("da_ready", l), 1)
                bank = open_bank(f"cum{l}")
                for d in range(2):
                    nc.tensor.matmul(bank[:, 32 * d:32 * d + 32], tri[d], sc[:, 2, 32 * d:32 * d + 32], start=True,
                                     stop=True)
                close_bank(nc.tensor.matmul(bank[:, 64:128], ones[:, :], sc[:, 2, :], start=True, stop=True))
                read_back(f"btok{l}")
                for n, (d, t, _) in enumerate(state_steps(l)):
                    pe.wait_ge(S("xde_ready", l), n + 1)
                    bank = open_bank(f"state{l}{n}")
                    for g in range(2):
                        last = nc.tensor.matmul(bank[64 * g:64 * g + 64, 0:256], b_tok[:, t, 64 * g:64 * g + 64],
                                                xdt[:, n % 2, 256 * g:256 * g + 256], start=True, stop=True)
                    close_bank(last)
                for i, t in enumerate(range(first, TT)):
                    for g in range(2):
                        bank = open_bank(f"cb{l}{t}{g}")
                        r = slice(64 * g, 64 * g + 64)
                        last = nc.tensor.matmul(bank[:, 0:P], xbc[r, 4, P * t:P * t + P],
                                                xbc[r, 5, P * t:P * t + P], start=True, stop=True)
                        close_bank(last)
                    for d in range(2):
                        n = 2 * i + d
                        pe.wait_ge(S("rows_built", l), n + 1)
                        if n >= 1:
                            pe.wait_ge(S("decay_clamped", l), n)
                        for b in range(2):
                            last = nc.tensor.matmul(ps[:, 2 + b, :], ones[:, :], 
                                                    ew[:, d, 4 * b:4 * b + 4, :].rearrange("p h i -> p (h i)"),
                                                    start=True, stop=True)
                        last.then_inc(S("rows_cast", l), 1)
                    if i == 0:
                        pe.wait_ge(S("states_done", l), 1)
                    else:
                        pe.wait_ge(S("y_banks_read", l), i)
                    for d in range(2):
                        pe.wait_ge(S("w_ready", l), 2 * i + d + 1)
                        for hh in range(SSD_H):
                            last = nc.tensor.matmul(ps[:, 4, 64 * hh:64 * hh + 64], ew[:, d, hh, :],
                                                    xdt[:, d, 64 * hh:64 * hh + 64], start=(d == 0 and hh == 0),
                                                    stop=(d == 1 and hh == 7), skip_group_check=True)
                        for g in range(2):
                            r = slice(64 * g, 64 * g + 64)
                            last = nc.tensor.matmul(ps[:, 5 + g, 256 * d:256 * d + 256], xbc[r, 5, P * t:P * t + P],
                                                    state[r, d, t, :], start=True, stop=True)
                    last.then_inc(S("y_summed", l), 1)
                    if i > 0:
                        y_transposes(l, t - 1, i)
                y_transposes(l, TT - 1, TT - first)

            def y_transposes(l, t, count):
                pe.wait_ge(S("y_normed", l), count)
                bank = open_bank(f"yT{l}{t}")
                for m in range(4):
                    last = tr(bank[:, P * m:P * m + P], y_acc[:, P * m:P * m + P])
                close_bank(last)

            def attention(l):
                units = attention_units(l)
                pe.wait_ge(S("roped", l), 1)
                groups = 0
                for s in range(len(units) + 2):
                    if s < len(units):
                        kind, t, hh, nk = units[s]
                        if s >= 2:
                            pe.wait_ge(S("exp_done", l), s - 1)
                        pair = 2 + 2 * (s % 2)
                        if kind == "da":
                            r0 = 64 * (hh % 2)
                            for m in range(2):
                                r = slice(r0 + 32 * m, r0 + 32 * m + 32)
                                last = nc.tensor.matmul(ps[:, pair + m, 0:nk], qk[r, hh // 2, P * t:P * t + P],
                                                        qk[r, 2 + hh // 2, 0:nk], start=True, stop=True)
                        else:
                            last = nc.tensor.matmul(ps[:, pair, 0:nk], qm[0:HD, hh, P * t:P * t + P],
                                                    km[0:HD, hh, 0:nk], start=True, stop=True)
                        last.then_inc(S("scores_done", l), 1)
                    if 1 <= s <= len(units):
                        n = s - 1
                        kind, t, hh, nk = units[n]
                        if kind == "da":
                            pe.wait_ge(S("mixed", l), sum(1 for x in units[:n + 1] if x[0] == "da"))
                        else:
                            pe.wait_ge(S("exp_done", l), n + 1)
                        if n >= 2:
                            pe.wait_ge(S("probs_t_ready", l), n - 1)
                        for k in range(nk // P):
                            last = tr(ps[:, 6 + n % 2, P * k:P * k + P], probs[:, n % 2, 0, P * k:P * k + P])
                        last.then_inc(S("probs_turned", l), 1)
                    if s >= 2:
                        n = s - 2
                        kind, t, hh, nk = units[n]
                        if hh == 0:
                            o_bank = open_bank(f"o{kind}{l}{t}")
                        pe.wait_ge(S("probs_t_ready", l), n + 1)
                        v = v_da if kind == "da" else v_ml
                        for k in range(nk // P):
                            last = nc.tensor.matmul(o_bank[:, 64 * hh:64 * hh + 64], probs_t[:, n % 2, k, :],
                                                    v[:, k, 64 * hh:64 * hh + 64], start=(k == 0),
                                                    stop=(k == nk // P - 1))
                        if hh == DA_H - 1:
                            close_bank(last)
                            groups += 1
                            head_out(l, kind, t, groups)
                        else:
                            last.then_inc(S("heads_done", l), 1)

            def head_out(l, kind, t, count):
                pe.wait_ge(S("o_ready", l), count)
                bank = open_bank(f"oT{kind}{l}{t}")
                for m in range(2):
                    last = tr(bank[:, P * m:P * m + P], o_sb[:, kind == "ml", P * m:P * m + P])
                close_bank(last)

            def out_projection(l):
                c0 = P * FIRST_T[l]
                pe.wait_ge(evacuated, len(entry))
                for n in range(2):
                    w = wait_chunk(("out", l, n, 0)).rearrange("p (k n) -> p k n", n=512)
                    for m in range(4):
                        name = f"mix{l}{4 * n + m}"
                        bank = open_bank(name)
                        for k in range(KT):
                            last = nc.tensor.matmul(bank[:, 0:T - c0], w[:, k, P * m:P * m + P], u[:, k, c0:T],
                                                    start=(k == 0), stop=(k == KT - 1))
                        close_bank(last)
                    free_chunk(("out", l, n, 0), name)

            def router(l):
                bank = open_bank(f"logits{l}")
                for i, t in enumerate(range(FIRST_T[l], TT)):
                    for k in range(KT):
                        if i == 0:
                            pe.wait_ge(S("u_ready", f"{l}ffn"), (2 if l == 0 else 1) * (k + 1))
                        last = nc.tensor.matmul(bank[:, NE * t:NE * t + NE], u[:, k, P * t:P * t + P], rw[:, k, :],
                                                start=(k == 0), stop=(k == KT - 1))
                close_bank(last)

            def experts(l):
                tiles = TT - FIRST_T[l]
                nu, base = NU[l], moe_base[l]
                pe.wait_ge(evacuated, len(entry))
                with pe.Fori(0, NE // GROUP) as it:
                    def slot(c):
                        return (base + c) % RING

                    def wait_slot(c):
                        pe.wait_ge(landed[slot(c)], it * (16 * GROUP * PER_EXPERT // RING) + landed_count(base + c))

                    def gate_up(n):
                        e, i = n // tiles, n % tiles
                        t = FIRST_T[l] + i
                        for j in range(2):
                            if i == 0:
                                wait_slot(PER_EXPERT * e + j)
                            w = ring[:, slot(PER_EXPERT * e + j), :].rearrange("p (k n) -> p k n", n=DE)
                            for k in range(KT):
                                last = nc.tensor.matmul(ps[:, 2 * (n % 2) + j, :], u[:, k, P * t:P * t + P],
                                                        w[:, k, :], start=(k == 0), stop=(k == KT - 1))
                        last.then_inc(S("gate_up_done", l), 1)

                    gate_up(0)
                    for n in range(nu):
                        e, i = n // tiles, n % tiles
                        if n + 1 < nu:
                            gate_up(n + 1)
                        pe.wait_ge(S("hid_ready", l), it * nu + (n + 1))
                        for f in range(4):
                            last = tr(ps[:, 4 + n % 2, P * f:P * f + P], hid[:, n % 2, P * f:P * f + P])
                        last.then_inc(S("hid_turned", l), 1)
                        pe.wait_ge(S("hid_t_ready", l), it * nu + (n + 1))
                        pe.wait_ge(S("y_added", l), it * nu + (n + 1))
                        if i == 0:
                            wait_slot(PER_EXPERT * e + 2)
                        w = ring[:, slot(PER_EXPERT * e + 2), :].rearrange("p (f n) -> p f n", n=DM)
                        for b in range(2):
                            for f in range(4):
                                last = nc.tensor.matmul(ps[:, 6 + b, :], hid_t[:, n % 2, f, :],
                                                        w[:, f, 512 * b:512 * b + 512], start=(f == 0), stop=(f == 3))
                        last.then_inc(S("down_done", l), 1)

            def add_experts(l):
                tiles = range(FIRST_T[l], TT)
                pe.wait_ge(S("y_added", l), NE * len(tiles) + 1)
                for m in range(KT):
                    bank = open_bank(f"y{l}{m}")
                    for t in tiles:
                        last = tr(bank[:, P * t:P * t + P], y_tok[:, t, P * m:P * m + P])
                    close_bank(last)

            pe.wait_ge(S("const_landed"), 16 * (1 + n_vec_dmas))
            pe.wait_ge(S("ones_ready"), 2)
            bank = open_bank("vecs")
            for l in range(DEPTH):
                last = tr(bank[:, P * l:P * l + NVEC], vecrows[0:NVEC, l, :])
            close_bank(last)
            pe.wait_ge(S("tokens_landed"), 32)
            for t in range(TT):
                for half in range(2):
                    bank = open_bank(f"h{t}{half}")
                    for m in range(4):
                        last = tr(bank[:, P * m:P * m + P], tok[:, t, 512 * half + P * m:512 * half + P * m + P])
                    close_bank(last)
            for l in range(DEPTH):
                sq = S("squares", f"{l}mix")
                mean_square(f"ms{l}mix", (sq, 0), u, KT, 0)
                if l == 0:
                    pe.wait_ge(S("cond_ready"), 1)
                    modulation(0, 0)
                project(l)
                if l == 0:
                    for g in (1, 2):
                        modulation(0, g)
                    for g in range(3):
                        modulation(1, g)
                latents_up(l)
                rotate(l)
                scan(l)
                attention(l)
                out_projection(l)
                c0 = P * FIRST_T[l]
                mean_square(f"ms{l}ffn", (S("squares", f"{l}ffn"), 0), u, KT, c0)
                router(l)
                experts(l)
                add_experts(l)
            mean_square("msfinal", (S("squares", "final"), 0), u, KT, NCTX)
            for t in (2, 3):
                for half in range(2):
                    bank = open_bank(f"out{t}{half}")
                    for m in range(4):
                        k = 4 * half + m
                        pe.wait_ge(S("u_ready", "final"), k + 1)
                        last = tr(bank[:, P * m:P * m + P], u[:, k, P * t:P * t + P])
                    close_bank(last)

        @block.vector
        def _(dve):
            step = Tally(S("vector_step"))
            read = Tally(evacuated)

            def link(ins):
                dve.wait_ge(step.sem, step.by(ins))

            def claim(name):
                assert read.n == entry[name], (name, read.n, entry[name])
                dve.wait_ge(filled, read.n + 1)
                return ps[:, read.n % 2, :]

            def emptied(ins):
                read.by(ins)

            def own_read():
                dve.wait_ge(read.sem, read.n)

            v = nc.vector
            tt, ts, stt = v.tensor_tensor, v.tensor_scalar, v.scalar_tensor_tensor

            def modulation(l, g):
                bank = claim(f"mod{l}{g}")
                emptied(v.tensor_copy(modrow[:, :], bank))
                bank = claim(f"modT{l}{g}")
                emptied(tt(mod[:, l, 16 * g:16 * g + 16, :].rearrange("p (j s) c -> p j s c", s=4),
                           bank.rearrange("p (s j r) -> p j s r", s=4, j=4)[:, :, :, 0:2],
                           vec[:, l, 16 * g:16 * g + 16].rearrange("p (j s) -> p j s", s=4).unsqueeze(3)
                           .to_broadcast([P, 4, 4, 2]), ALU.add))
                own_read()
                if g != 1:
                    n, at_v = (0, V_GMIX) if g == 0 else (1, V_GFFN)
                    scale = mod[:, l, 8:16, :] if g == 0 else mod[:, l, 32:40, :]
                    stt(gain[:, l, n, :, :], scale, 1.0,
                        vec[:, l, at_v:at_v + KT].unsqueeze(2).to_broadcast([P, KT, 2]), ALU.add,
                        ALU.mult).then_inc(S("gain_ready"), 1)

            def norm(name, c0):
                bank = claim(f"ms{name}")
                emptied(ts(rstd[:, c0:T], bank[:, 0:T - c0], EPS, None, ALU.add))
                dve.wait_ge(S("rstd_ready", name), 1)
                for k in range(KT):
                    tt(u[:, k, c0:T], h[:, k, c0:T], rstd[:, c0:T], ALU.mult).then_inc(S("u_scaled", name), 1)

            def project(l):
                first = FIRST_T[l]
                for m in range(6):
                    bank = claim(f"xbc{l}{m}").rearrange("p (s t) -> p s t", s=2)
                    acc = xbc[:, m, :].rearrange("p (s t) -> p s t", s=2)
                    w = vec[:, l, V_CONVW + m:V_CONVW + 18:6]
                    dve.wait_ge(S("conv_mid", l), m + 1)
                    link(stt(acc[:, :, 1:256], bank[:, :, 0:255], w[:, 0:1], acc[:, :, 1:256], ALU.mult, ALU.add))
                    emptied(stt(acc[:, :, 0:255], bank[:, :, 1:256], w[:, 2:3], acc[:, :, 0:255], ALU.mult, ALU.add))
                for i in range(2):
                    emptied(v.tensor_copy(v_da[:, 2 * i:2 * i + 2, :],
                                          claim(f"v{l}{i}").rearrange("p (t n) -> p t n", n=256)))
                bank = claim(f"dt{l}")[:, 0:64].rearrange("p (t d h) -> p d t h", t=TT, d=2)
                emptied(tt(sc[:, 0, :].rearrange("p (d t h) -> p d t h", d=2, t=TT), bank,
                           bcast[:, l, B_DTB:B_DTB + 16].rearrange("p (d h) -> p d h", d=2).unsqueeze(2)
                           .to_broadcast([P, 2, TT, SSD_H]), ALU.add))
                for m in range(3):
                    emptied(v.tensor_copy(latent[:, m, :], claim(f"lat{l}{m}")))
                emptied(v.tensor_copy(km[NOPE:HD, 0, :], claim(f"kr{l}")[NOPE:HD, :]))
                for m in range(4):
                    c0 = 0 if m >= 2 or l == 0 else NCTX
                    emptied(v.tensor_copy(qk[:, m, c0:T], claim(f"qk{l}{m}")[:, 0:T - c0]))
                for t in range(first, TT):
                    emptied(v.tensor_copy(z[:, t, :], claim(f"z{l}{t}")))

            def latents_up(l):
                c0 = P * FIRST_T[l]
                bank = claim(f"cqms{l}")
                emptied(ts(r_lat[:, 0, c0:T], bank[:, 0:T - c0], DM / QR, EPS, ALU.mult, ALU.add))
                bank = claim(f"ckvms{l}")
                emptied(ts(r_lat[:, 1, :], bank, DM / KVR, EPS, ALU.mult, ALU.add))
                dve.wait_ge(S("r_lat_ready", l), 2)
                for m in range(3):
                    g = vec[:, l, V_QG + m:V_QG + m + 1]
                    cc = c0 if m < 2 else 0
                    stt(latent[:, m, cc:T], latent[:, m, cc:T], g, r_lat[:, m // 2, cc:T], ALU.mult,
                        ALU.mult).then_inc(S("latent_normed", l), 1)
                for hh in range(DA_H):
                    emptied(v.tensor_copy(qm[0:HD, hh, c0:T], claim(f"qm{l}{hh}")[0:HD, 0:T - c0]))
                for hh in range(DA_H):
                    emptied(v.tensor_copy(km[0:NOPE, hh, :], claim(f"km{l}{hh}")[0:NOPE, :]))
                for i in range(2):
                    emptied(v.tensor_copy(v_ml[:, 2 * i:2 * i + 2, :],
                                          claim(f"vm{l}{i}").rearrange("p (t n) -> p t n", n=256)))

            def rope(dst, bank, cos, sin, r):
                emptied(tt(rope_tmp[r, :], bank[r, 0:NLAT], sin[r, :], ALU.mult))
                link(tt(dst, dst, cos[r, :], ALU.mult))
                own_read()
                link(tt(dst, dst, rope_tmp[r, :], ALU.add))

            def rotate(l):
                cos, sin = cst[:, C_COS:C_COS + NLAT], cst[:, C_SIN:C_SIN + NLAT]
                for m in range(4):
                    rope(qk[:, m, NCTX:T], claim(f"qkrot{l}{m}"), cos, sin, slice(0, P))
                for hh in range(DA_H):
                    rope(qm[0:HD, hh, NCTX:T], claim(f"qmrot{l}{hh}"), cst[:, C_MCOS:C_MCOS + NLAT],
                         cst[:, C_MSIN:C_MSIN + NLAT], slice(0, HD))
                rope(km[NOPE:HD, 0, NCTX:T], claim(f"krrot{l}"), cos, sin, slice(NOPE, HD))
                v.tensor_copy(km[NOPE:HD, 1:4, :], km[NOPE:HD, 0:1, :].to_broadcast([ROPE, 3, T])).then_inc(
                    S("roped", l), 1)

            def scan(l):
                first = FIRST_T[l]
                stt(sc[:, 1, :], sc[:, 0, :], -1.0, sc[:, 0, :], ALU.mult, ALU.max).then_inc(S("dt_abs", l), 1)
                dve.wait_ge(S("dt_exp", l), 1)
                ts(sc[:, 3, :], sc[:, 2, :], 1.0, None, ALU.add).then_inc(S("dt_u", l), 1)
                dve.wait_ge(S("dt_u", l), 1)
                link(ts(sc[:, 4, :], sc[:, 3, :], 1.0, None, ALU.is_equal))
                link(stt(sc[:, 5, :], sc[:, 3, :], -1.0, sc[:, 4, :], ALU.add, ALU.add))
                link(v.reciprocal(sc[:, 5, :], sc[:, 5, :]))
                dve.wait_ge(S("dt_exp", l), 2)
                link(tt(sc[:, 5, :], sc[:, 5, :], sc[:, 6, :], ALU.mult))
                link(tt(sc[:, 5, :], sc[:, 5, :], sc[:, 4, :], ALU.add))
                link(tt(sc[:, 5, :], sc[:, 5, :], sc[:, 2, :], ALU.mult))
                link(stt(sc[:, 1, :], sc[:, 0, :], 0.0, sc[:, 5, :], ALU.max, ALU.add))
                link(stt(sc[:, 2, 0:32].rearrange("p (t h) -> p t h", t=TT),
                         sc[:, 1, 0:32].rearrange("p (t h) -> p t h", t=TT), -1.0,
                         sc[:, 7, 0:8].unsqueeze(1).to_broadcast([P, TT, SSD_H]), ALU.mult, ALU.mult))
                stt(sc[:, 2, 32:64].rearrange("p (t h) -> p t h", t=TT),
                    sc[:, 1, 32:64].rearrange("p (t h) -> p t h", t=TT), -1.0,
                    sc[:, 7, 8:16].unsqueeze(1).to_broadcast([P, TT, SSD_H]), ALU.mult,
                    ALU.mult).then_inc(S("da_ready", l), 1)
                for t in range(TT):
                    emptied(v.tensor_copy(xbc[:, 0:4, P * t:P * t + P],
                                          claim(f"xs{l}{t}").rearrange("p (m n) -> p m n", n=P)))
                emptied(v.tensor_copy(b_tok, claim(f"btok{l}").rearrange("p (t n) -> p t n", n=P)))
                bank = claim(f"cum{l}")
                emptied(v.tensor_copy(sc[:, 8:10, :], bank[:, 0:128].rearrange("p (a n) -> p a n", n=64)))
                own_read()
                tt(sc[:, 10, :], sc[:, 9, :], sc[:, 8, :], ALU.subtract).then_inc(S("cum_ready", l), 1)
                dve.wait_ge(S("decays_ready", l), 1)
                tt(sc[:, 5, :], sc[:, 5, :], sc[:, 1, :], ALU.mult).then_inc(S("to_end_ready", l), 1)
                first_of = {0: 0, 1: 1}
                for d in range(2):
                    v.memset(state[:, d, first_of[d], :], 0.0).then_inc(S("state_zeroed", l), 1)
                dve.wait_ge(S("state_zeroed", l), 2)
                for n, (d, t, nxt) in enumerate(state_steps(l)):
                    bank = claim(f"state{l}{n}")
                    for g in range(2):
                        r = slice(64 * g, 64 * g + 64)
                        dec = sc[r, 4, 32 * d + 8 * t + 4 * g:32 * d + 8 * t + 4 * g + 4]
                        last = tt(state[r, d, nxt, :].rearrange("p (h n) -> p h n", n=64),
                                  state[r, d, t, :].rearrange("p (h n) -> p h n", n=64),
                                  dec.unsqueeze(2).to_broadcast([64, 4, 64]), ALU.mult)
                    link(last)
                    emptied(tt(state[:, d, nxt, :], state[:, d, nxt, :], bank[:, 0:256], ALU.add))
                    own_read()
                dve.sem_inc(S("states_done", l), 1)
                for i, t in enumerate(range(first, TT)):
                    if i:
                        dve.wait_ge(S("w_ready", l), 2 * i)
                    for g in range(2):
                        bank = claim(f"cb{l}{t}{g}")
                        for d in range(2):
                            last = tt(gm[:, d, g, :], bank[:, 0:P], tri[d], ALU.mult)
                        emptied(last)
                    for d in range(2):
                        n = 2 * i + d
                        dve.wait_ge(S("rows_cast", l), n + 1)
                        for hh in range(SSD_H):
                            last = ts(ew[:, d, hh, :], ps[:, 2 + hh // 4, P * (hh % 4):P * (hh % 4) + P],
                                      sc[:, 8, 32 * d + 8 * t + hh:32 * d + 8 * t + hh + 1], 0.0, ALU.subtract,
                                      ALU.min)
                        last.then_inc(S("decay_clamped", l), 1)
                    if i:
                        y_turned(l, t - 1)
                    dve.wait_ge(S("y_summed", l), i + 1)
                    for d, dst in ((1, y_two), (0, y_acc)):
                        last = tt(dst.rearrange("p (g h n) -> p g h n", g=2, h=4),
                                  ps[:, 5:7, 256 * d:256 * d + 256].rearrange("p g (h n) -> p g h n", h=4),
                                  sc[:, 3, 32 * d + 8 * t:32 * d + 8 * t + 8].rearrange("p (g h) -> p g h", g=2)
                                  .unsqueeze(3).to_broadcast([P, 2, 4, SSD_P]), ALU.mult)
                    link(last)
                    link(tt(y_acc, y_acc, y_two, ALU.add))
                    tt(y_acc, y_acc, ps[:, 4, :], ALU.add).then_inc(S("y_banks_read", l), 1)
                    dve.wait_ge(S("y_banks_read", l), i + 1)
                    dve.wait_ge(S("skip_ready", l), i + 1)
                    link(tt(y_acc, y_acc, y_skip, ALU.add))
                    dve.wait_ge(S("z_ready", l), 1)
                    tt(y_acc, y_acc, z[:, t, :], ALU.mult).then_inc(S("y_gated", l), 1)
                    dve.wait_ge(S("y_gated", l), i + 1)
                    dve.wait_ge(S("y_squared", l), i + 1)
                    ts(y_acc, y_acc, small[:, 0:1], None, ALU.mult).then_inc(S("y_normed", l), 1)
                y_turned(l, TT - 1)

            def y_turned(l, t):
                bank = claim(f"yT{l}{t}")
                for m in range(4):
                    last = ts(u[:, 2 + m, P * t:P * t + P], bank[:, P * m:P * m + P],
                              vec[:, l, V_SSDG + m:V_SSDG + m + 1], None, ALU.mult)
                emptied(last)

            def lam(l):
                lv = bcast[:, l, B_LAM:B_LAM + 128].rearrange("p (a b n) -> p a b n", a=2, b=2)
                link(tt(o_sq[:, 0:64].rearrange("p (a n) -> p a n", a=2), lv[:, :, 0, :], lv[:, :, 1, :], ALU.mult))
                v.tensor_reduce(small[:, 4:6], o_sq[:, 0:64].rearrange("p (a n) -> p a n", a=2), AX.X,
                                ALU.add).then_inc(S("lam_sums", l), 1)
                dve.wait_ge(S("lam_exp", l), 1)
                link(tt(small[:, 8:9], small[:, 7:8], small[:, 6:7], ALU.subtract))
                link(ts(small[:, 8:9], small[:, 8:9], lam_init(l), None, ALU.subtract))

            def attention(l):
                units = attention_units(l)
                mx, nb, rs, rr = (stats[:, s] for s in range(4))
                lam(l)
                for s in range(len(units) + 1):
                    if s < len(units):
                        kind, t, hh, nk = units[s]
                        nm = 2 if kind == "da" else 1
                        pair = 2 + 2 * (s % 2)
                        dve.wait_ge(S("scores_done", l), s + 1)
                        link(v.tensor_reduce(mx[:, s, 0:nm], ps[:, pair:pair + nm, 0:nk], AX.X, ALU.max))
                        ts(nb[:, s, 0:nm], mx[:, s, 0:nm], -(DA_SCALE if kind == "da" else MLA_SCALE), None,
                           ALU.mult).then_inc(S("max_ready", l), 1)
                    if s >= 1:
                        n = s - 1
                        kind, t, hh, nk = units[n]
                        dve.wait_ge(S("exp_done", l), n + 1)
                        if kind == "da":
                            link(v.reciprocal(rr[:, n, :], rs[:, n, :]))
                            link(tt(rr[:, n, 1:2], rr[:, n, 1:2], small[:, 8:9], ALU.mult))
                            link(ts(probs[:, n % 2, 1, 0:nk], probs[:, n % 2, 1, 0:nk], rr[:, n, 1:2], None, ALU.mult))
                            stt(probs[:, n % 2, 0, 0:nk], probs[:, n % 2, 0, 0:nk], rr[:, n, 0:1],
                                probs[:, n % 2, 1, 0:nk], ALU.mult, ALU.add).then_inc(S("mixed", l), 1)
                        else:
                            link(v.reciprocal(rr[:, n, 0:1], rs[:, n, 0:1]))
                        if n % 4 == 0 and n >= 4:
                            head_out(l, n - 4)
                head_out(l, len(units) - 4)

            def head_out(l, n0):
                kind, t, _, _ = attention_units(l)[n0]
                bank = claim(f"o{kind}{l}{t}")[:, 0:256].rearrange("p (h n) -> p h n", n=DA_V)
                ob = o_sb[:, int(kind == "ml"), :].rearrange("p (h n) -> p h n", n=DA_V)
                if kind == "ml":
                    emptied(tt(ob, bank, stats[:, 3, n0:n0 + 4, 0:1].to_broadcast([P, DA_H, DA_V]), ALU.mult))
                    own_read()
                    dve.sem_inc(S("o_ready", l), 1)
                else:
                    emptied(v.tensor_copy(ob, bank))
                    own_read()
                    sq = o_sq.rearrange("p (h n) -> p h n", n=DA_V)
                    link(tt(sq, ob, ob, ALU.mult))
                    v.tensor_reduce(small[:, 12:16], sq, AX.X, ALU.add).then_inc(S("o_squared", l), 1)
                    dve.wait_ge(S("o_rstd", l), t - FIRST_T[l] + 1)
                    tt(ob, ob, small[:, 12:16].unsqueeze(2).to_broadcast([P, DA_H, DA_V]),
                       ALU.mult).then_inc(S("o_ready", l), 1)
                bank = claim(f"oT{kind}{l}{t}")
                for m in range(2):
                    if kind == "da":
                        last = ts(u[:, m, P * t:P * t + P], bank[:, P * m:P * m + P], vec[:, l, V_SUBG:V_SUBG + 1],
                                  1.0 - lam_init(l), ALU.mult, ALU.mult)
                    else:
                        last = v.tensor_copy(u[:, 6 + m, P * t:P * t + P], bank[:, P * m:P * m + P])
                emptied(last)

            def residual(l, name, gate):
                c0 = P * FIRST_T[l]
                for m in range(KT):
                    bank = claim(f"{name}{l}{m}")
                    off = c0 if name == "mix" else 0
                    for s in range(c0 // NCTX, 2):
                        a = NCTX * s
                        last = stt(h[:, m, a:a + NCTX], bank[:, a - off:a - off + NCTX],
                                   mod[:, l, gate + m, s:s + 1], h[:, m, a:a + NCTX], ALU.mult, ALU.add)
                    emptied(last)

            def router(l):
                f = FIRST_T[l]
                lg, aff, sel, pair, w1, w2, w3, oh1, oh2, sm, key, msk = (rt[:, s, f:TT, :] for s in range(12))
                n = TT - f

                def g4(ap):
                    return ap.rearrange("p t (g e) -> p t g e", g=NG)

                bank = claim(f"logits{l}")[:, 0:TT * NE].rearrange("p (t e) -> p t e", e=NE)[:, f:TT, :]
                emptied(v.tensor_copy(lg, bank))
                dve.wait_ge(S("logits_exp", l), 1)
                link(ts(aff, aff, 1.0, None, ALU.add))
                link(v.reciprocal(aff, aff))
                link(tt(sel, aff, bcast[:, l, B_RB:B_RB + NE].unsqueeze(1).to_broadcast([P, n, NE]), ALU.add))
                s4 = g4(sel)
                pr = pair.rearrange("p t (g e) -> p t g e", g=NG)
                pr2 = w1.rearrange("p t (g e) -> p t g e", g=NG)
                for t in range(n):
                    tt(pr[:, t, :, 0:3], s4[:, t, :, 0:3], s4[:, t, :, 1:4], ALU.add)
                    tt(pr2[:, t, :, 0:2], s4[:, t, :, 0:2], s4[:, t, :, 2:4], ALU.add)
                    link(tt(pr[:, t, :, 3:4], s4[:, t, :, 0:1], s4[:, t, :, 3:4], ALU.add))
                    link(tt(pr[:, t, :, 0:2], pr[:, t, :, 0:2], pr2[:, t, :, 0:2], ALU.max))
                gs = w2[:, :, 0:4]
                gb = w2[:, :, 4:5]
                gk = w2[:, :, 8:12]
                link(v.tensor_reduce(gs, pr, AX.X, ALU.max))
                link(v.tensor_reduce(gb, gs, AX.X, ALU.max))
                link(tt(gk, gs, gb.to_broadcast([P, n, 4]), ALU.is_equal))
                link(tt(gk, gk, cst[:, C_PG:C_PG + NG].unsqueeze(1).to_broadcast([P, n, 4]), ALU.mult))
                link(v.tensor_reduce(gb, gk, AX.X, ALU.max))
                link(tt(gk, gk, gb.to_broadcast([P, n, 4]), ALU.is_equal))
                for t in range(n):
                    last = v.tensor_copy(g4(msk)[:, t], gk[:, t, :].unsqueeze(2).to_broadcast([P, NG, 4]))
                link(last)
                link(tt(sm, sel, msk, ALU.mult))
                link(ts(msk, msk, -1.0, 1e30, ALU.add, ALU.mult))
                link(tt(sm, sm, msk, ALU.add))
                for oh in (oh1, oh2):
                    link(v.tensor_reduce(w3[:, :, 0:1], sm, AX.X, ALU.max))
                    link(tt(key, sm, w3[:, :, 0:1].to_broadcast([P, n, NE]), ALU.is_equal))
                    link(tt(key, key, cst[:, C_PE:C_PE + NE].unsqueeze(1).to_broadcast([P, n, NE]), ALU.mult))
                    link(v.tensor_reduce(w3[:, :, 0:1], key, AX.X, ALU.max))
                    link(tt(oh, key, w3[:, :, 0:1].to_broadcast([P, n, NE]), ALU.is_equal))
                    if oh is oh1:
                        link(stt(sm, oh, -2e30, sm, ALU.mult, ALU.add))
                link(tt(oh1, oh1, oh2, ALU.add))
                link(tt(oh1, oh1, aff, ALU.mult))
                link(v.tensor_reduce(w3[:, :, 0:1], oh1, AX.X, ALU.add))
                link(v.reciprocal(w3[:, :, 0:1], w3[:, :, 0:1]))
                link(tt(gates[:, f:TT, :], oh1, w3[:, :, 0:1].to_broadcast([P, n, NE]), ALU.mult))

            def experts(l):
                f, nu = FIRST_T[l], NU[l]
                tiles = TT - f
                v.memset(y_tok[:, f:TT, :], 0.0).then_inc(S("y_added", l), 1)
                with dve.Fori(0, NE // GROUP) as it:
                    def hidden(n):
                        dve.wait_ge(S("silu_done", l), it * nu + (n + 1))
                        tt(hid[:, n % 2, :], silu_g[:, n % 2, :], ps[:, 2 * (n % 2) + 1, :],
                           ALU.mult).then_inc(S("hid_ready", l), 1)

                    hidden(0)
                    for n in range(nu):
                        if n + 1 < nu:
                            hidden(n + 1)
                        e, t = n // tiles, f + n % tiles
                        dve.wait_ge(S("down_done", l), it * nu + (n + 1))
                        dve.wait_ge(S("y_added", l), it * nu + (n + 1))
                        stt(y_tok[:, t, :].rearrange("p (b n) -> p b n", b=2), ps[:, 6:8, :],
                            gates[:, t, bass.ds(it * GROUP + e, 1)], y_tok[:, t, :].rearrange("p (b n) -> p b n", b=2),
                            ALU.mult, ALU.add).then_inc(S("y_added", l), 1)

            v.memset(ones[:, :], 1.0).then_inc(S("ones_ready"), 1)
            v.memset(ones_mean[:, :], 1.0 / DM).then_inc(S("ones_ready"), 1)
            v.memset(small[:, 20:21], EPS)
            link(v.memset(cond[:, :, :], 0.0))
            emptied(v.tensor_copy(vec[:, :, :], claim("vecs")[:, 0:2 * P].rearrange("p (l n) -> p l n", l=2)
                                  [:, :, 0:NVEC]))
            own_read()
            dve.wait_ge(S("cond_exp"), 1)
            link(ts(small[:, 32:48], small[:, 32:48], 1.0, None, ALU.add))
            link(v.reciprocal(small[:, 32:48], small[:, 32:48]))
            tt(cond[:, :, 0:2].rearrange("p k c -> p c k"), vec[:, 0, V_CCTX:V_CCTX + 16].rearrange(
                "p (c k) -> p c k", c=2), small[:, 32:48].rearrange("p (c k) -> p c k", c=2),
               ALU.mult).then_inc(S("cond_ready"), 1)
            for t in range(TT):
                for half in range(2):
                    emptied(v.tensor_copy(h[:, 4 * half:4 * half + 4, P * t:P * t + P],
                                          claim(f"h{t}{half}").rearrange("p (m n) -> p m n", n=P)))
            dve.wait_ge(S("bcast_landed"), 16 * n_bcast_dmas)
            for l in range(DEPTH):
                norm(f"{l}mix", 0)
                if l == 0:
                    modulation(0, 0)
                project(l)
                if l == 0:
                    for g in (1, 2):
                        modulation(0, g)
                    for g in range(3):
                        modulation(1, g)
                latents_up(l)
                rotate(l)
                scan(l)
                attention(l)
                own_read()
                residual(l, "mix", 16)
                norm(f"{l}ffn", P * FIRST_T[l])
                router(l)
                own_read()
                experts(l)
                residual(l, "y", 40)
            norm("final", NCTX)
            for t in (2, 3):
                for half in range(2):
                    emptied(v.tensor_copy(tok[:, t, 512 * half:512 * half + 512], claim(f"out{t}{half}")))

        @block.scalar
        def _(act):
            a = nc.scalar.activation
            step = Tally(S("scalar_step"))

            def link(ins):
                act.wait_ge(step.sem, step.by(ins))

            def wait_evac(name):
                act.wait_ge(evacuated, entry[name] + 1)

            def rsqrt(dst, src, sem, scale=1.0, bias=0.0):
                link(a(dst, src, ACT.Ln, scale=scale, bias=bias))
                a(dst, dst, ACT.Exp, scale=-0.5).then_inc(sem, 1)

            def norm(name, c0, last_entry, gains, shifts):
                wait_evac(last_entry)
                for k in range(KT):
                    a(u[:, k, c0:T], h[:, k, c0:T], ACT.Square).then_inc(S("squares", name), 1)
                wait_evac(f"ms{name}")
                rsqrt(rstd[:, c0:T], rstd[:, c0:T], S("rstd_ready", name))
                if gains is not None:
                    act.wait_ge(S("gain_ready"), gains[0])
                for k in range(KT):
                    act.wait_ge(S("u_scaled", name), k + 1)
                    if gains is None:
                        a(u[:, k, c0:T], u[:, k, c0:T], ACT.Identity,
                          scale=vec[:, 0, V_FING + k:V_FING + k + 1]).then_inc(S("u_ready", name), 1)
                    else:
                        for s in range(c0 // NCTX, 2):
                            cols = u[:, k, NCTX * s:NCTX * s + NCTX]
                            a(cols, cols, ACT.Identity, scale=gains[1][:, k, s:s + 1],
                              bias=shifts[:, k, s:s + 1]).then_inc(S("u_ready", name), 1)

            def project(l):
                for m in range(6):
                    act.wait_ge(filled, entry[f"xbc{l}{m}"] + 1)
                    a(xbc[:, m, :], ps[:, entry[f"xbc{l}{m}"] % 2, :], ACT.Identity,
                      scale=vec[:, l, V_CONVW + 6 + m:V_CONVW + 7 + m],
                      bias=vec[:, l, V_CONVB + m:V_CONVB + m + 1]).then_inc(S("conv_mid", l), 1)
                for m in range(6):
                    wait_evac(f"xbc{l}{m}")
                    a(xbc[:, m, :], xbc[:, m, :], ACT.Silu).then_inc(S("xbc_ready", l), 1)
                for m in range(3):
                    wait_evac(f"lat{l}{m}")
                    a(latent_sq[:, m, :], latent[:, m, :], ACT.Square).then_inc(S("latent_sq", l), 1)
                wait_evac(f"z{l}{TT - 1}")
                a(z[:, FIRST_T[l]:TT, :], z[:, FIRST_T[l]:TT, :], ACT.Silu).then_inc(S("z_ready", l), 1)
                c0 = P * FIRST_T[l]
                wait_evac(f"cqms{l}")
                rsqrt(r_lat[:, 0, c0:T], r_lat[:, 0, c0:T], S("r_lat_ready", l))
                wait_evac(f"ckvms{l}")
                rsqrt(r_lat[:, 1, :], r_lat[:, 1, :], S("r_lat_ready", l))

            def scan(l):
                act.wait_ge(S("dt_abs", l), 1)
                a(sc[:, 2, :], sc[:, 1, :], ACT.Exp, scale=-1.0).then_inc(S("dt_exp", l), 1)
                link(a(sc[:, 7, 0:16], bcast[:, l, B_ALOG:B_ALOG + 16], ACT.Exp))
                act.wait_ge(S("dt_u", l), 1)
                a(sc[:, 6, :], sc[:, 3, :], ACT.Ln).then_inc(S("dt_exp", l), 1)
                act.wait_ge(S("cum_ready", l), 1)
                a(sc[:, 3, :], sc[:, 8, :], ACT.Exp)
                a(sc[:, 4, :], sc[:, 9, :], ACT.Exp)
                a(sc[:, 5, :], sc[:, 10, :], ACT.Exp).then_inc(S("decays_ready", l), 1)
                for i in range(TT - FIRST_T[l]):
                    for d in range(2):
                        act.wait_ge(S("decay_clamped", l), 2 * i + d + 1)
                        a(ew[:, d, :, :], ew[:, d, :, :], ACT.Exp).then_inc(S("decay_exp", l), 1)
                    act.wait_ge(S("y_gated", l), i + 1)
                    link(a(y_two, y_acc, ACT.Square, accum_out=small[:, 1:2]))
                    rsqrt(small[:, 0:1], small[:, 1:2], S("y_squared", l), 1.0 / SSD_INNER, small[:, 20:21])

            def attention(l):
                units = attention_units(l)
                mx, nb, rs, rr = (stats[:, s] for s in range(4))
                act.wait_ge(S("lam_sums", l), 1)
                a(small[:, 6:8], small[:, 4:6], ACT.Exp).then_inc(S("lam_exp", l), 1)
                for s in range(len(units) + 1):
                    if s < len(units):
                        kind, t, hh, nk = units[s]
                        nm = 2 if kind == "da" else 1
                        act.wait_ge(S("max_ready", l), s + 1)
                        if s >= 2:
                            act.wait_ge(S("probs_turned", l), s - 1)
                        for m in range(nm):
                            last = a(probs[:, s % 2, m, 0:nk], ps[:, 2 + 2 * (s % 2) + m, 0:nk], ACT.Exp,
                                     scale=DA_SCALE if kind == "da" else MLA_SCALE, bias=nb[:, s, m:m + 1],
                                     accum_out=rs[:, s, m:m + 1])
                        last.then_inc(S("exp_done", l), 1)
                    if s >= 1:
                        n = s - 1
                        nk = units[n][3]
                        act.wait_ge(S("probs_turned", l), n + 1)
                        if n >= 2:
                            wait_heads(l, n - 2)
                        nc.scalar.copy(probs_t[:, n % 2, 0:nk // P, :],
                                       ps[:, 6 + n % 2, 0:nk].rearrange("p (k q) -> p k q", q=P)).then_inc(
                            S("probs_t_ready", l), 1)
                        if n % 4 == 0 and n >= 4:
                            head_rstd(l, n - 4)
                head_rstd(l, len(units) - 4)

            def head_rstd(l, n0):
                kind, t, _, _ = attention_units(l)[n0]
                if kind == "da":
                    act.wait_ge(S("o_squared", l), t - FIRST_T[l] + 1)
                    rsqrt(small[:, 12:16], small[:, 12:16], S("o_rstd", l), 1.0 / DA_V, small[:, 20:21])

            def wait_heads(l, n):
                kind, t, hh, _ = attention_units(l)[n]
                if hh == DA_H - 1:
                    act.wait_ge(filled, entry[f"o{kind}{l}{t}"] + 1)
                else:
                    act.wait_ge(S("heads_done", l), 3 * (n // 4) + hh + 1)

            def experts(l):
                f, nu = FIRST_T[l], NU[l]
                wait_evac(f"logits{l}")
                lg, aff = rt[:, 0, f:TT, :], rt[:, 1, f:TT, :]
                a(aff, lg, ACT.Exp, scale=-1.0).then_inc(S("logits_exp", l), 1)
                with act.Fori(0, NE // GROUP) as it:
                    def silu(n):
                        act.wait_ge(S("gate_up_done", l), it * nu + (n + 1))
                        a(silu_g[:, n % 2, :], ps[:, 2 * (n % 2), :], ACT.Silu).then_inc(S("silu_done", l), 1)

                    silu(0)
                    for n in range(nu):
                        if n + 1 < nu:
                            silu(n + 1)
                        act.wait_ge(S("hid_turned", l), it * nu + (n + 1))
                        nc.scalar.copy(hid_t[:, n % 2, :, :],
                                       ps[:, 4 + n % 2, :].rearrange("p (f t) -> p f t", t=P)).then_inc(
                            S("hid_t_ready", l), 1)

            act.dma_start(cst[:, :], consts).then_inc(S("const_landed"), 16)
            for dst, src in vec_loads:
                act.dma_start(dst, src).then_inc(S("const_landed"), 16)
            act.dma_start(tok[:, 0:2, :], ctx.rearrange("b (t p) n -> p (b t) n", p=P)).then_inc(S("tokens_landed"), 16)
            act.dma_start(tok[:, 2:4, :], x.rearrange("b (t p) n -> p (b t) n", p=P)).then_inc(S("tokens_landed"), 16)
            for dst, src in bcast_loads:
                act.dma_start(dst, src).then_inc(S("bcast_landed"), 16)
            act.dma_start(rw[:, :, :], router_w.rearrange("(k p) e -> p k e", p=P)).then_inc(S("bcast_landed"), 16)

            def load_up(l):
                act.dma_start(wuq[:, :, :], mla_w_uq[l].rearrange("(k p) n -> p k n", p=P)).then_inc(S("wu_landed"), 16)
                act.dma_start(wukv[:, :], mla_w_ukv[l]).then_inc(S("wu_landed"), 16)

            load_up(0)
            wait_evac("vecs")
            a(small[:, 32:48], vec[:, 0, V_CCTX:V_CCTX + 16], ACT.Exp, scale=-1.0).then_inc(S("cond_exp"), 1)
            gain_count = {(0, 0): 1, (0, 1): 2, (1, 0): 3, (1, 1): 4}
            for l in range(DEPTH):
                norm(f"{l}mix", 0, "h31" if l == 0 else "y07", (gain_count[(l, 0)], gain[:, l, 0]), mod[:, l, 0:8, :])
                project(l)
                scan(l)
                attention(l)
                if l == 0:
                    load_up(1)
                norm(f"{l}ffn", P * FIRST_T[l], f"mix{l}7", (gain_count[(l, 1)], gain[:, l, 1]), mod[:, l, 24:32, :])
                experts(l)
            norm("final", NCTX, "y17", None, None)

        @block.gpsimd
        def _(pool):
            g = nc.gpsimd

            def hb(ap):
                return ap.unsqueeze(2).to_broadcast([P, SSD_H, SSD_P])

            def xs(t):
                return xbc[:, 0:4, P * t:P * t + P].rearrange("p m (a n) -> p m a n", a=2)

            def xb(ap):
                return ap.rearrange("p (m a) -> p m a", a=2).unsqueeze(3).to_broadcast([P, 4, 2, SSD_P])

            for l in range(DEPTH):
                first = FIRST_T[l]
                pool.wait_ge(S("to_end_ready", l), 1)
                for n, (d, t, _) in enumerate(state_steps(l)):
                    if n >= 2:
                        pool.wait_ge(filled, entry[f"state{l}{n - 2}"] + 1)
                    g.tensor_tensor(xdt[:, n % 2, :].rearrange("p (m a n) -> p m a n", m=4, a=2), xs(t),
                                    xb(sc[:, 5, 32 * d + 8 * t:32 * d + 8 * t + 8]), ALU.mult).then_inc(
                        S("xde_ready", l), 1)
                for i, t in enumerate(range(first, TT)):
                    for d in range(2):
                        if i:
                            pool.wait_ge(S("y_summed", l), i)
                        g.tensor_tensor(ew[:, d, :, :], tri[d].unsqueeze(1).to_broadcast([P, SSD_H, P]),
                                        sc[:, 2, 32 * d + 8 * t:32 * d + 8 * t + 8].unsqueeze(2).to_broadcast(
                                            [P, SSD_H, P]), ALU.mult).then_inc(S("rows_built", l), 1)
                    for d in range(2):
                        if i == 0:
                            pool.wait_ge(filled, entry[f"state{l}{len(state_steps(l)) - 1}"] + 1)
                        last = g.tensor_tensor(xdt[:, d, :].rearrange("p (m a n) -> p m a n", m=4, a=2), xs(t),
                                               xb(sc[:, 1, 32 * d + 8 * t:32 * d + 8 * t + 8]), ALU.mult)
                    if i:
                        pool.wait_ge(S("y_gated", l), i)
                    g.tensor_tensor(y_skip.rearrange("p (m a n) -> p m a n", m=4, a=2), xs(t),
                                    xb(bcast[:, l, B_D:B_D + 8]), ALU.mult).then_inc(S("skip_ready", l), 1)
                    pool.wait_ge(evacuated, entry[f"cb{l}{t}1"] + 1)
                    for d in range(2):
                        pool.wait_ge(S("decay_exp", l), 2 * i + d + 1)
                        for gg in range(2):
                            part = ew[:, d, 4 * gg:4 * gg + 4, :]
                            last = g.tensor_tensor(part, part, gm[:, d, gg, :].unsqueeze(1).to_broadcast([P, 4, P]),
                                                   ALU.mult)
                        last.then_inc(S("w_ready", l), 1)

        @block.sync
        def _(sp):
            def chunk_source(key):
                kind, l, n, k = key
                if kind == "mod":
                    return [(2 * 2048, w_mod[l].rearrange("(k p) n -> p k n", p=P)[:, 2 * k:2 * k + 2,
                                                                                 2048 * n:2048 * n + 2048], 0, 2048)]
                w = w_in[l].rearrange("(k p) n -> p k n", p=P)
                if kind == "out":
                    return [(SLOT, w_out[l].rearrange("(k p) n -> p k n", p=P)[:, :, 512 * n:512 * n + 512], 0, 512)]
                if n == "bcv":
                    return [(SLOT, w[:, :, COL_BC:COL_BC + 256], 0, 512), (SLOT, w[:, :, COL_V:COL_V + 256], 256, 512)]
                col, width = IN_COLS[n]
                return [(KT * width, w[:, :, col:col + width], 0, width)]

            def load(i, key):
                if i >= RING:
                    sp.wait_ge(*released[i - RING])
                for total, src, a, row in chunk_source(key):
                    dst = ring[:, i % RING, 0:total].rearrange("p (k n) -> p k n", n=row)[:, :, a:a + src.shape[2]]
                    sp.dma_start(dst, src).then_inc(landed[i % RING], 16)

            def experts(l):
                base, nu = moe_base[l], NU[l]
                tiles = TT - FIRST_T[l]
                gate = exp_w_gate[l].rearrange("e (k p) n -> p e k n", p=P)
                up = exp_w_up[l].rearrange("e (k p) n -> p e k n", p=P)
                down = exp_w_down[l].rearrange("e (f p) n -> p e f n", p=P)

                def send(c, e):
                    src, n = ((gate, DE), (up, DE), (down, DM))[c % PER_EXPERT]
                    s = (base + c) % RING
                    sp.dma_start(ring[:, s, :].rearrange("p (o k n) -> p o k n", o=1, n=n),
                                 src[:, bass.ds(e, 1), :, :]).then_inc(landed[s], 16)

                for c in range(RING):
                    sp.wait_ge(*released[base + c - RING])
                    send(c, c // PER_EXPERT)
                per = GROUP * PER_EXPERT

                def body(it, last=False):
                    for c in range(RING, per + (0 if last else RING)):
                        q = c - RING
                        n = (q // PER_EXPERT) * tiles + tiles
                        sem = S("down_done", l) if q % PER_EXPERT == 2 else S("gate_up_done", l)
                        sp.wait_ge(sem, it * nu + n)
                        send(c, it * GROUP + c // PER_EXPERT)

                with sp.Fori(0, NE // GROUP - 1) as it:
                    body(it)
                body(NE // GROUP - 1, last=True)
                for c in range(NE * PER_EXPERT - RING, NE * PER_EXPERT):
                    sem = S("down_done", l) if c % PER_EXPERT == 2 else S("gate_up_done", l)
                    released[base + c] = (sem, (c // PER_EXPERT) * tiles + tiles)

            for i, key in enumerate(chunks):
                load(i, key)
            experts(0)
            for i, key in enumerate(after):
                load(second + i, key)
            experts(1)
            for t in (2, 3):
                for half in range(2):
                    sp.wait_ge(evacuated, entry[f"out{t}{half}"] + 1)
                    sp.dma_start(out.rearrange("b (t p) n -> p (b t) n", p=P)[:, t - 2, 512 * half:512 * half + 512],
                                 tok[:, t, 512 * half:512 * half + 512]).then_inc(S("out_stored"), 16)
            sp.wait_ge(S("out_stored"), 64)


_INS = ["x", "c", "ctx", "c_ctx", "norm_mix_g", "norm_ffn_g", "w_mod", "b_mod", "w_in", "w_out", "da_lambda",
        "da_subln_g", "ssd_conv_w", "ssd_conv_b", "ssd_dt_bias", "ssd_a_log", "ssd_d", "ssd_norm_g", "mla_q_norm_g",
        "mla_kv_norm_g", "mla_w_uq", "mla_w_ukv", "router_w", "router_bias", "exp_w_gate", "exp_w_up", "exp_w_down",
        "final_norm_g"]


def kernel(**inputs):
    import concourse.bacc as bacc
    from concourse.bass_utils import run_bass_kernel_spmd as run

    nc = bacc.Bacc("TRN2", target_bir_lowering=False, num_devices=1)
    arrays = {"in_constants": shape_constants()}
    args = [nc.dram_tensor("in_constants", (P, NCONST), F32, kind="ExternalInput").ap()]
    for name in _INS:
        a = np.ascontiguousarray(inputs[name])
        arrays[f"in_{name}"] = a
        args.append(nc.dram_tensor(f"in_{name}", a.shape, mybir.dt.from_np(a.dtype), kind="ExternalInput").ap())
    args.append(nc.dram_tensor("out_0", (1, NLAT, DM), F32, kind="ExternalOutput").ap())
    hybrid_dit_kernel(nc, *args)
    r = run(nc, [arrays], core_ids=[0])
    return r.results[0]["out_0"]
```

```python
import math
from contextlib import ExitStack

import numpy as np

import concourse.bass as bass
from concourse import mybir

ALU = mybir.AluOpType
ACT = mybir.ActivationFunctionType
F32 = mybir.dt.float32
I32 = mybir.dt.int32
AX = mybir.AxisListType

P = 128
DM = 1024
KT = DM // P
NCTX, NLAT = 256, 256
T = NCTX + NLAT
TT = T // P
DEPTH = 2
GRID_W = 64
EPS = 1e-6
DA_H, DA_QK, DA_V = 4, 32, 64
SSD_H, SSD_P, SSD_N, SSD_INNER = 8, 64, 64, 512
QR, KVR = 256, 128
NOPE, ROPE = 64, 32
HD = NOPE + ROPE
IN_W = 2480
COL_QK, COL_V, COL_Z, COL_X, COL_BC, COL_DT = 0, 512, 768, 1280, 1792, 2048
NE, NG, DE = 16, 4, 512
DA_SCALE = DA_QK ** -0.5
MLA_SCALE = HD ** -0.5

V_BMOD, V_GMIX, V_GFFN, V_CONVW, V_CONVB, V_QG, V_KVG, V_FING, V_SSDG, V_SUBG, V_CCTX, V_C, NVEC = (
    0, 48, 56, 64, 82, 88, 90, 91, 99, 103, 104, 112, 120)
B_DTB, B_ALOG, B_D, B_LAM, B_RB, NB = 0, 16, 32, 40, 168, 184
C_ID, C_MF, C_MB, C_ROT, C_COS, C_SIN, C_MROT, C_MCOS, C_MSIN, C_PE, C_PG, C_IOTA, C_TOK, NCONST = (
    0, 128, 256, 384, 512, 768, 1024, 1152, 1408, 1664, 1680, 1684, 1812, 1816)

RING = 4
SLOT = 4096
PER_EXPERT = 3
GROUP = 4
GATHERS = 4
STEPS = NE // GROUP - 1
NOWHERE = 4096


def shape_constants():
    c = np.zeros((P, NCONST), np.float32)
    i = np.arange(P)
    c[:, C_ID:C_ID + P] = np.eye(P)
    c[:, C_MF:C_MF + P] = i[:, None] <= i[None, :]
    c[:, C_MB:C_MB + P] = i[:, None] >= i[None, :]
    half = DA_QK // 2
    for m in range(P):
        if m % DA_QK < half:
            c[m + half, C_ROT + m] = -1.0
        else:
            c[m - half, C_ROT + m] = 1.0
    rows = NLAT // GRID_W
    row = np.repeat(np.arange(rows), GRID_W).astype(np.float32)
    col = np.tile(np.arange(GRID_W), rows).astype(np.float32)
    nf = DA_QK // 4
    inv = np.float32(10000.0) ** (-np.arange(nf, dtype=np.float32) / np.float32(nf))
    ang = np.concatenate([row[:, None] * inv, col[:, None] * inv], axis=-1)
    cos, sin = np.cos(ang).T, np.sin(ang).T
    for m in range(P):
        c[m, C_COS:C_COS + NLAT] = cos[m % half]
        c[m, C_SIN:C_SIN + NLAT] = sin[m % half]
    c[:NOPE, C_MCOS:C_MCOS + NLAT] = 1.0
    c[NOPE:HD, C_MCOS:C_MCOS + NLAT] = c[NOPE:HD, C_COS:C_COS + NLAT]
    c[NOPE:HD, C_MSIN:C_MSIN + NLAT] = c[NOPE:HD, C_SIN:C_SIN + NLAT]
    c[NOPE:HD, C_MROT + NOPE:C_MROT + HD] = c[NOPE:HD, C_ROT + NOPE:C_ROT + HD]
    c[:, C_PE:C_PE + NE] = NE - np.arange(NE)
    c[:, C_PG:C_PG + NG] = NG - np.arange(NG)
    c[:, C_IOTA:C_IOTA + P] = np.arange(P)
    c[:, C_TOK:C_TOK + TT] = P * np.arange(TT)[None, :] + i[:, None]
    return c


def lam_init(layer):
    return 0.8 - 0.6 * math.exp(-0.3 * layer)


def attention_units(layer):
    return [(kind, t, hh, NCTX if P * t < NCTX else T)
            for t in range(0 if layer == 0 else NCTX // P, TT) for kind in ("da", "ml") for hh in range(DA_H)]


def state_steps(layer):
    return [(0, 0, 1), (1, 1, 0), (0, 1, 2), (1, 0, 3), (0, 2, 3), (1, 3, 2)]


def chunk_place(kind, n):
    if kind == 2:
        return PER_EXPERT * n + 4 if n < NE - 1 else PER_EXPERT * NE - 1
    return kind if n == 0 else PER_EXPERT * n - 1 + kind


CHUNK_AT = {chunk_place(kind, n): (kind, n) for kind in range(3) for n in range(NE)}


class Tally:

    def __init__(self, sem):
        self.sem, self.n = sem, 0

    def by(self, instruction):
        instruction.then_inc(self.sem, 1)
        self.n += 1
        return self.n


def hybrid_dit_kernel(nc, consts, x, c, ctx, c_ctx, norm_mix_g, norm_ffn_g, w_mod, b_mod, w_in, w_out, da_lambda,
                      da_subln_g, ssd_conv_w, ssd_conv_b, ssd_dt_bias, ssd_a_log, ssd_d, ssd_norm_g, mla_q_norm_g,
                      mla_kv_norm_g, mla_w_uq, mla_w_ukv, router_w, router_bias, exp_w_gate, exp_w_up, exp_w_down,
                      final_norm_g, out):
    with ExitStack() as stack:
        def sb(name, *shape, dtype=F32):
            return stack.enter_context(nc.sbuf_tensor(name, list(shape), dtype))

        sems = {}

        def S(name, layer=None):
            key = name if layer is None else f"{name}_{layer}"
            if key not in sems:
                sems[key] = stack.enter_context(nc.semaphore(key))
            return sems[key]

        FIRST_T = [0, 2]
        cst = sb("cst", P, NCONST)
        ident = cst[:, C_ID:C_ID + P]
        tri = [cst[:, C_MF:C_MF + P], cst[:, C_MB:C_MB + P]]
        ones = sb("ones", P, P)
        ones_mean = sb("ones_mean", P, P)
        h = sb("h", P, KT, T)
        u = sb("u", P, KT, T)
        ring = sb("ring", P, RING, SLOT)
        vec = sb("vec", P, DEPTH, NVEC)
        bcast = sb("bcast", P, DEPTH, NB)
        cond = sb("cond", P, KT, 32)
        modrow = sb("modrow", P, 512)
        mod = sb("mod", P, DEPTH, 48, 2)
        gain = sb("gain", P, DEPTH, 2, KT, 2)
        wuq = sb("wuq", P, 2, DA_H * HD)
        wukv = sb("wukv", P, 512)
        rw = sb("rw", P, KT, NE)
        rstd = sb("rstd", P, T)
        small = sb("small", P, 64)
        rt = sb("rt", P, 12, TT, NE)
        pos = sb("pos", P, TT, NE)
        vals = sb("vals", P, TT, NE, 3)
        gate_list = sb("gate_list", P, NE)
        row_in = sb("row_in", P, NE, dtype=I32)
        row_out = sb("row_out", P, NE, dtype=I32)
        row_in_now = sb("row_in_now", P, GROUP, dtype=I32)
        row_out_now = sb("row_out_now", P, GROUP, dtype=I32)
        passes = sb("passes", P, DEPTH, dtype=I32)
        arena = sb("arena", P, 21760)

        at = [0]

        def take(n, where=None):
            a = at[0] if where is None else where
            if where is None:
                at[0] += n
            return arena[:, a:a + n]

        xbc = take(6 * T).rearrange("p (m t) -> p m t", t=T)
        v_da = take(TT * 256).rearrange("p (t n) -> p t n", n=256)
        z = take(TT * 512).rearrange("p (t n) -> p t n", n=512)
        qk = take(4 * T).rearrange("p (m t) -> p m t", t=T)
        qm = take(4 * T).rearrange("p (h t) -> p h t", t=T)
        km = take(4 * T).rearrange("p (h t) -> p h t", t=T)
        v_ml = take(TT * 256).rearrange("p (t n) -> p t n", n=256)
        b_tok = take(TT * P).rearrange("p (t n) -> p t n", n=P)
        state = take(2 * TT * 256).rearrange("p (d t n) -> p d t n", d=2, n=256)
        tmp_at = at[0]
        ew = take(2 * 1024).rearrange("p (d h i) -> p d h i", d=2, i=P)
        xdt = take(2 * 512).rearrange("p (d n) -> p d n", d=2)
        gm = take(512).rearrange("p (d g i) -> p d g i", d=2, i=P)
        y_acc = take(512)
        y_two = take(512)
        y_skip = take(512)
        sc = take(64 * 12).rearrange("p (k n) -> p k n", n=64)
        assert at[0] <= 21760, at[0]
        probs = take(2048, tmp_at).rearrange("p (b m k) -> p b m k", b=2, m=2)
        probs_t = take(1024, tmp_at + 2048).rearrange("p (b k q) -> p b k q", b=2, q=P)
        stats = take(4 * 64, tmp_at + 3072).rearrange("p (s u m) -> p s u m", s=4, m=2)
        o_sb = take(512, tmp_at + 3328).rearrange("p (k n) -> p k n", n=256)
        o_sq = take(256, tmp_at + 3840)
        latent = take(3 * T, tmp_at).rearrange("p (m t) -> p m t", t=T)
        latent_sq = take(3 * T, tmp_at + 3 * T).rearrange("p (m t) -> p m t", t=T)
        r_lat = take(2 * T, tmp_at + 6 * T).rearrange("p (m t) -> p m t", t=T)
        rope_tmp = take(256, tmp_at + 8 * T)
        assert tmp_at + 8 * T + 256 <= 21760
        y_tok = take(TT * DM, 0).rearrange("p (t n) -> p t n", n=DM)
        y_tok2 = take(TT * DM, TT * DM).rearrange("p (t n) -> p t n", n=DM)
        moe_at = 2 * TT * DM
        x_slots = take(GATHERS * DM, 0).rearrange("p (b n) -> p b n", b=GATHERS)
        x_t = take(2 * DM, moe_at + 2 * DM).rearrange("p (b k s) -> p b k s", b=2, s=P)
        y_slots = take(2 * DM, moe_at + 4 * DM).rearrange("p (b n) -> p b n", b=2)
        onehot = take(GROUP * TT * P, moe_at + 6 * DM).rearrange("p (b s) -> p b s", s=P)
        silu_g = take(DE, moe_at + 8 * DM)
        hid = take(DE, moe_at + 8 * DM + DE)
        hid_t = take(DE, moe_at + 9 * DM).rearrange("p (f s) -> p f s", s=P)
        u_tok = y_tok2
        vecrows = take(DEPTH * P, moe_at).rearrange("p (l n) -> p l n", l=DEPTH)
        tok = y_tok
        u_rows = [nc.dram_tensor(f"u_rows{l}", (T - P * FIRST_T[l], DM), F32, kind="Internal").ap() for l in range(DEPTH)]
        y_rows = [nc.dram_tensor(f"y_rows{l}", (2 * T, DM), F32, kind="Internal").ap() for l in range(DEPTH)]

        ps = stack.enter_context(nc.psum_tensor("ps", [P, 8, 512], F32))

        chunks = []
        for g in range(3):
            chunks += [("mod", 0, g, k) for k in range(4)]
            if g == 0:
                chunks += [("in", 0, n, 0) for n in ("x", "bcv", "dtm", "qk", "z")]
        chunks += [("mod", 1, g, k) for g in range(3) for k in range(4)]
        chunks += [("out", 0, n, 0) for n in range(2)]
        moe_base = [len(chunks)]
        after = [("in", 1, n, 0) for n in ("x", "bcv", "dtm", "qk", "z")] + [("out", 1, n, 0) for n in range(2)]
        second = len(chunks) + NE * PER_EXPERT
        moe_base.append(second + len(after))
        ring_at = {k: i for i, k in enumerate(chunks)}
        ring_at.update({k: second + i for i, k in enumerate(after)})
        landed = [[S(f"ring_landed{s}", l) for s in range(RING)] for l in range(DEPTH)]

        def landed_sem(i):
            return landed[int(i >= second)][i % RING]

        pairs = [i for k, i in ring_at.items() if k[2] == "bcv"]

        def landed_count(i):
            start = second if i >= second else 0
            return 16 * sum(2 if j in pairs else 1 for j in range(start, i + 1) if j % RING == i % RING)

        IN_COLS = {"x": (COL_X, 512), "qk": (COL_QK, 512), "z": (COL_Z, 512), "dtm": (COL_DT, 432)}

        NORMS = ["0mix", "0ffn", "1mix", "1ffn", "final"]
        eights = {n: 8 * i for i, n in enumerate(NORMS)}
        ready_base = dict(zip(NORMS, (0, 16, 32, 48, 56)))
        units0 = len(attention_units(0))

        entry = {}
        released = {}
        filled, evacuated = S("bank_filled"), S("bank_evacuated")

        vec_loads, bcast_loads = [], []
        for l in range(DEPTH):
            for row, n, src in ((V_BMOD, 48, b_mod[l].rearrange("(r p) -> r p", p=P)),
                                (V_GMIX, 8, norm_mix_g[l].rearrange("(r p) -> r p", p=P)),
                                (V_GFFN, 8, norm_ffn_g[l].rearrange("(r p) -> r p", p=P)),
                                (V_CONVW, 6, ssd_conv_w[l, 0].rearrange("(r p) -> r p", p=P)),
                                (V_CONVW + 6, 6, ssd_conv_w[l, 1].rearrange("(r p) -> r p", p=P)),
                                (V_CONVW + 12, 6, ssd_conv_w[l, 2].rearrange("(r p) -> r p", p=P)),
                                (V_CONVB, 6, ssd_conv_b[l].rearrange("(r p) -> r p", p=P)),
                                (V_QG, 2, mla_q_norm_g[l].rearrange("(r p) -> r p", p=P)),
                                (V_KVG, 1, mla_kv_norm_g[l].rearrange("(r p) -> r p", p=P)),
                                (V_FING, 8, final_norm_g.rearrange("(r p) -> r p", p=P)),
                                (V_SSDG, 4, ssd_norm_g[l].rearrange("(r p) -> r p", p=P)),
                                (V_CCTX, 8, c_ctx.rearrange("(r p) -> r p", p=P)),
                                (V_C, 8, c[0].rearrange("(r p) -> r p", p=P))):
                vec_loads.append((vecrows[row:row + n, l, :], src))
            for a in range(2):
                vec_loads.append((vecrows[V_SUBG:V_SUBG + 1, l, 64 * a:64 * a + 64],
                                  da_subln_g[l].rearrange("(r p) -> r p", r=1)))
            for at_b, n, src in ((B_DTB, 16, ssd_dt_bias[l].rearrange("a n -> (a n)")),
                                 (B_ALOG, 16, ssd_a_log[l].rearrange("a n -> (a n)")),
                                 (B_D, 8, ssd_d[l]), (B_LAM, 128, da_lambda[l].rearrange("a n -> (a n)")),
                                 (B_RB, 16, router_bias)):
                bcast_loads.append((bcast[:, l, at_b:at_b + n], src.partition_broadcast(P)))
        n_vec_dmas, n_bcast_dmas = len(vec_loads), len(bcast_loads) + 1

        block = stack.enter_context(nc.Block())

        def alone(engine):
            engine.sem_inc(S("carriers"), 1)

        @block.tensor
        def _(pe):
            def wait_chunk(key):
                i = ring_at[key]
                pe.wait_ge(landed_sem(i), landed_count(i))
                return ring[:, i % RING, :]

            def open_bank(name):
                i = len(entry)
                entry[name] = i
                if i >= 2:
                    pe.wait_ge(evacuated, i - 1)
                return ps[:, i % 2, :]

            def close_bank(last):
                last.then_inc(filled, 1)

            def read_back(name):
                pe.wait_ge(evacuated, entry[name] + 1)

            def tr(dst, src):
                n = src.shape[0]
                return nc.tensor.transpose(dst, src, ident[0:n, 0:n])

            def modulation(l, g):
                bank = open_bank(f"mod{l}{g}")
                for kk in range(4):
                    w = wait_chunk(("mod", l, g, kk)).rearrange("p (k n) -> p k n", k=2)
                    for k2 in range(2):
                        k = 2 * kk + k2
                        for j in range(4):
                            last = nc.tensor.matmul(bank[32 * j:32 * j + 32, :], cond[:, k, :],
                                                    w[:, k2, 512 * j:512 * j + 512], start=(k == 0), stop=(k == 7),
                                                    tile_position=(0, 32 * j))
                    if kk < 3:
                        last.then_inc(S("mod_chunk_used"), 1)
                        mod_used[0] += 1
                        released[ring_at[("mod", l, g, kk)]] = (S("mod_chunk_used"), mod_used[0])
                close_bank(last)
                released[ring_at[("mod", l, g, 3)]] = (filled, entry[f"mod{l}{g}"] + 1)
                read_back(f"mod{l}{g}")
                bank = open_bank(f"modT{l}{g}")
                for s in range(4):
                    last = tr(bank[:, P * s:P * s + P], modrow[:, P * s:P * s + P])
                close_bank(last)

            mod_used = [0]

            def mean_square(name, ready, src, n, c0):
                bank = open_bank(name)
                for k in range(n):
                    pe.wait_ge(ready[0], ready[1] + k + 1)
                    last = nc.tensor.matmul(bank[:, 0:T - c0], ones_mean[:, :], src[:, k, c0:T], start=(k == 0),
                                            stop=(k == n - 1))
                close_bank(last)

            def feature_major(name, w, n, c0, ready=None, width=P, row=0):
                bank = open_bank(name)
                for k in range(KT):
                    if ready is not None:
                        pe.wait_ge(S("u_ready"), ready + 2 * (k + 1))
                    last = nc.tensor.matmul(bank[row:row + width, 0:T - c0], w[:, k, n:n + width], u[:, k, c0:T],
                                            start=(k == 0), stop=(k == KT - 1))
                close_bank(last)

            def token_major(name, w, n, width, tiles):
                bank = open_bank(name)
                for i, t in enumerate(tiles):
                    for k in range(KT):
                        last = nc.tensor.matmul(bank[:, i * width:(i + 1) * width], u[:, k, P * t:P * t + P],
                                                w[:, k, n:n + width], start=(k == 0), stop=(k == KT - 1))
                close_bank(last)

            def in_chunk(l, n):
                width = 432 if n == "dtm" else 512
                w = wait_chunk(("in", l, n, 0))
                return w[:, 0:KT * width].rearrange("p (k n) -> p k n", n=width)

            def free_chunk(key, name):
                released[ring_at[key]] = (filled, entry[name] + 1)

            def project(l):
                first = FIRST_T[l]
                w = in_chunk(l, "x")
                for m in range(4):
                    feature_major(f"xbc{l}{m}", w, P * m, 0, ready_base[f"{l}mix"] if m == 0 else None)
                free_chunk(("in", l, "x", 0), f"xbc{l}3")
                w = in_chunk(l, "bcv")
                for m in range(2):
                    feature_major(f"xbc{l}{4 + m}", w, P * m, 0)
                for i in range(2):
                    token_major(f"v{l}{i}", w, 256, 256, [2 * i, 2 * i + 1])
                free_chunk(("in", l, "bcv", 0), f"v{l}1")
                w = in_chunk(l, "dtm")
                token_major(f"dt{l}", w, 0, 16, range(TT))
                for m in range(3):
                    feature_major(f"lat{l}{m}", w, 16 + P * m, 0)
                feature_major(f"kr{l}", w, 16 + QR + KVR, 0, width=ROPE, row=NOPE)
                free_chunk(("in", l, "dtm", 0), f"kr{l}")
                w = in_chunk(l, "qk")
                for m in range(4):
                    feature_major(f"qk{l}{m}", w, P * m, 0 if m >= 2 or l == 0 else NCTX)
                free_chunk(("in", l, "qk", 0), f"qk{l}3")
                w = in_chunk(l, "z")
                for t in range(first, TT):
                    token_major(f"z{l}{t}", w, 0, 512, [t])
                free_chunk(("in", l, "z", 0), f"z{l}{TT - 1}")

            def latents_up(l):
                c0 = P * FIRST_T[l]
                mean_square(f"cqms{l}", (S("latent_sq"), 3 * l), latent_sq, 2, c0)
                mean_square(f"ckvms{l}", (S("latent_sq"), 3 * l + 2), latent_sq[:, 2:3, :], 1, 0)
                pe.wait_ge(S("wu_landed"), 32 * (l + 1))
                pe.wait_ge(S("latent_normed"), 3 * l + 3)
                for hh in range(DA_H):
                    bank = open_bank(f"qm{l}{hh}")
                    for m in range(2):
                        last = nc.tensor.matmul(bank[0:HD, 0:T - c0], wuq[:, m, HD * hh:HD * hh + HD],
                                                latent[:, m, c0:T], start=(m == 0), stop=(m == 1))
                    close_bank(last)
                for hh in range(DA_H):
                    bank = open_bank(f"km{l}{hh}")
                    close_bank(nc.tensor.matmul(bank[0:NOPE, :], wukv[:, P * hh:P * hh + NOPE], latent[:, 2, :],
                                                start=True, stop=True))
                wv = wukv[:, :].rearrange("p (h n) -> p h n", n=P)[:, :, NOPE:P]
                for i in range(2):
                    bank = open_bank(f"vm{l}{i}")
                    for j in range(2):
                        t = 2 * i + j
                        last = nc.tensor.matmul(bank[:, 256 * j:256 * j + 256].rearrange("p (h n) -> p h n", h=4),
                                                latent[:, 2, P * t:P * t + P], wv,
                                                start=True, stop=True)
                    close_bank(last)

            def rotate(l):
                for m in range(4):
                    read_back(f"qk{l}{m}")
                    bank = open_bank(f"qkrot{l}{m}")
                    close_bank(nc.tensor.matmul(bank[:, 0:NLAT], cst[:, C_ROT:C_ROT + P], qk[:, m, NCTX:T],
                                                start=True, stop=True))
                for hh in range(DA_H):
                    read_back(f"qm{l}{hh}")
                    bank = open_bank(f"qmrot{l}{hh}")
                    close_bank(nc.tensor.matmul(bank[0:HD, 0:NLAT], cst[0:HD, C_MROT:C_MROT + HD],
                                                qm[0:HD, hh, NCTX:T], start=True, stop=True))
                read_back(f"kr{l}")
                bank = open_bank(f"krrot{l}")
                close_bank(nc.tensor.matmul(bank[NOPE:HD, 0:NLAT],
                                            cst[NOPE:HD, C_ROT + NOPE:C_ROT + HD], km[NOPE:HD, 0, NCTX:T],
                                            start=True, stop=True))

            def scan(l):
                first = FIRST_T[l]
                pe.wait_ge(S("xbc_ready"), 6 * l + 6)
                for t in range(TT):
                    bank = open_bank(f"xs{l}{t}")
                    for m in range(4):
                        last = tr(bank[:, P * m:P * m + P], xbc[:, m, P * t:P * t + P])
                    close_bank(last)
                bank = open_bank(f"btok{l}")
                for t in range(TT):
                    last = tr(bank[:, P * t:P * t + P], xbc[:, 4, P * t:P * t + P])
                close_bank(last)
                pe.wait_ge(S("da_ready"), l + 1)
                bank = open_bank(f"cum{l}")
                for d in range(2):
                    nc.tensor.matmul(bank[:, 32 * d:32 * d + 32], tri[d], sc[:, 2, 32 * d:32 * d + 32], start=True,
                                     stop=True)
                close_bank(nc.tensor.matmul(bank[:, 64:128], ones[:, :], sc[:, 2, :], start=True, stop=True))
                read_back(f"btok{l}")
                for n, (d, t, _) in enumerate(state_steps(l)):
                    pe.wait_ge(S("xde_ready", l), n + 1)
                    bank = open_bank(f"state{l}{n}")
                    for g in range(2):
                        last = nc.tensor.matmul(bank[64 * g:64 * g + 64, 0:256], b_tok[:, t, 64 * g:64 * g + 64],
                                                xdt[:, n % 2, 256 * g:256 * g + 256], start=True, stop=True)
                    close_bank(last)
                for i, t in enumerate(range(first, TT)):
                    for g in range(2):
                        bank = open_bank(f"cb{l}{t}{g}")
                        r = slice(64 * g, 64 * g + 64)
                        last = nc.tensor.matmul(bank[:, 0:P], xbc[r, 4, P * t:P * t + P],
                                                xbc[r, 5, P * t:P * t + P], start=True, stop=True)
                        close_bank(last)
                    for d in range(2):
                        n = 2 * i + d
                        pe.wait_ge(S("rows_built", l), n + 1)
                        if n >= 1:
                            pe.wait_ge(S("decay_clamped", l), n)
                        for b in range(2):
                            last = nc.tensor.matmul(ps[:, 2 + b, :], ones[:, :], 
                                                    ew[:, d, 4 * b:4 * b + 4, :].rearrange("p h i -> p (h i)"),
                                                    start=True, stop=True)
                        last.then_inc(S("rows_cast", l), 1)
                    if i == 0:
                        pe.wait_ge(S("states_done"), l + 1)
                    else:
                        pe.wait_ge(S("y_banks_read", l), i)
                    for d in range(2):
                        pe.wait_ge(S("w_ready", l), 2 * i + d + 1)
                        for hh in range(SSD_H):
                            last = nc.tensor.matmul(ps[:, 4, 64 * hh:64 * hh + 64], ew[:, d, hh, :],
                                                    xdt[:, d, 64 * hh:64 * hh + 64], start=(d == 0 and hh == 0),
                                                    stop=(d == 1 and hh == 7), skip_group_check=True)
                        for g in range(2):
                            r = slice(64 * g, 64 * g + 64)
                            last = nc.tensor.matmul(ps[:, 5 + g, 256 * d:256 * d + 256], xbc[r, 5, P * t:P * t + P],
                                                    state[r, d, t, :], start=True, stop=True)
                    last.then_inc(S("y_summed", l), 1)
                    if i > 0:
                        y_transposes(l, t - 1, i)
                y_transposes(l, TT - 1, TT - first)

            def y_transposes(l, t, count):
                pe.wait_ge(S("y_normed", l), count)
                bank = open_bank(f"yT{l}{t}")
                for m in range(4):
                    last = tr(bank[:, P * m:P * m + P], y_acc[:, P * m:P * m + P])
                close_bank(last)

            def attention(l):
                units = attention_units(l)
                pe.wait_ge(S("roped"), l + 1)
                groups = 0
                for s in range(len(units) + 2):
                    if s < len(units):
                        kind, t, hh, nk = units[s]
                        if s >= 2:
                            pe.wait_ge(S("exp_done"), units0 * l + s - 1)
                        pair = 2 + 2 * (s % 2)
                        if kind == "da":
                            r0 = 64 * (hh % 2)
                            for m in range(2):
                                r = slice(r0 + 32 * m, r0 + 32 * m + 32)
                                last = nc.tensor.matmul(ps[:, pair + m, 0:nk], qk[r, hh // 2, P * t:P * t + P],
                                                        qk[r, 2 + hh // 2, 0:nk], start=True, stop=True)
                        else:
                            last = nc.tensor.matmul(ps[:, pair, 0:nk], qm[0:HD, hh, P * t:P * t + P],
                                                    km[0:HD, hh, 0:nk], start=True, stop=True)
                        last.then_inc(S("scores_done"), 1)
                    if 1 <= s <= len(units):
                        n = s - 1
                        kind, t, hh, nk = units[n]
                        if kind == "da":
                            pe.wait_ge(S("mixed"), units0 // 2 * l + sum(1 for x in units[:n + 1] if x[0] == "da"))
                        else:
                            pe.wait_ge(S("exp_done"), units0 * l + n + 1)
                        if n >= 2:
                            pe.wait_ge(S("probs_t_ready"), units0 * l + n - 1)
                        for k in range(nk // P):
                            last = tr(ps[:, 6 + n % 2, P * k:P * k + P], probs[:, n % 2, 0, P * k:P * k + P])
                        last.then_inc(S("probs_turned"), 1)
                    if s >= 2:
                        n = s - 2
                        kind, t, hh, nk = units[n]
                        if hh == 0:
                            o_bank = open_bank(f"o{kind}{l}{t}")
                        pe.wait_ge(S("probs_t_ready"), units0 * l + n + 1)
                        v = v_da if kind == "da" else v_ml
                        for k in range(nk // P):
                            last = nc.tensor.matmul(o_bank[:, 64 * hh:64 * hh + 64], probs_t[:, n % 2, k, :],
                                                    v[:, k, 64 * hh:64 * hh + 64], start=(k == 0),
                                                    stop=(k == nk // P - 1))
                        if hh == DA_H - 1:
                            close_bank(last)
                            groups += 1
                            head_out(l, kind, t, groups)
                        else:
                            last.then_inc(S("heads_done"), 1)

            def head_out(l, kind, t, count):
                pe.wait_ge(S("o_ready"), units0 // 4 * l + count)
                bank = open_bank(f"oT{kind}{l}{t}")
                for m in range(2):
                    last = tr(bank[:, P * m:P * m + P], o_sb[:, kind == "ml", P * m:P * m + P])
                close_bank(last)

            def out_projection(l):
                c0 = P * FIRST_T[l]
                pe.wait_ge(evacuated, len(entry))
                for n in range(2):
                    w = wait_chunk(("out", l, n, 0)).rearrange("p (k n) -> p k n", n=512)
                    for m in range(4):
                        name = f"mix{l}{4 * n + m}"
                        bank = open_bank(name)
                        for k in range(KT):
                            last = nc.tensor.matmul(bank[:, 0:T - c0], w[:, k, P * m:P * m + P], u[:, k, c0:T],
                                                    start=(k == 0), stop=(k == KT - 1))
                        close_bank(last)
                    free_chunk(("out", l, n, 0), name)

            def router(l):
                bank = open_bank(f"logits{l}")
                for i, t in enumerate(range(FIRST_T[l], TT)):
                    for k in range(KT):
                        if i == 0:
                            pe.wait_ge(S("u_ready"), ready_base[f"{l}ffn"] + (2 if l == 0 else 1) * (k + 1))
                        last = nc.tensor.matmul(bank[:, NE * t:NE * t + NE], u[:, k, P * t:P * t + P], rw[:, k, :],
                                                start=(k == 0), stop=(k == KT - 1))
                close_bank(last)

            def to_rows(l):
                for t in range(FIRST_T[l], TT):
                    for half in range(2):
                        bank = open_bank(f"ut{l}{t}{half}")
                        for m in range(4):
                            last = tr(bank[:, P * m:P * m + P], u[:, 4 * half + m, P * t:P * t + P])
                        close_bank(last)

            def places(l):
                tiles = range(FIRST_T[l], TT)
                pe.wait_ge(S("chosen_ready"), l + 1)
                bank = open_bank(f"places{l}")
                chosen = rt[:, 11, :, :]
                for t in tiles:
                    for t2 in range(FIRST_T[l], t):
                        nc.tensor.matmul(bank[:, NE * t:NE * t + NE], ones[:, :], chosen[:, t2, :],
                                         start=(t2 == FIRST_T[l]), stop=False)
                    nc.tensor.matmul(bank[:, NE * t:NE * t + NE], tri[0], chosen[:, t, :],
                                     start=(t == FIRST_T[l]), stop=True)
                for t in tiles:
                    last = nc.tensor.matmul(bank[:, NE * TT:NE * TT + NE], ones[:, :], chosen[:, t, :],
                                            start=(t == FIRST_T[l]), stop=(t == TT - 1))
                close_bank(last)

            def experts(l):
                base, tiles = moe_base[l], range(FIRST_T[l], TT)
                nt = len(tiles)
                pe.wait_ge(S("passes_ready"), l + 1)
                n_more = nc.tensor.value_load(passes[0:1, l:l + 1], min_val=0, max_val=TT - 1)
                with pe.Fori(0, n_more + 1) as p:
                    with pe.Fori(0, NE // GROUP) as q:
                        for j in range(GROUP):
                            for i, t in enumerate(tiles):
                                k = j * nt + i
                                pe.wait_ge(S("onehot_ready", l), p * (NE * nt) + q * (GROUP * nt) + (k + 1))
                                last = nc.tensor.matmul(ps[:, 4, 3 * j:3 * j + 3], onehot[:, k, :],
                                                        vals[:, t, bass.ds(q * GROUP + j, 1), :].rearrange(
                                                            "p o c -> p (o c)"), start=(i == 0), stop=(i == nt - 1))
                        last.then_inc(S("lists_summed", l), 1)
                        pe.wait_ge(S("lists_ready", l), p * (NE // GROUP) + q + 1)

                    def wait_slot(q, n, kind):
                        c = chunk_place(kind, n)
                        rounds = 16 * GROUP * PER_EXPERT // RING
                        pe.wait_ge(landed[l][(base + c) % RING], p * (rounds * NE // GROUP) + q * rounds
                                   + landed_count(base + c))
                        return ring[:, (base + c) % RING, :]

                    def turn_x(q, n, half):
                        if half == 0:
                            pe.wait_ge(S(f"gathered{n % GATHERS}", l), p * (16 * NE // GATHERS)
                                       + q * (16 * GROUP // GATHERS) + 16 * (n // GATHERS + 1))
                        else:
                            pe.wait_ge(S("x_t_ready", l), p * (2 * NE) + q * (2 * GROUP) + (2 * n + 1))
                        for m in range(4):
                            k = 4 * half + m
                            last = tr(ps[:, 4, P * m:P * m + P], x_slots[:, n % GATHERS, P * k:P * k + P])
                        last.then_inc(S("x_turned", l), 1)

                    def project_up(q, n, kind):
                        w = wait_slot(q, n, kind).rearrange("p (k n) -> p k n", n=DE)
                        if kind == 0:
                            pe.wait_ge(S("x_t_ready", l), p * (2 * NE) + q * (2 * GROUP) + (2 * n + 2))
                        for k in range(KT):
                            last = nc.tensor.matmul(ps[:, 2 * (n % 2) + kind, :], x_t[:, n % 2, k, :], w[:, k, :],
                                                    start=(k == 0), stop=(k == KT - 1))
                        last.then_inc(S("gate_done" if kind == 0 else "up_done", l), 1)

                    def project_down(q, n):
                        pe.wait_ge(S("hid_t_ready", l), p * NE + q * GROUP + (n + 1))
                        pe.wait_ge(S("y_scaled", l), p * NE + q * GROUP + (n + 1))
                        w = wait_slot(q, n, 2).rearrange("p (f n) -> p f n", n=DM)
                        for b in range(2):
                            for f in range(4):
                                last = nc.tensor.matmul(ps[:, 6 + b, :], hid_t[:, f, :],
                                                        w[:, f, 512 * b:512 * b + 512], start=(f == 0), stop=(f == 3))
                        last.then_inc(S("down_done", l), 1)

                    def turn_hidden(q, n):
                        pe.wait_ge(S("hid_ready", l), p * NE + q * GROUP + (n + 1))
                        for f in range(4):
                            last = tr(ps[:, 5, P * f:P * f + P], hid[:, P * f:P * f + P])
                        last.then_inc(S("hid_turned", l), 1)

                    def step(q, n):
                        project_up(q, n + 1, 0)
                        if n + 2 < NE:
                            turn_x(q, n + 2, 0)
                        project_up(q, n + 1, 1)
                        if n + 2 < NE:
                            turn_x(q, n + 2, 1)
                        project_down(q, n)
                        turn_hidden(q, n + 1)

                    turn_x(0, 0, 0)
                    turn_x(0, 0, 1)
                    project_up(0, 0, 0)
                    turn_x(0, 1, 0)
                    project_up(0, 0, 1)
                    turn_x(0, 1, 1)
                    turn_hidden(0, 0)
                    with pe.Fori(0, STEPS) as q:
                        for n in range(GROUP):
                            step(q, n)
                    for n in range(STEPS * GROUP, NE - 1):
                        step(0, n)
                    project_down(0, NE - 1)

            def add_experts(l):
                tiles = range(FIRST_T[l], TT)
                pe.wait_ge(S("y_combined", l), len(tiles))
                for m in range(KT):
                    bank = open_bank(f"y{l}{m}")
                    for t in tiles:
                        last = tr(bank[:, P * t:P * t + P], y_tok[:, t, P * m:P * m + P])
                    close_bank(last)

            pe.wait_ge(S("const_landed"), 16 * (1 + n_vec_dmas))
            pe.wait_ge(S("ones_ready"), 2)
            bank = open_bank("vecs")
            for l in range(DEPTH):
                last = tr(bank[:, P * l:P * l + NVEC], vecrows[0:NVEC, l, :])
            close_bank(last)
            pe.wait_ge(S("tokens_landed"), 32)
            for t in range(TT):
                for half in range(2):
                    bank = open_bank(f"h{t}{half}")
                    for m in range(4):
                        last = tr(bank[:, P * m:P * m + P], tok[:, t, 512 * half + P * m:512 * half + P * m + P])
                    close_bank(last)
            for l in range(DEPTH):
                mean_square(f"ms{l}mix", (S("squares"), eights[f"{l}mix"]), u, KT, 0)
                if l == 0:
                    pe.wait_ge(S("cond_ready"), 1)
                    modulation(0, 0)
                project(l)
                if l == 0:
                    for g in (1, 2):
                        modulation(0, g)
                    for g in range(3):
                        modulation(1, g)
                latents_up(l)
                rotate(l)
                scan(l)
                attention(l)
                out_projection(l)
                c0 = P * FIRST_T[l]
                mean_square(f"ms{l}ffn", (S("squares"), eights[f"{l}ffn"]), u, KT, c0)
                router(l)
                to_rows(l)
                places(l)
                experts(l)
                add_experts(l)
            mean_square("msfinal", (S("squares"), eights["final"]), u, KT, NCTX)
            for t in (2, 3):
                for half in range(2):
                    bank = open_bank(f"out{t}{half}")
                    for m in range(4):
                        k = 4 * half + m
                        pe.wait_ge(S("u_ready"), ready_base["final"] + k + 1)
                        last = tr(bank[:, P * m:P * m + P], u[:, k, P * t:P * t + P])
                    close_bank(last)

        @block.vector
        def _(dve):
            step = Tally(S("vector_step"))
            read = Tally(evacuated)

            def link(ins):
                dve.wait_ge(step.sem, step.by(ins))

            def claim(name):
                assert read.n == entry[name], (name, read.n, entry[name])
                dve.wait_ge(filled, read.n + 1)
                return ps[:, read.n % 2, :]

            def emptied(ins):
                read.by(ins)

            def own_read():
                dve.wait_ge(read.sem, read.n)

            v = nc.vector
            tt, ts, stt = v.tensor_tensor, v.tensor_scalar, v.scalar_tensor_tensor

            def modulation(l, g):
                bank = claim(f"mod{l}{g}")
                emptied(v.tensor_copy(modrow[:, :], bank))
                bank = claim(f"modT{l}{g}")
                emptied(tt(mod[:, l, 16 * g:16 * g + 16, :].rearrange("p (j s) c -> p j s c", s=4),
                           bank.rearrange("p (s j r) -> p j s r", s=4, j=4)[:, :, :, 0:2],
                           vec[:, l, 16 * g:16 * g + 16].rearrange("p (j s) -> p j s", s=4).unsqueeze(3)
                           .to_broadcast([P, 4, 4, 2]), ALU.add))
                own_read()
                if g != 1:
                    n, at_v = (0, V_GMIX) if g == 0 else (1, V_GFFN)
                    scale = mod[:, l, 8:16, :] if g == 0 else mod[:, l, 32:40, :]
                    stt(gain[:, l, n, :, :], scale, 1.0,
                        vec[:, l, at_v:at_v + KT].unsqueeze(2).to_broadcast([P, KT, 2]), ALU.add,
                        ALU.mult).then_inc(S("gain_ready"), 1)

            def norm(name, c0):
                bank = claim(f"ms{name}")
                emptied(ts(rstd[:, c0:T], bank[:, 0:T - c0], EPS, None, ALU.add))
                dve.wait_ge(S("rstd_ready"), NORMS.index(name) + 1)
                for k in range(KT):
                    tt(u[:, k, c0:T], h[:, k, c0:T], rstd[:, c0:T], ALU.mult).then_inc(S("u_scaled"), 1)

            def project(l):
                first = FIRST_T[l]
                for m in range(6):
                    bank = claim(f"xbc{l}{m}").rearrange("p (s t) -> p s t", s=2)
                    acc = xbc[:, m, :].rearrange("p (s t) -> p s t", s=2)
                    w = vec[:, l, V_CONVW + m:V_CONVW + 18:6]
                    dve.wait_ge(S("conv_mid"), 6 * l + m + 1)
                    link(stt(acc[:, :, 1:256], bank[:, :, 0:255], w[:, 0:1], acc[:, :, 1:256], ALU.mult, ALU.add))
                    emptied(stt(acc[:, :, 0:255], bank[:, :, 1:256], w[:, 2:3], acc[:, :, 0:255], ALU.mult, ALU.add))
                for i in range(2):
                    emptied(v.tensor_copy(v_da[:, 2 * i:2 * i + 2, :],
                                          claim(f"v{l}{i}").rearrange("p (t n) -> p t n", n=256)))
                bank = claim(f"dt{l}")[:, 0:64].rearrange("p (t d h) -> p d t h", t=TT, d=2)
                emptied(tt(sc[:, 0, :].rearrange("p (d t h) -> p d t h", d=2, t=TT), bank,
                           bcast[:, l, B_DTB:B_DTB + 16].rearrange("p (d h) -> p d h", d=2).unsqueeze(2)
                           .to_broadcast([P, 2, TT, SSD_H]), ALU.add))
                for m in range(3):
                    emptied(v.tensor_copy(latent[:, m, :], claim(f"lat{l}{m}")))
                emptied(v.tensor_copy(km[NOPE:HD, 0, :], claim(f"kr{l}")[NOPE:HD, :]))
                for m in range(4):
                    c0 = 0 if m >= 2 or l == 0 else NCTX
                    emptied(v.tensor_copy(qk[:, m, c0:T], claim(f"qk{l}{m}")[:, 0:T - c0]))
                for t in range(first, TT):
                    emptied(v.tensor_copy(z[:, t, :], claim(f"z{l}{t}")))

            def latents_up(l):
                c0 = P * FIRST_T[l]
                bank = claim(f"cqms{l}")
                emptied(ts(r_lat[:, 0, c0:T], bank[:, 0:T - c0], DM / QR, EPS, ALU.mult, ALU.add))
                bank = claim(f"ckvms{l}")
                emptied(ts(r_lat[:, 1, :], bank, DM / KVR, EPS, ALU.mult, ALU.add))
                dve.wait_ge(S("r_lat_ready"), 2 * l + 2)
                for m in range(3):
                    g = vec[:, l, V_QG + m:V_QG + m + 1]
                    cc = c0 if m < 2 else 0
                    stt(latent[:, m, cc:T], latent[:, m, cc:T], g, r_lat[:, m // 2, cc:T], ALU.mult,
                        ALU.mult).then_inc(S("latent_normed"), 1)
                for hh in range(DA_H):
                    emptied(v.tensor_copy(qm[0:HD, hh, c0:T], claim(f"qm{l}{hh}")[0:HD, 0:T - c0]))
                for hh in range(DA_H):
                    emptied(v.tensor_copy(km[0:NOPE, hh, :], claim(f"km{l}{hh}")[0:NOPE, :]))
                for i in range(2):
                    emptied(v.tensor_copy(v_ml[:, 2 * i:2 * i + 2, :],
                                          claim(f"vm{l}{i}").rearrange("p (t n) -> p t n", n=256)))

            def rope(dst, bank, cos, sin, r):
                emptied(tt(rope_tmp[r, :], bank[r, 0:NLAT], sin[r, :], ALU.mult))
                link(tt(dst, dst, cos[r, :], ALU.mult))
                own_read()
                link(tt(dst, dst, rope_tmp[r, :], ALU.add))

            def rotate(l):
                cos, sin = cst[:, C_COS:C_COS + NLAT], cst[:, C_SIN:C_SIN + NLAT]
                for m in range(4):
                    rope(qk[:, m, NCTX:T], claim(f"qkrot{l}{m}"), cos, sin, slice(0, P))
                for hh in range(DA_H):
                    rope(qm[0:HD, hh, NCTX:T], claim(f"qmrot{l}{hh}"), cst[:, C_MCOS:C_MCOS + NLAT],
                         cst[:, C_MSIN:C_MSIN + NLAT], slice(0, HD))
                rope(km[NOPE:HD, 0, NCTX:T], claim(f"krrot{l}"), cos, sin, slice(NOPE, HD))
                v.tensor_copy(km[NOPE:HD, 1:4, :], km[NOPE:HD, 0:1, :].to_broadcast([ROPE, 3, T])).then_inc(
                    S("roped"), 1)

            def scan(l):
                first = FIRST_T[l]
                stt(sc[:, 1, :], sc[:, 0, :], -1.0, sc[:, 0, :], ALU.mult, ALU.max).then_inc(S("dt_abs"), 1)
                dve.wait_ge(S("dt_exp"), 2 * l + 1)
                ts(sc[:, 3, :], sc[:, 2, :], 1.0, None, ALU.add).then_inc(S("dt_u"), 1)
                dve.wait_ge(S("dt_u"), l + 1)
                link(ts(sc[:, 4, :], sc[:, 3, :], 1.0, None, ALU.is_equal))
                link(stt(sc[:, 5, :], sc[:, 3, :], -1.0, sc[:, 4, :], ALU.add, ALU.add))
                link(v.reciprocal(sc[:, 5, :], sc[:, 5, :]))
                dve.wait_ge(S("dt_exp"), 2 * l + 2)
                link(tt(sc[:, 5, :], sc[:, 5, :], sc[:, 6, :], ALU.mult))
                link(tt(sc[:, 5, :], sc[:, 5, :], sc[:, 4, :], ALU.add))
                link(tt(sc[:, 5, :], sc[:, 5, :], sc[:, 2, :], ALU.mult))
                link(stt(sc[:, 1, :], sc[:, 0, :], 0.0, sc[:, 5, :], ALU.max, ALU.add))
                link(stt(sc[:, 2, 0:32].rearrange("p (t h) -> p t h", t=TT),
                         sc[:, 1, 0:32].rearrange("p (t h) -> p t h", t=TT), -1.0,
                         sc[:, 7, 0:8].unsqueeze(1).to_broadcast([P, TT, SSD_H]), ALU.mult, ALU.mult))
                stt(sc[:, 2, 32:64].rearrange("p (t h) -> p t h", t=TT),
                    sc[:, 1, 32:64].rearrange("p (t h) -> p t h", t=TT), -1.0,
                    sc[:, 7, 8:16].unsqueeze(1).to_broadcast([P, TT, SSD_H]), ALU.mult,
                    ALU.mult).then_inc(S("da_ready"), 1)
                for t in range(TT):
                    emptied(v.tensor_copy(xbc[:, 0:4, P * t:P * t + P],
                                          claim(f"xs{l}{t}").rearrange("p (m n) -> p m n", n=P)))
                emptied(v.tensor_copy(b_tok, claim(f"btok{l}").rearrange("p (t n) -> p t n", n=P)))
                bank = claim(f"cum{l}")
                emptied(v.tensor_copy(sc[:, 8:10, :], bank[:, 0:128].rearrange("p (a n) -> p a n", n=64)))
                own_read()
                tt(sc[:, 10, :], sc[:, 9, :], sc[:, 8, :], ALU.subtract).then_inc(S("cum_ready"), 1)
                dve.wait_ge(S("decays_ready"), l + 1)
                tt(sc[:, 5, :], sc[:, 5, :], sc[:, 1, :], ALU.mult).then_inc(S("to_end_ready"), 1)
                first_of = {0: 0, 1: 1}
                for d in range(2):
                    v.memset(state[:, d, first_of[d], :], 0.0).then_inc(S("state_zeroed", l), 1)
                dve.wait_ge(S("state_zeroed", l), 2)
                for n, (d, t, nxt) in enumerate(state_steps(l)):
                    bank = claim(f"state{l}{n}")
                    for g in range(2):
                        r = slice(64 * g, 64 * g + 64)
                        dec = sc[r, 4, 32 * d + 8 * t + 4 * g:32 * d + 8 * t + 4 * g + 4]
                        last = tt(state[r, d, nxt, :].rearrange("p (h n) -> p h n", n=64),
                                  state[r, d, t, :].rearrange("p (h n) -> p h n", n=64),
                                  dec.unsqueeze(2).to_broadcast([64, 4, 64]), ALU.mult)
                    link(last)
                    emptied(tt(state[:, d, nxt, :], state[:, d, nxt, :], bank[:, 0:256], ALU.add))
                    own_read()
                dve.sem_inc(S("states_done"), 1)
                for i, t in enumerate(range(first, TT)):
                    if i:
                        dve.wait_ge(S("w_ready", l), 2 * i)
                    for g in range(2):
                        bank = claim(f"cb{l}{t}{g}")
                        for d in range(2):
                            last = tt(gm[:, d, g, :], bank[:, 0:P], tri[d], ALU.mult)
                        emptied(last)
                    for d in range(2):
                        n = 2 * i + d
                        dve.wait_ge(S("rows_cast", l), n + 1)
                        for hh in range(SSD_H):
                            last = ts(ew[:, d, hh, :], ps[:, 2 + hh // 4, P * (hh % 4):P * (hh % 4) + P],
                                      sc[:, 8, 32 * d + 8 * t + hh:32 * d + 8 * t + hh + 1], 0.0, ALU.subtract,
                                      ALU.min)
                        last.then_inc(S("decay_clamped", l), 1)
                    if i:
                        y_turned(l, t - 1)
                    dve.wait_ge(S("y_summed", l), i + 1)
                    for d, dst in ((1, y_two), (0, y_acc)):
                        last = tt(dst.rearrange("p (g h n) -> p g h n", g=2, h=4),
                                  ps[:, 5:7, 256 * d:256 * d + 256].rearrange("p g (h n) -> p g h n", h=4),
                                  sc[:, 3, 32 * d + 8 * t:32 * d + 8 * t + 8].rearrange("p (g h) -> p g h", g=2)
                                  .unsqueeze(3).to_broadcast([P, 2, 4, SSD_P]), ALU.mult)
                    link(last)
                    link(tt(y_acc, y_acc, y_two, ALU.add))
                    tt(y_acc, y_acc, ps[:, 4, :], ALU.add).then_inc(S("y_banks_read", l), 1)
                    dve.wait_ge(S("y_banks_read", l), i + 1)
                    dve.wait_ge(S("skip_ready", l), i + 1)
                    link(tt(y_acc, y_acc, y_skip, ALU.add))
                    dve.wait_ge(S("z_ready"), l + 1)
                    tt(y_acc, y_acc, z[:, t, :], ALU.mult).then_inc(S("y_gated", l), 1)
                    dve.wait_ge(S("y_gated", l), i + 1)
                    dve.wait_ge(S("y_squared", l), i + 1)
                    ts(y_acc, y_acc, small[:, 0:1], None, ALU.mult).then_inc(S("y_normed", l), 1)
                y_turned(l, TT - 1)

            def y_turned(l, t):
                bank = claim(f"yT{l}{t}")
                for m in range(4):
                    last = ts(u[:, 2 + m, P * t:P * t + P], bank[:, P * m:P * m + P],
                              vec[:, l, V_SSDG + m:V_SSDG + m + 1], None, ALU.mult)
                emptied(last)

            def lam(l):
                lv = bcast[:, l, B_LAM:B_LAM + 128].rearrange("p (a b n) -> p a b n", a=2, b=2)
                link(tt(o_sq[:, 0:64].rearrange("p (a n) -> p a n", a=2), lv[:, :, 0, :], lv[:, :, 1, :], ALU.mult))
                v.tensor_reduce(small[:, 4:6], o_sq[:, 0:64].rearrange("p (a n) -> p a n", a=2), AX.X,
                                ALU.add).then_inc(S("lam_sums"), 1)
                dve.wait_ge(S("lam_exp"), l + 1)
                link(tt(small[:, 8:9], small[:, 7:8], small[:, 6:7], ALU.subtract))
                link(ts(small[:, 8:9], small[:, 8:9], lam_init(l), None, ALU.subtract))

            def attention(l):
                units = attention_units(l)
                mx, nb, rs, rr = (stats[:, s] for s in range(4))
                lam(l)
                for s in range(len(units) + 1):
                    if s < len(units):
                        kind, t, hh, nk = units[s]
                        nm = 2 if kind == "da" else 1
                        pair = 2 + 2 * (s % 2)
                        dve.wait_ge(S("scores_done"), units0 * l + s + 1)
                        link(v.tensor_reduce(mx[:, s, 0:nm], ps[:, pair:pair + nm, 0:nk], AX.X, ALU.max))
                        ts(nb[:, s, 0:nm], mx[:, s, 0:nm], -(DA_SCALE if kind == "da" else MLA_SCALE), None,
                           ALU.mult).then_inc(S("max_ready"), 1)
                    if s >= 1:
                        n = s - 1
                        kind, t, hh, nk = units[n]
                        dve.wait_ge(S("exp_done"), units0 * l + n + 1)
                        if kind == "da":
                            link(v.reciprocal(rr[:, n, :], rs[:, n, :]))
                            link(tt(rr[:, n, 1:2], rr[:, n, 1:2], small[:, 8:9], ALU.mult))
                            link(ts(probs[:, n % 2, 1, 0:nk], probs[:, n % 2, 1, 0:nk], rr[:, n, 1:2], None, ALU.mult))
                            stt(probs[:, n % 2, 0, 0:nk], probs[:, n % 2, 0, 0:nk], rr[:, n, 0:1],
                                probs[:, n % 2, 1, 0:nk], ALU.mult, ALU.add).then_inc(S("mixed"), 1)
                        else:
                            link(v.reciprocal(rr[:, n, 0:1], rs[:, n, 0:1]))
                        if n % 4 == 0 and n >= 4:
                            head_out(l, n - 4)
                head_out(l, len(units) - 4)

            def head_out(l, n0):
                kind, t, _, _ = attention_units(l)[n0]
                bank = claim(f"o{kind}{l}{t}")[:, 0:256].rearrange("p (h n) -> p h n", n=DA_V)
                ob = o_sb[:, int(kind == "ml"), :].rearrange("p (h n) -> p h n", n=DA_V)
                if kind == "ml":
                    emptied(tt(ob, bank, stats[:, 3, n0:n0 + 4, 0:1].to_broadcast([P, DA_H, DA_V]), ALU.mult))
                    own_read()
                    dve.sem_inc(S("o_ready"), 1)
                else:
                    emptied(v.tensor_copy(ob, bank))
                    own_read()
                    sq = o_sq.rearrange("p (h n) -> p h n", n=DA_V)
                    link(tt(sq, ob, ob, ALU.mult))
                    v.tensor_reduce(small[:, 12:16], sq, AX.X, ALU.add).then_inc(S("o_squared"), 1)
                    dve.wait_ge(S("o_rstd"), units0 // 8 * l + t - FIRST_T[l] + 1)
                    tt(ob, ob, small[:, 12:16].unsqueeze(2).to_broadcast([P, DA_H, DA_V]),
                       ALU.mult).then_inc(S("o_ready"), 1)
                bank = claim(f"oT{kind}{l}{t}")
                for m in range(2):
                    if kind == "da":
                        last = ts(u[:, m, P * t:P * t + P], bank[:, P * m:P * m + P], vec[:, l, V_SUBG:V_SUBG + 1],
                                  1.0 - lam_init(l), ALU.mult, ALU.mult)
                    else:
                        last = v.tensor_copy(u[:, 6 + m, P * t:P * t + P], bank[:, P * m:P * m + P])
                emptied(last)

            def residual(l, name, gate):
                c0 = P * FIRST_T[l]
                for m in range(KT):
                    bank = claim(f"{name}{l}{m}")
                    off = c0 if name == "mix" else 0
                    for s in range(c0 // NCTX, 2):
                        a = NCTX * s
                        last = stt(h[:, m, a:a + NCTX], bank[:, a - off:a - off + NCTX],
                                   mod[:, l, gate + m, s:s + 1], h[:, m, a:a + NCTX], ALU.mult, ALU.add)
                    emptied(last)

            def router(l):
                f = FIRST_T[l]
                lg, aff, sel, pair, w1, w2, w3, oh1, oh2, sm, key, msk = (rt[:, s, f:TT, :] for s in range(12))
                n = TT - f

                def g4(ap):
                    return ap.rearrange("p t (g e) -> p t g e", g=NG)

                bank = claim(f"logits{l}")[:, 0:TT * NE].rearrange("p (t e) -> p t e", e=NE)[:, f:TT, :]
                emptied(v.tensor_copy(lg, bank))
                for t in range(f, TT):
                    for half in range(2):
                        emptied(v.tensor_copy(u_tok[:, t, 512 * half:512 * half + 512], claim(f"ut{l}{t}{half}")))
                dve.wait_ge(S("logits_exp"), l + 1)
                link(ts(aff, aff, 1.0, None, ALU.add))
                link(v.reciprocal(aff, aff))
                link(tt(sel, aff, bcast[:, l, B_RB:B_RB + NE].unsqueeze(1).to_broadcast([P, n, NE]), ALU.add))
                s4 = g4(sel)
                pr = pair.rearrange("p t (g e) -> p t g e", g=NG)
                pr2 = w1.rearrange("p t (g e) -> p t g e", g=NG)
                for t in range(n):
                    tt(pr[:, t, :, 0:3], s4[:, t, :, 0:3], s4[:, t, :, 1:4], ALU.add)
                    tt(pr2[:, t, :, 0:2], s4[:, t, :, 0:2], s4[:, t, :, 2:4], ALU.add)
                    link(tt(pr[:, t, :, 3:4], s4[:, t, :, 0:1], s4[:, t, :, 3:4], ALU.add))
                    link(tt(pr[:, t, :, 0:2], pr[:, t, :, 0:2], pr2[:, t, :, 0:2], ALU.max))
                gs = w2[:, :, 0:4]
                gb = w2[:, :, 4:5]
                gk = w2[:, :, 8:12]
                link(v.tensor_reduce(gs, pr, AX.X, ALU.max))
                link(v.tensor_reduce(gb, gs, AX.X, ALU.max))
                link(tt(gk, gs, gb.to_broadcast([P, n, 4]), ALU.is_equal))
                link(tt(gk, gk, cst[:, C_PG:C_PG + NG].unsqueeze(1).to_broadcast([P, n, 4]), ALU.mult))
                link(v.tensor_reduce(gb, gk, AX.X, ALU.max))
                link(tt(gk, gk, gb.to_broadcast([P, n, 4]), ALU.is_equal))
                for t in range(n):
                    last = v.tensor_copy(g4(msk)[:, t], gk[:, t, :].unsqueeze(2).to_broadcast([P, NG, 4]))
                link(last)
                link(tt(sm, sel, msk, ALU.mult))
                link(ts(msk, msk, -1.0, 1e30, ALU.add, ALU.mult))
                link(tt(sm, sm, msk, ALU.add))
                for oh in (oh1, oh2):
                    link(v.tensor_reduce(w3[:, :, 0:1], sm, AX.X, ALU.max))
                    link(tt(key, sm, w3[:, :, 0:1].to_broadcast([P, n, NE]), ALU.is_equal))
                    link(tt(key, key, cst[:, C_PE:C_PE + NE].unsqueeze(1).to_broadcast([P, n, NE]), ALU.mult))
                    link(v.tensor_reduce(w3[:, :, 0:1], key, AX.X, ALU.max))
                    link(tt(oh, key, w3[:, :, 0:1].to_broadcast([P, n, NE]), ALU.is_equal))
                    if oh is oh1:
                        link(stt(sm, oh, -2e30, sm, ALU.mult, ALU.add))
                tt(msk, oh1, oh2, ALU.add).then_inc(S("chosen_ready"), 1)
                dve.wait_ge(S("chosen_ready"), l + 1)
                link(tt(oh1, msk, aff, ALU.mult))
                link(v.tensor_reduce(w3[:, :, 0:1], oh1, AX.X, ALU.add))
                link(v.reciprocal(w3[:, :, 0:1], w3[:, :, 0:1]))
                tok_id = cst[:, C_TOK + f:C_TOK + TT].unsqueeze(2).to_broadcast([P, n, NE])
                vl = vals[:, f:TT, :, :]
                tt(vl[:, :, :, 2], oh1, w3[:, :, 0:1].to_broadcast([P, n, NE]), ALU.mult)
                ts(vl[:, :, :, 0], tok_id, -float(NOWHERE + P * f), None, ALU.add)
                link(ts(key, oh2, float(T), -float(NOWHERE), ALU.mult, ALU.add))
                link(tt(vl[:, :, :, 1], key, tok_id, ALU.add))
                bank = claim(f"places{l}")
                ps_pl = bank[:, 0:TT * NE].rearrange("p (t e) -> p t e", e=NE)[:, f:TT, :]
                link(tt(pos[:, f:TT, :], ps_pl, msk, ALU.mult))
                emptied(v.tensor_reduce(small[:, 24:25], bank[:, NE * TT:NE * TT + NE], AX.X, ALU.max))
                link(ts(pos[:, f:TT, :], pos[:, f:TT, :], -1.0, None, ALU.add))
                own_read()
                link(ts(small[:, 25:26], small[:, 24:25], float(P), None, ALU.is_gt))
                for k in range(2, n):
                    link(stt(small[:, 25:26], small[:, 24:25], float(k * P), small[:, 25:26], ALU.is_gt, ALU.add))
                v.tensor_copy(passes[:, l:l + 1], small[:, 25:26]).then_inc(S("passes_ready"), 1)

            def experts(l):
                tiles = range(FIRST_T[l], TT)
                nt = len(tiles)
                iota = cst[:, C_IOTA:C_IOTA + P]
                dve.wait_ge(S("passes_ready"), l + 1)
                dve.sem_inc(S("y_scaled", l), 1)
                n_more = v.value_load(passes[0:1, l:l + 1], min_val=0, max_val=TT - 1)
                with dve.Fori(0, n_more + 1) as p:
                    dve.wait_ge(S("scatters_ended", l), p * (NE + 1) + 1)
                    alone(dve)
                    with dve.Fori(0, NE // GROUP) as q:
                        for j in range(GROUP):
                            for i, t in enumerate(tiles):
                                ts(onehot[:, j * nt + i, :], iota, pos[:, t, bass.ds(q * GROUP + j, 1)], None,
                                   ALU.is_equal).then_inc(S("onehot_ready", l), 1)
                        dve.wait_ge(S("lists_summed", l), p * (NE // GROUP) + q + 1)
                        sums = ps[:, 4, 0:3 * GROUP].rearrange("p (j c) -> p j c", c=3)
                        here = bass.ds(q * GROUP, GROUP)
                        ts(row_in[:, here], sums[:, :, 0], float(NOWHERE), None, ALU.add)
                        ts(row_out[:, here], sums[:, :, 1], float(NOWHERE), None, ALU.add)
                        v.tensor_copy(gate_list[:, here], sums[:, :, 2]).then_inc(S("lists_ready", l), 1)
                    ts(pos[:, FIRST_T[l]:TT, :], pos[:, FIRST_T[l]:TT, :], -float(P), None,
                       ALU.add).then_inc(S("pos_moved", l), 1)
                    dve.wait_ge(S("pos_moved", l), p + 1)

                    def hidden(q, n):
                        dve.wait_ge(S("silu_done", l), p * NE + q * GROUP + (n + 1))
                        dve.wait_ge(S("up_done", l), p * NE + q * GROUP + (n + 1))
                        tt(hid, silu_g, ps[:, 2 * (n % 2) + 1, :], ALU.mult).then_inc(S("hid_ready", l), 1)

                    def scale(q, n):
                        dve.wait_ge(S("down_done", l), p * NE + q * GROUP + (n + 1))
                        dve.wait_ge(S("scatters_ended", l), p * (NE + 1) + q * GROUP + (n + 1))
                        ts(y_slots[:, n % 2, :].rearrange("p (b n) -> p b n", b=2), ps[:, 6:8, :],
                           gate_list[:, bass.ds(q * GROUP + n, 1)], None, ALU.mult).then_inc(S("y_scaled", l), 1)

                    hidden(0, 0)
                    with dve.Fori(0, STEPS) as q:
                        for n in range(GROUP):
                            hidden(q, n + 1)
                            scale(q, n)
                    for n in range(STEPS * GROUP, NE - 1):
                        hidden(0, n + 1)
                        scale(0, n)
                    scale(0, NE - 1)
                dve.wait_ge(S("y_back", l), 32 * nt)
                for t in tiles:
                    tt(y_tok[:, t, :], y_tok[:, t, :], y_tok2[:, t, :], ALU.add).then_inc(S("y_combined", l), 1)

            v.memset(ones[:, :], 1.0).then_inc(S("ones_ready"), 1)
            v.memset(ones_mean[:, :], 1.0 / DM).then_inc(S("ones_ready"), 1)
            v.memset(small[:, 20:21], EPS)
            link(v.memset(cond[:, :, :], 0.0))
            emptied(v.tensor_copy(vec[:, :, :], claim("vecs")[:, 0:2 * P].rearrange("p (l n) -> p l n", l=2)
                                  [:, :, 0:NVEC]))
            own_read()
            dve.wait_ge(S("cond_exp"), 1)
            link(ts(small[:, 32:48], small[:, 32:48], 1.0, None, ALU.add))
            link(v.reciprocal(small[:, 32:48], small[:, 32:48]))
            tt(cond[:, :, 0:2].rearrange("p k c -> p c k"), vec[:, 0, V_CCTX:V_CCTX + 16].rearrange(
                "p (c k) -> p c k", c=2), small[:, 32:48].rearrange("p (c k) -> p c k", c=2),
               ALU.mult).then_inc(S("cond_ready"), 1)
            for t in range(TT):
                for half in range(2):
                    emptied(v.tensor_copy(h[:, 4 * half:4 * half + 4, P * t:P * t + P],
                                          claim(f"h{t}{half}").rearrange("p (m n) -> p m n", n=P)))
            dve.wait_ge(S("bcast_landed"), 16 * n_bcast_dmas)
            for l in range(DEPTH):
                norm(f"{l}mix", 0)
                if l == 0:
                    modulation(0, 0)
                project(l)
                if l == 0:
                    for g in (1, 2):
                        modulation(0, g)
                    for g in range(3):
                        modulation(1, g)
                latents_up(l)
                rotate(l)
                scan(l)
                attention(l)
                own_read()
                residual(l, "mix", 16)
                norm(f"{l}ffn", P * FIRST_T[l])
                router(l)
                own_read()
                experts(l)
                residual(l, "y", 40)
            norm("final", NCTX)
            for t in (2, 3):
                for half in range(2):
                    emptied(v.tensor_copy(tok[:, t, 512 * half:512 * half + 512], claim(f"out{t}{half}")))

        @block.scalar
        def _(act):
            a = nc.scalar.activation
            step = Tally(S("scalar_step"))

            def link(ins):
                act.wait_ge(step.sem, step.by(ins))

            def wait_evac(name):
                act.wait_ge(evacuated, entry[name] + 1)

            def rsqrt(dst, src, sem, scale=1.0, bias=0.0):
                link(a(dst, src, ACT.Ln, scale=scale, bias=bias))
                a(dst, dst, ACT.Exp, scale=-0.5).then_inc(sem, 1)

            def norm(name, c0, last_entry, gains, shifts):
                wait_evac(last_entry)
                for k in range(KT):
                    a(u[:, k, c0:T], h[:, k, c0:T], ACT.Square).then_inc(S("squares"), 1)
                wait_evac(f"ms{name}")
                rsqrt(rstd[:, c0:T], rstd[:, c0:T], S("rstd_ready"))
                if gains is not None:
                    act.wait_ge(S("gain_ready"), gains[0])
                for k in range(KT):
                    act.wait_ge(S("u_scaled"), eights[name] + k + 1)
                    if gains is None:
                        a(u[:, k, c0:T], u[:, k, c0:T], ACT.Identity,
                          scale=vec[:, 0, V_FING + k:V_FING + k + 1]).then_inc(S("u_ready"), 1)
                    else:
                        for s in range(c0 // NCTX, 2):
                            cols = u[:, k, NCTX * s:NCTX * s + NCTX]
                            a(cols, cols, ACT.Identity, scale=gains[1][:, k, s:s + 1],
                              bias=shifts[:, k, s:s + 1]).then_inc(S("u_ready"), 1)

            def project(l):
                for m in range(6):
                    act.wait_ge(filled, entry[f"xbc{l}{m}"] + 1)
                    a(xbc[:, m, :], ps[:, entry[f"xbc{l}{m}"] % 2, :], ACT.Identity,
                      scale=vec[:, l, V_CONVW + 6 + m:V_CONVW + 7 + m],
                      bias=vec[:, l, V_CONVB + m:V_CONVB + m + 1]).then_inc(S("conv_mid"), 1)
                for m in range(6):
                    wait_evac(f"xbc{l}{m}")
                    a(xbc[:, m, :], xbc[:, m, :], ACT.Silu).then_inc(S("xbc_ready"), 1)
                for m in range(3):
                    wait_evac(f"lat{l}{m}")
                    a(latent_sq[:, m, :], latent[:, m, :], ACT.Square).then_inc(S("latent_sq"), 1)
                wait_evac(f"z{l}{TT - 1}")
                a(z[:, FIRST_T[l]:TT, :], z[:, FIRST_T[l]:TT, :], ACT.Silu).then_inc(S("z_ready"), 1)
                c0 = P * FIRST_T[l]
                wait_evac(f"cqms{l}")
                rsqrt(r_lat[:, 0, c0:T], r_lat[:, 0, c0:T], S("r_lat_ready"))
                wait_evac(f"ckvms{l}")
                rsqrt(r_lat[:, 1, :], r_lat[:, 1, :], S("r_lat_ready"))

            def scan(l):
                act.wait_ge(S("dt_abs"), l + 1)
                a(sc[:, 2, :], sc[:, 1, :], ACT.Exp, scale=-1.0).then_inc(S("dt_exp"), 1)
                link(a(sc[:, 7, 0:16], bcast[:, l, B_ALOG:B_ALOG + 16], ACT.Exp))
                act.wait_ge(S("dt_u"), l + 1)
                a(sc[:, 6, :], sc[:, 3, :], ACT.Ln).then_inc(S("dt_exp"), 1)
                act.wait_ge(S("cum_ready"), l + 1)
                a(sc[:, 3, :], sc[:, 8, :], ACT.Exp)
                a(sc[:, 4, :], sc[:, 9, :], ACT.Exp)
                a(sc[:, 5, :], sc[:, 10, :], ACT.Exp).then_inc(S("decays_ready"), 1)
                for i in range(TT - FIRST_T[l]):
                    for d in range(2):
                        act.wait_ge(S("decay_clamped", l), 2 * i + d + 1)
                        a(ew[:, d, :, :], ew[:, d, :, :], ACT.Exp).then_inc(S("decay_exp", l), 1)
                    act.wait_ge(S("y_gated", l), i + 1)
                    link(a(y_two, y_acc, ACT.Square, accum_out=small[:, 1:2]))
                    rsqrt(small[:, 0:1], small[:, 1:2], S("y_squared", l), 1.0 / SSD_INNER, small[:, 20:21])

            def attention(l):
                units = attention_units(l)
                mx, nb, rs, rr = (stats[:, s] for s in range(4))
                act.wait_ge(S("lam_sums"), l + 1)
                a(small[:, 6:8], small[:, 4:6], ACT.Exp).then_inc(S("lam_exp"), 1)
                for s in range(len(units) + 1):
                    if s < len(units):
                        kind, t, hh, nk = units[s]
                        nm = 2 if kind == "da" else 1
                        act.wait_ge(S("max_ready"), units0 * l + s + 1)
                        if s >= 2:
                            act.wait_ge(S("probs_turned"), units0 * l + s - 1)
                        for m in range(nm):
                            last = a(probs[:, s % 2, m, 0:nk], ps[:, 2 + 2 * (s % 2) + m, 0:nk], ACT.Exp,
                                     scale=DA_SCALE if kind == "da" else MLA_SCALE, bias=nb[:, s, m:m + 1],
                                     accum_out=rs[:, s, m:m + 1])
                        last.then_inc(S("exp_done"), 1)
                    if s >= 1:
                        n = s - 1
                        nk = units[n][3]
                        act.wait_ge(S("probs_turned"), units0 * l + n + 1)
                        if n >= 2:
                            wait_heads(l, n - 2)
                        nc.scalar.copy(probs_t[:, n % 2, 0:nk // P, :],
                                       ps[:, 6 + n % 2, 0:nk].rearrange("p (k q) -> p k q", q=P)).then_inc(
                            S("probs_t_ready"), 1)
                        if n % 4 == 0 and n >= 4:
                            head_rstd(l, n - 4)
                head_rstd(l, len(units) - 4)

            def head_rstd(l, n0):
                kind, t, _, _ = attention_units(l)[n0]
                if kind == "da":
                    act.wait_ge(S("o_squared"), units0 // 8 * l + t - FIRST_T[l] + 1)
                    rsqrt(small[:, 12:16], small[:, 12:16], S("o_rstd"), 1.0 / DA_V, small[:, 20:21])

            def wait_heads(l, n):
                kind, t, hh, _ = attention_units(l)[n]
                if hh == DA_H - 1:
                    act.wait_ge(filled, entry[f"o{kind}{l}{t}"] + 1)
                else:
                    act.wait_ge(S("heads_done"), 3 * units0 // 4 * l + 3 * (n // 4) + hh + 1)

            def experts(l):
                f = FIRST_T[l]
                wait_evac(f"logits{l}")
                lg, aff = rt[:, 0, f:TT, :], rt[:, 1, f:TT, :]
                a(aff, lg, ACT.Exp, scale=-1.0).then_inc(S("logits_exp"), 1)
                for t in range(f, TT - 1):
                    wait_evac(f"ut{l}{t}1")
                    act.dma_start(u_rows[l][P * (t - f):P * (t - f) + P, :], u_tok[:, t, :]).then_inc(S("u_stored", l), 16)
                act.wait_ge(S("passes_ready"), l + 1)
                n_more = nc.scalar.value_load(passes[0:1, l:l + 1], min_val=0, max_val=TT - 1)
                with act.Fori(0, n_more + 1) as p:
                    def copy_x(q, n, half):
                        act.wait_ge(S("x_turned", l), p * (2 * NE) + q * (2 * GROUP) + (2 * n + half + 1))
                        nc.scalar.copy(x_t[:, n % 2, 4 * half:4 * half + 4, :],
                                       ps[:, 4, :].rearrange("p (k s) -> p k s", s=P)).then_inc(S("x_t_ready", l), 1)

                    def silu(q, n):
                        act.wait_ge(S("gate_done", l), p * NE + q * GROUP + (n + 1))
                        a(silu_g, ps[:, 2 * (n % 2), :], ACT.Silu).then_inc(S("silu_done", l), 1)

                    def copy_hidden(q, n):
                        act.wait_ge(S("hid_turned", l), p * NE + q * GROUP + (n + 1))
                        nc.scalar.copy(hid_t, ps[:, 5, :].rearrange("p (f s) -> p f s", s=P)).then_inc(
                            S("hid_t_ready", l), 1)

                    def step(q, n):
                        silu(q, n + 1)
                        if n + 2 < NE:
                            copy_x(q, n + 2, 0)
                            copy_x(q, n + 2, 1)
                        copy_hidden(q, n + 1)

                    copy_x(0, 0, 0)
                    copy_x(0, 0, 1)
                    silu(0, 0)
                    copy_x(0, 1, 0)
                    copy_x(0, 1, 1)
                    copy_hidden(0, 0)
                    with act.Fori(0, STEPS) as q:
                        for n in range(GROUP):
                            step(q, n)
                    for n in range(STEPS * GROUP, NE - 1):
                        step(0, n)
                act.wait_ge(S("all_scattered", l), 1)
                for t in range(f, TT):
                    for k, dst in enumerate((y_tok, y_tok2)):
                        act.dma_start(dst[:, t, :], y_rows[l][T * k + P * t:T * k + P * t + P, :]).then_inc(
                            S("y_back", l), 16)

            act.dma_start(cst[:, :], consts).then_inc(S("const_landed"), 16)
            for dst, src in vec_loads:
                act.dma_start(dst, src).then_inc(S("const_landed"), 16)
            act.dma_start(tok[:, 0:2, :], ctx.rearrange("b (t p) n -> p (b t) n", p=P)).then_inc(S("tokens_landed"), 16)
            act.dma_start(tok[:, 2:4, :], x.rearrange("b (t p) n -> p (b t) n", p=P)).then_inc(S("tokens_landed"), 16)
            for dst, src in bcast_loads:
                act.dma_start(dst, src).then_inc(S("bcast_landed"), 16)
            act.dma_start(rw[:, :, :], router_w.rearrange("(k p) e -> p k e", p=P)).then_inc(S("bcast_landed"), 16)

            def load_up(l):
                act.dma_start(wuq[:, :, :], mla_w_uq[l].rearrange("(k p) n -> p k n", p=P)).then_inc(S("wu_landed"), 16)
                act.dma_start(wukv[:, :], mla_w_ukv[l]).then_inc(S("wu_landed"), 16)

            load_up(0)
            wait_evac("vecs")
            a(small[:, 32:48], vec[:, 0, V_CCTX:V_CCTX + 16], ACT.Exp, scale=-1.0).then_inc(S("cond_exp"), 1)
            gain_count = {(0, 0): 1, (0, 1): 2, (1, 0): 3, (1, 1): 4}
            for l in range(DEPTH):
                norm(f"{l}mix", 0, "h31" if l == 0 else "y07", (gain_count[(l, 0)], gain[:, l, 0]), mod[:, l, 0:8, :])
                project(l)
                scan(l)
                attention(l)
                if l == 0:
                    load_up(1)
                norm(f"{l}ffn", P * FIRST_T[l], f"mix{l}7", (gain_count[(l, 1)], gain[:, l, 1]), mod[:, l, 24:32, :])
                experts(l)
            norm("final", NCTX, "y17", None, None)

        @block.gpsimd
        def _(pool):
            g = nc.gpsimd

            def hb(ap):
                return ap.unsqueeze(2).to_broadcast([P, SSD_H, SSD_P])

            def xs(t):
                return xbc[:, 0:4, P * t:P * t + P].rearrange("p m (a n) -> p m a n", a=2)

            def xb(ap):
                return ap.rearrange("p (m a) -> p m a", a=2).unsqueeze(3).to_broadcast([P, 4, 2, SSD_P])

            def experts(l):
                pool.sem_inc(S("scatters_ended", l), 1)
                pool.wait_ge(evacuated, entry[f"ut{l}{TT - 1}1"] + 1)
                g.dma_start(u_rows[l][P * (TT - 1 - FIRST_T[l]):P * (TT - FIRST_T[l]), :],
                            u_tok[:, TT - 1, :]).then_inc(S("scattered", l), 16)
                pool.wait_ge(S("passes_ready"), l + 1)
                n_more = g.value_load(passes[0:1, l:l + 1], min_val=0, max_val=TT - 1)
                pool.wait_ge(S("u_stored", l), 16 * (TT - FIRST_T[l] - 1))
                pool.wait_ge(S("scattered", l), 16)
                with pool.Fori(0, n_more + 1) as p:
                    def gather(q, n):
                        pool.wait_ge(S("lists_ready", l), p * (NE // GROUP) + q + (n // GROUP + 1))
                        if n >= GATHERS:
                            pool.wait_ge(S("x_turned", l), p * (2 * NE) + q * (2 * GROUP) + 2 * (n - GATHERS + 1))
                        alone(pool)
                        k = n % GROUP
                        g.tensor_copy(row_in_now[:, k:k + 1], row_in[:, bass.ds(q * GROUP + n, 1)]).then_inc(
                            S("row_in_copied", l), 1)
                        pool.wait_ge(S("row_in_copied", l), p * NE + q * GROUP + (n + 1))
                        alone(pool)
                        g.indirect_dma_start(x_slots[:, n % GATHERS, :], None, u_rows[l],
                                             bass.IndirectOffsetOnAxis(ap=row_in_now[:, k:k + 1], axis=0),
                                             bounds_check=P * (TT - FIRST_T[l]) - 1, oob_is_err=False).then_inc(
                            S(f"gathered{n % GATHERS}", l), 16)

                    def scatter(q, n):
                        pool.wait_ge(S("y_scaled", l), p * NE + q * GROUP + (n + 2))
                        alone(pool)
                        k = n % GROUP
                        g.tensor_copy(row_out_now[:, k:k + 1], row_out[:, bass.ds(q * GROUP + n, 1)]).then_inc(
                            S("row_out_copied", l), 1)
                        pool.wait_ge(S("row_out_copied", l), p * NE + q * GROUP + (n + 1))
                        pool.wait_ge(S("scattered", l), p * (16 * NE) + q * (16 * GROUP) + 16 * (n + 1))
                        pool.sem_inc(S("scatters_ended", l), 1)
                        g.indirect_dma_start(y_rows[l], bass.IndirectOffsetOnAxis(ap=row_out_now[:, k:k + 1], axis=0),
                                             y_slots[:, n % 2, :], None, bounds_check=2 * T - 1,
                                             oob_is_err=False).then_inc(S("scattered", l), 16)

                    for n in range(GATHERS):
                        gather(0, n)
                    with pool.Fori(0, STEPS) as q:
                        for n in range(GROUP):
                            gather(q, n + GATHERS)
                            scatter(q, n)
                    for n in range(STEPS * GROUP, NE):
                        if n + GATHERS < NE:
                            gather(0, n + GATHERS)
                        scatter(0, n)
                    pool.wait_ge(S("scattered", l), p * (16 * NE) + 16 * (NE + 1))
                    pool.sem_inc(S("scatters_ended", l), 1)
                pool.sem_inc(S("all_scattered", l), 1)

            for l in range(DEPTH):
                first = FIRST_T[l]
                pool.wait_ge(S("to_end_ready"), l + 1)
                for n, (d, t, _) in enumerate(state_steps(l)):
                    if n >= 2:
                        pool.wait_ge(filled, entry[f"state{l}{n - 2}"] + 1)
                    g.tensor_tensor(xdt[:, n % 2, :].rearrange("p (m a n) -> p m a n", m=4, a=2), xs(t),
                                    xb(sc[:, 5, 32 * d + 8 * t:32 * d + 8 * t + 8]), ALU.mult).then_inc(
                        S("xde_ready", l), 1)
                for i, t in enumerate(range(first, TT)):
                    for d in range(2):
                        if i:
                            pool.wait_ge(S("y_summed", l), i)
                        g.tensor_tensor(ew[:, d, :, :], tri[d].unsqueeze(1).to_broadcast([P, SSD_H, P]),
                                        sc[:, 2, 32 * d + 8 * t:32 * d + 8 * t + 8].unsqueeze(2).to_broadcast(
                                            [P, SSD_H, P]), ALU.mult).then_inc(S("rows_built", l), 1)
                    for d in range(2):
                        if i == 0:
                            pool.wait_ge(filled, entry[f"state{l}{len(state_steps(l)) - 1}"] + 1)
                        last = g.tensor_tensor(xdt[:, d, :].rearrange("p (m a n) -> p m a n", m=4, a=2), xs(t),
                                               xb(sc[:, 1, 32 * d + 8 * t:32 * d + 8 * t + 8]), ALU.mult)
                    if i:
                        pool.wait_ge(S("y_gated", l), i)
                    g.tensor_tensor(y_skip.rearrange("p (m a n) -> p m a n", m=4, a=2), xs(t),
                                    xb(bcast[:, l, B_D:B_D + 8]), ALU.mult).then_inc(S("skip_ready", l), 1)
                    pool.wait_ge(evacuated, entry[f"cb{l}{t}1"] + 1)
                    for d in range(2):
                        pool.wait_ge(S("decay_exp", l), 2 * i + d + 1)
                        for gg in range(2):
                            part = ew[:, d, 4 * gg:4 * gg + 4, :]
                            last = g.tensor_tensor(part, part, gm[:, d, gg, :].unsqueeze(1).to_broadcast([P, 4, P]),
                                                   ALU.mult)
                        last.then_inc(S("w_ready", l), 1)

                experts(l)

        @block.sync
        def _(sp):
            def chunk_source(key):
                kind, l, n, k = key
                if kind == "mod":
                    return [(2 * 2048, w_mod[l].rearrange("(k p) n -> p k n", p=P)[:, 2 * k:2 * k + 2,
                                                                                 2048 * n:2048 * n + 2048], 0, 2048)]
                w = w_in[l].rearrange("(k p) n -> p k n", p=P)
                if kind == "out":
                    return [(SLOT, w_out[l].rearrange("(k p) n -> p k n", p=P)[:, :, 512 * n:512 * n + 512], 0, 512)]
                if n == "bcv":
                    return [(SLOT, w[:, :, COL_BC:COL_BC + 256], 0, 512), (SLOT, w[:, :, COL_V:COL_V + 256], 256, 512)]
                col, width = IN_COLS[n]
                return [(KT * width, w[:, :, col:col + width], 0, width)]

            def load(i, key):
                if i >= RING:
                    sp.wait_ge(*released[i - RING])
                for total, src, a, row in chunk_source(key):
                    dst = ring[:, i % RING, 0:total].rearrange("p (k n) -> p k n", n=row)[:, :, a:a + src.shape[2]]
                    sp.dma_start(dst, src).then_inc(landed_sem(i), 16)

            def experts(l):
                base = moe_base[l]
                gate = exp_w_gate[l].rearrange("e (k p) n -> p e k n", p=P)
                up = exp_w_up[l].rearrange("e (k p) n -> p e k n", p=P)
                down = exp_w_down[l].rearrange("e (f p) n -> p e f n", p=P)
                readers = [S("gate_done", l), S("up_done", l), S("down_done", l)]

                per = GROUP * PER_EXPERT
                total = NE * PER_EXPERT

                def send(c, q):
                    kind, n = CHUNK_AT[c % total]
                    src, width = ((gate, DE), (up, DE), (down, DM))[kind]
                    slot = (base + c) % RING
                    sp.dma_start(ring[:, slot, :].rearrange("p (o k n) -> p o k n", o=1, n=width),
                                 src[:, bass.ds(q * GROUP + n, 1), :, :]).then_inc(landed[l][slot], 16)

                def wait_reader(c, p, q):
                    kind, n = CHUNK_AT[c - RING]
                    sp.wait_ge(readers[kind], p * NE + q * GROUP + (n + 1))

                for c in range(RING):
                    sp.wait_ge(*released[base + c - RING])
                    send(c, 0)

                def one_pass(p):
                    first = RING + 2
                    for c in range(RING, first):
                        wait_reader(c, p, 0)
                        send(c, 0)
                    with sp.Fori(0, STEPS) as q:
                        for c in range(first, first + per):
                            wait_reader(c, p, q)
                            send(c, q)
                    for c in range(first + STEPS * per, total):
                        wait_reader(c, p, 0)
                        send(c, 0)

                sp.wait_ge(S("passes_ready"), l + 1)
                n_more = nc.sync.value_load(passes[0:1, l:l + 1], min_val=0, max_val=TT - 1)
                with sp.If(n_more > 0):
                    with sp.Fori(0, n_more) as p:
                        one_pass(p)
                        for c in range(total, total + RING):
                            wait_reader(c, p, 0)
                            send(c, 0)
                one_pass(n_more)
                for c in range(total - RING, total):
                    kind, n = CHUNK_AT[c]
                    released[base + c] = (readers[kind], n_more * NE + (n + 1))

            for i, key in enumerate(chunks):
                load(i, key)
            experts(0)
            for i, key in enumerate(after):
                load(second + i, key)
            experts(1)
            for t in (2, 3):
                for half in range(2):
                    sp.wait_ge(evacuated, entry[f"out{t}{half}"] + 1)
                    sp.dma_start(out.rearrange("b (t p) n -> p (b t) n", p=P)[:, t - 2, 512 * half:512 * half + 512],
                                 tok[:, t, 512 * half:512 * half + 512]).then_inc(S("out_stored"), 16)
            sp.wait_ge(S("out_stored"), 64)


_INS = ["x", "c", "ctx", "c_ctx", "norm_mix_g", "norm_ffn_g", "w_mod", "b_mod", "w_in", "w_out", "da_lambda",
        "da_subln_g", "ssd_conv_w", "ssd_conv_b", "ssd_dt_bias", "ssd_a_log", "ssd_d", "ssd_norm_g", "mla_q_norm_g",
        "mla_kv_norm_g", "mla_w_uq", "mla_w_ukv", "router_w", "router_bias", "exp_w_gate", "exp_w_up", "exp_w_down",
        "final_norm_g"]


def kernel(**inputs):
    import concourse.bacc as bacc
    from concourse.bass_utils import run_bass_kernel_spmd as run

    nc = bacc.Bacc("TRN2", target_bir_lowering=False, num_devices=1)
    arrays = {"in_constants": shape_constants()}
    args = [nc.dram_tensor("in_constants", (P, NCONST), F32, kind="ExternalInput").ap()]
    for name in _INS:
        a = np.ascontiguousarray(inputs[name])
        arrays[f"in_{name}"] = a
        args.append(nc.dram_tensor(f"in_{name}", a.shape, mybir.dt.from_np(a.dtype), kind="ExternalInput").ap())
    args.append(nc.dram_tensor("out_0", (1, NLAT, DM), F32, kind="ExternalOutput").ap())
    hybrid_dit_kernel(nc, *args)
    r = run(nc, [arrays], core_ids=[0])
    return r.results[0]["out_0"]
```

```python
import math
from contextlib import ExitStack

import numpy as np

import concourse.bass as bass
from concourse import mybir

ALU = mybir.AluOpType
ACT = mybir.ActivationFunctionType
F32 = mybir.dt.float32
I32 = mybir.dt.int32
BF16 = mybir.dt.bfloat16
PARTS = 3
AX = mybir.AxisListType

P = 128
DM = 1024
KT = DM // P
NCTX, NLAT = 256, 256
T = NCTX + NLAT
TT = T // P
DEPTH = 2
GRID_W = 64
EPS = 1e-6
DA_H, DA_QK, DA_V = 4, 32, 64
SSD_H, SSD_P, SSD_N, SSD_INNER = 8, 64, 64, 512
QR, KVR = 256, 128
NOPE, ROPE = 64, 32
HD = NOPE + ROPE
IN_W = 2480
COL_QK, COL_V, COL_Z, COL_X, COL_BC, COL_DT = 0, 512, 768, 1280, 1792, 2048
NE, NG, DE = 16, 4, 512
DA_SCALE = DA_QK ** -0.5
MLA_SCALE = HD ** -0.5

V_BMOD, V_GMIX, V_GFFN, V_CONVW, V_CONVB, V_QG, V_KVG, V_SSDG, V_SUBG, V_FING, V_CCTX, V_C, NVEC = (
    0, 48, 56, 64, 82, 88, 90, 91, 95, 96, 104, 112, 120)
NVECS = (NVEC, V_FING)
V_GATE_MIX, V_GATE_FFN = 16, 40
B_DTB, B_ALOG, B_D, B_LAM, B_RB, NB = 0, 16, 32, 40, 168, 184
C_ID, C_MF, C_MB, C_ROT, C_COS, C_SIN, C_MROT, C_MCOS, C_MSIN, C_PE, C_PG, C_IOTA, C_TOK, NCONST = (
    0, 128, 256, 384, 512, 768, 1024, 1152, 1408, 1664, 1680, 1684, 1812, 1816)

RING = 4
SLOT = 4096
PER_EXPERT = 3
GROUP = 4
GATHERS = 4
MOD_BANK = 7
DEPTH_GROUPS = 3
MOD_PARTS = [(l, g, kk) for l in range(DEPTH) for g in range(DEPTH_GROUPS) for kk in range(5)]
LAG_OUT, LAG_NORM, LAG_TURN, LAG_PLACE = 7, 8, 9, 10
STEPS = NE // GROUP - 1
NOWHERE = 4096


def shape_constants():
    c = np.zeros((P, NCONST), np.float32)
    i = np.arange(P)
    c[:, C_ID:C_ID + P] = np.eye(P)
    c[:, C_MF:C_MF + P] = i[:, None] <= i[None, :]
    c[:, C_MB:C_MB + P] = i[:, None] >= i[None, :]
    half = DA_QK // 2
    for m in range(P):
        if m % DA_QK < half:
            c[m + half, C_ROT + m] = -1.0
        else:
            c[m - half, C_ROT + m] = 1.0
    rows = NLAT // GRID_W
    row = np.repeat(np.arange(rows), GRID_W).astype(np.float32)
    col = np.tile(np.arange(GRID_W), rows).astype(np.float32)
    nf = DA_QK // 4
    inv = np.float32(10000.0) ** (-np.arange(nf, dtype=np.float32) / np.float32(nf))
    ang = np.concatenate([row[:, None] * inv, col[:, None] * inv], axis=-1)
    cos, sin = np.cos(ang).T, np.sin(ang).T
    for m in range(P):
        c[m, C_COS:C_COS + NLAT] = cos[m % half]
        c[m, C_SIN:C_SIN + NLAT] = sin[m % half]
    c[:NOPE, C_MCOS:C_MCOS + NLAT] = 1.0
    c[NOPE:HD, C_MCOS:C_MCOS + NLAT] = c[NOPE:HD, C_COS:C_COS + NLAT]
    c[NOPE:HD, C_MSIN:C_MSIN + NLAT] = c[NOPE:HD, C_SIN:C_SIN + NLAT]
    c[NOPE:HD, C_MROT + NOPE:C_MROT + HD] = c[NOPE:HD, C_ROT + NOPE:C_ROT + HD]
    c[:, C_PE:C_PE + NE] = NE - np.arange(NE)
    c[:, C_PG:C_PG + NG] = NG - np.arange(NG)
    c[:, C_IOTA:C_IOTA + P] = np.arange(P)
    c[:, C_TOK:C_TOK + TT] = P * np.arange(TT)[None, :] + i[:, None]
    return c


def lam_init(layer):
    return 0.8 - 0.6 * math.exp(-0.3 * layer)


def attention_units(layer):
    return [(kind, t, hh, NCTX if P * t < NCTX else T)
            for t in range(0 if layer == 0 else NCTX // P, TT) for kind in ("da", "ml") for hh in range(DA_H)]


def state_steps(layer):
    return [(0, 0, 1), (1, 1, 0), (0, 1, 2), (1, 0, 3), (0, 2, 3), (1, 3, 2)]


def chunk_place(kind, n):
    if kind == 2:
        return PER_EXPERT * n + 4 if n < NE - 1 else PER_EXPERT * NE - 1
    return kind if n == 0 else PER_EXPERT * n - 1 + kind


CHUNK_AT = {chunk_place(kind, n): (kind, n) for kind in range(3) for n in range(NE)}


def head_part(s, lag):
    g, rest = divmod(s - lag, DA_H)
    return g if rest == 0 and g >= 0 else None


def z_after(layer, n):
    tiles = {1: 0, 3: 1, 5: 2} if layer == 0 else {1: 2, 3: 3}
    return tiles.get(n)


class Tally:

    def __init__(self, sem):
        self.sem, self.n = sem, 0

    def by(self, instruction):
        instruction.then_inc(self.sem, 1)
        self.n += 1
        return self.n


def hybrid_dit_kernel(nc, consts, x, c, ctx, c_ctx, norm_mix_g, norm_ffn_g, w_mod, b_mod, w_in, w_out, da_lambda,
                      da_subln_g, ssd_conv_w, ssd_conv_b, ssd_dt_bias, ssd_a_log, ssd_d, ssd_norm_g, mla_q_norm_g,
                      mla_kv_norm_g, mla_w_uq, mla_w_ukv, router_w, router_bias, exp_w_gate, exp_w_up, exp_w_down,
                      final_norm_g, out):
    with ExitStack() as stack:
        def sb(name, *shape, dtype=F32):
            return stack.enter_context(nc.sbuf_tensor(name, list(shape), dtype))

        sems = {}

        def S(name, layer=None):
            key = name if layer is None else f"{name}_{layer}"
            if key not in sems:
                sems[key] = stack.enter_context(nc.semaphore(key))
            return sems[key]

        FIRST_T = [0, 2]
        cst = sb("cst", P, NCONST)
        ident = cst[:, C_ID:C_ID + P]
        tri = [cst[:, C_MF:C_MF + P], cst[:, C_MB:C_MB + P]]
        ones = sb("ones", P, P)
        ones_mean = sb("ones_mean", P, P)
        h = sb("h", P, KT, T)
        u = sb("u", P, KT, T)
        ring = sb("ring", P, RING, SLOT)
        vec = sb("vec", P, DEPTH, NVEC)
        bcast = sb("bcast", P, DEPTH, NB)
        cond = sb("cond", P, KT, 32)
        modrow = sb("modrow", P, 512)
        mod = sb("mod", P, DEPTH, 48, 2)
        gain = sb("gain", P, DEPTH, 2, KT, 2)
        wuq = sb("wuq", P, 2, DA_H * HD)
        wukv = sb("wukv", P, 512)
        rw = sb("rw", P, KT, NE)
        rstd = sb("rstd", P, T)
        small = sb("small", P, 64)
        rt = sb("rt", P, 12, TT, NE)
        pos = sb("pos", P, TT, NE)
        vals = sb("vals", P, TT, NE, 3)
        gate_list = sb("gate_list", P, NE)
        row_in = sb("row_in", P, NE, dtype=I32)
        row_out = sb("row_out", P, NE, dtype=I32)
        row_in_now = sb("row_in_now", P, GROUP, dtype=I32)
        row_out_now = sb("row_out_now", P, GROUP, dtype=I32)
        passes = sb("passes", P, DEPTH, dtype=I32)
        arena = sb("arena", P, 21760)

        at = [0]

        def take(n, where=None):
            a = at[0] if where is None else where
            if where is None:
                at[0] += n
            return arena[:, a:a + n]

        xbc = take(6 * T).rearrange("p (m t) -> p m t", t=T)
        v_da = take(TT * 256).rearrange("p (t n) -> p t n", n=256)
        z = take(TT * 512).rearrange("p (t n) -> p t n", n=512)
        qk = take(4 * T).rearrange("p (m t) -> p m t", t=T)
        qm = take(4 * T).rearrange("p (h t) -> p h t", t=T)
        km = take(4 * T).rearrange("p (h t) -> p h t", t=T)
        v_ml = take(TT * 256).rearrange("p (t n) -> p t n", n=256)
        b_tok = take(TT * P).rearrange("p (t n) -> p t n", n=P)
        state = take(2 * TT * 256).rearrange("p (d t n) -> p d t n", d=2, n=256)
        tmp_at = at[0]
        ew = take(2 * 1024).rearrange("p (d h i) -> p d h i", d=2, i=P)
        xdt = take(2 * 512).rearrange("p (d n) -> p d n", d=2)
        gm = take(512).rearrange("p (d g i) -> p d g i", d=2, i=P)
        y_acc = take(512)
        y_two = take(512)
        y_skip = take(512)
        sc = take(64 * 12).rearrange("p (k n) -> p k n", n=64)
        assert at[0] <= 21760, at[0]
        probs = take(3072, tmp_at).rearrange("p (b m k) -> p b m k", b=3, m=2)
        probs_t = take(1024, tmp_at + 3072).rearrange("p (b k q) -> p b k q", b=2, q=P)
        stats = take(4 * 64, tmp_at + 4096).rearrange("p (s u m) -> p s u m", s=4, m=2)
        o_sb = take(512, tmp_at + 4352).rearrange("p (k n) -> p k n", n=256)
        o_sq = take(256, tmp_at + 4864)
        latent = take(3 * T, tmp_at).rearrange("p (m t) -> p m t", t=T)
        latent_sq = take(3 * T, tmp_at + 3 * T).rearrange("p (m t) -> p m t", t=T)
        r_lat = take(2 * T, tmp_at + 6 * T).rearrange("p (m t) -> p m t", t=T)
        rope_tmp = take(256, tmp_at + 8 * T)
        assert tmp_at + 8 * T + 256 <= 21760
        y_tok = take(TT * DM, 0).rearrange("p (t n) -> p t n", n=DM)
        y_tok2 = take(TT * DM, TT * DM).rearrange("p (t n) -> p t n", n=DM)
        moe_at = 2 * TT * DM
        x_slots = take(GATHERS * DM, 0).rearrange("p (b n) -> p b n", b=GATHERS)
        x_t = take(2 * DM, moe_at + 2 * DM).rearrange("p (b k s) -> p b k s", b=2, s=P)
        y_slots = take(2 * DM, moe_at + 4 * DM).rearrange("p (b n) -> p b n", b=2)
        onehot = take(GROUP * TT * P // 2, moe_at + 6 * DM).bitcast(BF16).rearrange("p (b s) -> p b s", s=P)
        vals_parts = take(TT * NE * PARTS * 3 // 2, moe_at + 7 * DM).bitcast(BF16).rearrange(
            "p (t e s c) -> p t e s c", e=NE, s=PARTS, c=3)
        vals_rest = take(TT * NE * 3, moe_at + 7 * DM + 512).rearrange("p (t e c) -> p t e c", e=NE, c=3)
        silu_g = take(DE, moe_at + 8 * DM)
        hid = take(DE, moe_at + 8 * DM + DE)
        hid_t = take(DE, moe_at + 9 * DM).rearrange("p (f s) -> p f s", s=P)
        counts_at = moe_at + 7 * DM + 512 + 192
        tri_bf, ones_bf = (take(P // 2, counts_at + 64 * i).bitcast(BF16) for i in range(2))
        chosen_bf = take(TT * NE // 2, counts_at + 128).bitcast(BF16).rearrange("p (t e) -> p t e", e=NE)
        u_tok = y_tok2
        vecrows = take(DEPTH * P, moe_at).rearrange("p (l n) -> p l n", l=DEPTH)
        tok = y_tok
        squares = take(KT * T, 0).rearrange("p (k t) -> p k t", t=T)
        u_rows = [nc.dram_tensor(f"u_rows{l}", (T - P * FIRST_T[l], DM), F32, kind="Internal").ap() for l in range(DEPTH)]
        y_rows = [nc.dram_tensor(f"y_rows{l}", (2 * T, DM), F32, kind="Internal").ap() for l in range(DEPTH)]

        ps = stack.enter_context(nc.psum_tensor("ps", [P, 8, 512], F32))

        chunks = []
        for g in range(3):
            chunks += [("mod", 0, g, k) for k in range(4)]
            if g == 0:
                chunks += [("in", 0, n, 0) for n in ("x", "bcv", "dtm", "qk", "z")]
        chunks += [("mod", 1, g, k) for g in range(3) for k in range(4)]
        chunks += [("out", 0, n, 0) for n in range(2)]
        moe_base = [len(chunks)]
        after = [("in", 1, n, 0) for n in ("x", "bcv", "dtm", "qk", "z")] + [("out", 1, n, 0) for n in range(2)]
        second = len(chunks) + NE * PER_EXPERT
        moe_base.append(second + len(after))
        ring_at = {k: i for i, k in enumerate(chunks)}
        ring_at.update({k: second + i for i, k in enumerate(after)})
        landed = [[S(f"ring_landed{s}", l) for s in range(RING)] for l in range(DEPTH)]

        def landed_sem(i):
            return landed[int(i >= second)][i % RING]

        pairs = [i for k, i in ring_at.items() if k[2] == "bcv"]

        def landed_count(i):
            start = second if i >= second else 0
            return 16 * sum(2 if j in pairs else 1 for j in range(start, i + 1) if j % RING == i % RING)

        IN_COLS = {"x": (COL_X, 512), "qk": (COL_QK, 512), "z": (COL_Z, 512), "dtm": (COL_DT, 432)}

        def first_column(layer, name, m):
            return P * FIRST_T[layer] if (name, m) in (("xbc", 5), ("lat", 0), ("lat", 1)) else 0

        def squares_of(name):
            return squares if name.endswith("ffn") else u

        NORMS = ["0mix", "0ffn", "1mix", "1ffn", "final"]
        eights = {n: 8 * i for i, n in enumerate(NORMS)}
        squares_base = dict(zip(NORMS, (0, 8, 16, 16 + TT - FIRST_T[0], 24 + TT - FIRST_T[0])))
        ready_base = dict(zip(NORMS, (0, 16, 32, 48, 56)))
        units0 = len(attention_units(0))

        def ut_count(layer, t, half):
            return 2 * (TT * layer + t - FIRST_T[layer]) + half

        entry = {}
        released = {}
        filled, evacuated = S("bank_filled"), S("bank_evacuated")

        vec_loads, bcast_loads = [], []
        for row, n, src in ((V_BMOD, 48, b_mod), (V_GMIX, 8, norm_mix_g), (V_GFFN, 8, norm_ffn_g),
                            (V_CONVW, 18, ssd_conv_w.rearrange("l a n -> l (a n)")), (V_CONVB, 6, ssd_conv_b),
                            (V_QG, 2, mla_q_norm_g), (V_KVG, 1, mla_kv_norm_g), (V_SSDG, 4, ssd_norm_g)):
            vec_loads.append((vecrows[row:row + n, :, :], src.rearrange("l (r p) -> r l p", p=P)))
        for a in range(2):
            vec_loads.append((vecrows[V_SUBG:V_SUBG + 1, :, 64 * a:64 * a + 64],
                              da_subln_g.rearrange("l (r p) -> r l p", r=1)))
        for row, src in ((V_FING, final_norm_g), (V_CCTX, c_ctx), (V_C, c[0])):
            vec_loads.append((vecrows[row:row + 8, 0, :], src.rearrange("(r p) -> r p", p=P)))
        for l in range(DEPTH):
            for at_b, n, src in ((B_DTB, 16, ssd_dt_bias[l].rearrange("a n -> (a n)")),
                                 (B_ALOG, 16, ssd_a_log[l].rearrange("a n -> (a n)")),
                                 (B_D, 8, ssd_d[l]), (B_LAM, 128, da_lambda[l].rearrange("a n -> (a n)")),
                                 (B_RB, 16, router_bias)):
                bcast_loads.append((bcast[:, l, at_b:at_b + n], src.partition_broadcast(P)))
        n_vec_dmas, n_bcast_dmas = len(vec_loads), len(bcast_loads) + 1

        block = stack.enter_context(nc.Block())

        def alone(engine):
            engine.sem_inc(S("carriers"), 1)

        @block.tensor
        def _(pe):
            def wait_chunk(key):
                i = ring_at[key]
                pe.wait_ge(landed_sem(i), landed_count(i))
                return ring[:, i % RING, :]

            def open_bank(name):
                i = len(entry)
                entry[name] = i
                if i >= 2:
                    pe.wait_ge(evacuated, i - 1)
                return ps[:, i % 2, :]

            def close_bank(last):
                last.then_inc(filled, 1)

            def read_back(name):
                pe.wait_ge(evacuated, entry[name] + 1)

            def tr(dst, src):
                n = src.shape[0]
                return nc.tensor.transpose(dst, src, ident[0:n, 0:n])

            def modulation(part):
                l, g, kk = part
                group = DEPTH_GROUPS * l + g
                bank = ps[:, MOD_BANK, :]
                if kk == 4:
                    pe.wait_ge(S("modrow_ready"), group + 1)
                    for s in range(4):
                        last = tr(bank[:, P * s:P * s + P], modrow[:, P * s:P * s + P])
                    last.then_inc(S("mod_turned"), 1)
                    return
                if kk == 0 and group:
                    pe.wait_ge(S("mod_placed"), group)
                w = wait_chunk(("mod", l, g, kk)).rearrange("p (k n) -> p k n", k=2)
                for k2 in range(2):
                    k = 2 * kk + k2
                    for j in range(4):
                        last = nc.tensor.matmul(bank[32 * j:32 * j + 32, :], cond[:, k, :],
                                                w[:, k2, 512 * j:512 * j + 512], start=(k == 0), stop=(k == 7),
                                                tile_position=(0, 32 * j))
                last.then_inc(S("mod_chunk_used"), 1)
                released[ring_at[("mod", l, g, kk)]] = (S("mod_chunk_used"), 4 * group + kk + 1)

            def spare(n):
                for k in range(mod_done[0], min(mod_done[0] + n, len(MOD_PARTS))):
                    modulation(MOD_PARTS[k])
                mod_done[0] += n

            mod_done = [0]

            def mean_square(name, ready, src, n, c0):
                bank = open_bank(name)
                for k in range(n):
                    pe.wait_ge(ready[0], ready[1] + k + 1)
                    last = nc.tensor.matmul(bank[:, 0:T - c0], ones_mean[:, :], src[:, k, c0:T], start=(k == 0),
                                            stop=(k == n - 1))
                close_bank(last)

            def norm_mean(name, c0):
                pe.wait_ge(S("squares_summed"), NORMS.index(name) + 1)
                bank = open_bank(f"ms{name}")
                close_bank(nc.tensor.matmul(bank[:, 0:T - c0], ones_mean[:, :], rstd[:, c0:T], start=True, stop=True))

            def feature_major(name, w, n, c0, ready=None, width=P, row=0):
                bank = open_bank(name)
                for k in range(KT):
                    if ready is not None:
                        pe.wait_ge(S("u_ready"), ready + 2 * (k + 1))
                    last = nc.tensor.matmul(bank[row:row + width, 0:T - c0], w[:, k, n:n + width], u[:, k, c0:T],
                                            start=(k == 0), stop=(k == KT - 1))
                close_bank(last)

            def token_major(name, w, n, width, tiles):
                bank = open_bank(name)
                for i, t in enumerate(tiles):
                    for k in range(KT):
                        last = nc.tensor.matmul(bank[:, i * width:(i + 1) * width], u[:, k, P * t:P * t + P],
                                                w[:, k, n:n + width], start=(k == 0), stop=(k == KT - 1))
                close_bank(last)

            def in_chunk(l, n):
                width = 432 if n == "dtm" else 512
                w = wait_chunk(("in", l, n, 0))
                return w[:, 0:KT * width].rearrange("p (k n) -> p k n", n=width)

            def free_chunk(key, name):
                released[ring_at[key]] = (filled, entry[name] + 1)

            def project(l):
                first = FIRST_T[l]
                w = in_chunk(l, "x")
                for m in range(4):
                    feature_major(f"xbc{l}{m}", w, P * m, 0, ready_base[f"{l}mix"] if m == 0 else None)
                free_chunk(("in", l, "x", 0), f"xbc{l}3")
                w = in_chunk(l, "bcv")
                for m in range(2):
                    feature_major(f"xbc{l}{4 + m}", w, P * m, first_column(l, "xbc", 4 + m))
                for i in range(2):
                    token_major(f"v{l}{i}", w, 256, 256, [2 * i, 2 * i + 1])
                free_chunk(("in", l, "bcv", 0), f"v{l}1")
                w = in_chunk(l, "dtm")
                for m in range(3):
                    feature_major(f"lat{l}{m}", w, 16 + P * m, first_column(l, "lat", m))
                bank = open_bank(f"kr{l}")
                for k in range(KT):
                    for col, row in ((0, 0), (16 + QR + KVR, NOPE)):
                        last = nc.tensor.matmul(bank[row:row + ROPE, :], w[:, k, col:col + ROPE], u[:, k, :],
                                                start=(k == 0), stop=(k == KT - 1), tile_position=(0, row))
                close_bank(last)
                free_chunk(("in", l, "dtm", 0), f"kr{l}")

            def turn_steps(l):
                read_back(f"kr{l}")
                bank = open_bank(f"dt{l}")
                for t in range(TT):
                    last = tr(bank[:, 16 * t:16 * t + 16], rstd[0:16, P * t:P * t + P])
                close_bank(last)

            def project_qk(l, m):
                feature_major(f"qk{l}{m}", in_chunk(l, "qk"), P * m, 0 if m >= 2 or l == 0 else NCTX)
                if m == 3:
                    free_chunk(("in", l, "qk", 0), f"qk{l}3")

            def project_z(l, t):
                token_major(f"z{l}{t}", in_chunk(l, "z"), 0, 512, [t])
                if t == TT - 1:
                    free_chunk(("in", l, "z", 0), f"z{l}{TT - 1}")

            def latents_mean(l):
                c0 = P * FIRST_T[l]
                mean_square(f"cqms{l}", (S("latent_sq"), 3 * l), latent_sq, 2, c0)
                mean_square(f"ckvms{l}", (S("latent_sq"), 3 * l + 2), latent_sq[:, 2:3, :], 1, 0)

            def latents_up(l):
                c0 = P * FIRST_T[l]
                pe.wait_ge(S("wu_landed"), 32 * (l + 1))
                pe.wait_ge(S("latent_normed"), 3 * l + 3)
                for hh in range(DA_H):
                    bank = open_bank(f"qm{l}{hh}")
                    for m in range(2):
                        last = nc.tensor.matmul(bank[0:HD, 0:T - c0], wuq[:, m, HD * hh:HD * hh + HD],
                                                latent[:, m, c0:T], start=(m == 0), stop=(m == 1))
                    close_bank(last)
                for hh in range(DA_H):
                    bank = open_bank(f"km{l}{hh}")
                    close_bank(nc.tensor.matmul(bank[0:NOPE, :], wukv[:, P * hh:P * hh + NOPE], latent[:, 2, :],
                                                start=True, stop=True))
                wv = wukv[:, :].rearrange("p (h n) -> p h n", n=P)[:, :, NOPE:P]
                for i in range(2):
                    bank = open_bank(f"vm{l}{i}")
                    for j in range(2):
                        t = 2 * i + j
                        last = nc.tensor.matmul(bank[:, 256 * j:256 * j + 256].rearrange("p (h n) -> p h n", h=4),
                                                latent[:, 2, P * t:P * t + P], wv,
                                                start=True, stop=True)
                    close_bank(last)

            def rotate(l):
                for m in range(4):
                    if m == 2 and l == 0:
                        project_z(l, TT - 1)
                    read_back(f"qk{l}{m}")
                    bank = open_bank(f"qkrot{l}{m}")
                    close_bank(nc.tensor.matmul(bank[:, 0:NLAT], cst[:, C_ROT:C_ROT + P], qk[:, m, NCTX:T],
                                                start=True, stop=True))
                for hh in range(DA_H):
                    read_back(f"qm{l}{hh}")
                    bank = open_bank(f"qmrot{l}{hh}")
                    close_bank(nc.tensor.matmul(bank[0:HD, 0:NLAT], cst[0:HD, C_MROT:C_MROT + HD],
                                                qm[0:HD, hh, NCTX:T], start=True, stop=True))
                    spare(1)
                read_back(f"kr{l}")
                bank = open_bank(f"krrot{l}")
                close_bank(nc.tensor.matmul(bank[NOPE:HD, 0:NLAT],
                                            cst[NOPE:HD, C_ROT + NOPE:C_ROT + HD], km[NOPE:HD, 0, NCTX:T],
                                            start=True, stop=True))
                spare(1)

            def scan_start(l):
                pe.wait_ge(S("xbc_ready"), 6 * l + 6)
                for t in range(TT):
                    bank = open_bank(f"xs{l}{t}")
                    for m in range(4):
                        last = tr(bank[:, P * m:P * m + P], xbc[:, m, P * t:P * t + P])
                    close_bank(last)
                bank = open_bank(f"btok{l}")
                for t in range(TT):
                    last = tr(bank[:, P * t:P * t + P], xbc[:, 4, P * t:P * t + P])
                close_bank(last)
                pe.wait_ge(S("da_ready"), l + 1)
                bank = open_bank(f"cum{l}")
                for d in range(2):
                    nc.tensor.matmul(bank[:, 32 * d:32 * d + 32], tri[d], sc[:, 2, 32 * d:32 * d + 32], start=True,
                                     stop=True)
                close_bank(nc.tensor.matmul(bank[:, 64:128], ones[:, :], sc[:, 2, :], start=True, stop=True))

            def scan_states(l):
                read_back(f"btok{l}")
                for n, (d, t, _) in enumerate(state_steps(l)):
                    pe.wait_ge(S("xde_ready", l), n + 1)
                    bank = open_bank(f"state{l}{n}")
                    for g in range(2):
                        last = nc.tensor.matmul(bank[64 * g:64 * g + 64, 0:256], b_tok[:, t, 64 * g:64 * g + 64],
                                                xdt[:, n % 2, 256 * g:256 * g + 256], start=True, stop=True)
                    close_bank(last)
                    if z_after(l, n) is not None:
                        project_z(l, z_after(l, n))

            def scan_tiles(l):
                first = FIRST_T[l]
                for i, t in enumerate(range(first, TT)):
                    for g in range(2):
                        bank = open_bank(f"cb{l}{t}{g}")
                        r = slice(64 * g, 64 * g + 64)
                        last = nc.tensor.matmul(bank[:, 0:P], xbc[r, 4, P * t:P * t + P],
                                                xbc[r, 5, P * t:P * t + P], start=True, stop=True)
                        close_bank(last)
                    for d in range(2):
                        n = 2 * i + d
                        pe.wait_ge(S("rows_built", l), n + 1)
                        if n >= 1:
                            pe.wait_ge(S("decay_clamped", l), n)
                        for b in range(2):
                            last = nc.tensor.matmul(ps[:, 2 + b, :], ones[:, :], 
                                                    ew[:, d, 4 * b:4 * b + 4, :].rearrange("p h i -> p (h i)"),
                                                    start=True, stop=True)
                        last.then_inc(S("rows_cast", l), 1)
                        spare(2)
                    if i == 0:
                        pe.wait_ge(S("states_done"), l + 1)
                    else:
                        pe.wait_ge(S("y_banks_read", l), i)
                    for d in range(2):
                        pe.wait_ge(S("w_ready", l), 2 * i + d + 1)
                        for hh in range(SSD_H):
                            last = nc.tensor.matmul(ps[:, 4, 64 * hh:64 * hh + 64], ew[:, d, hh, :],
                                                    xdt[:, d, 64 * hh:64 * hh + 64], start=(d == 0 and hh == 0),
                                                    stop=(d == 1 and hh == 7), skip_group_check=True)
                        for g in range(2):
                            r = slice(64 * g, 64 * g + 64)
                            last = nc.tensor.matmul(ps[:, 5 + g, 256 * d:256 * d + 256], xbc[r, 5, P * t:P * t + P],
                                                    state[r, d, t, :], start=True, stop=True)
                    last.then_inc(S("y_summed", l), 1)
                    if i > 0:
                        y_transposes(l, t - 1, i)
                    spare(1)

            def y_transposes(l, t, count):
                pe.wait_ge(S("y_normed", l), count)
                bank = open_bank(f"yT{l}{t}")
                for m in range(4):
                    last = tr(bank[:, P * m:P * m + P], y_acc[:, P * m:P * m + P])
                close_bank(last)

            def attention(l):
                units = attention_units(l)
                before, groups_before = units0 * l, units0 // DA_H * l
                pe.wait_ge(S("roped"), l + 1)
                for s in range(len(units) - DA_H + LAG_TURN + 1):
                    if s == 1:
                        pe.wait_ge(S("y_banks_read", l), TT - FIRST_T[l])
                    if s == 2:
                        y_transposes(l, TT - 1, TT - FIRST_T[l])
                    if s == 3:
                        pe.wait_ge(evacuated, len(entry))
                    if s < len(units):
                        kind, t, hh, nk = units[s]
                        if s >= 2:
                            pe.wait_ge(S("exp_done"), before + s - 1)
                        pair = 2 + 2 * (s % 2)
                        if kind == "da":
                            r0 = 64 * (hh % 2)
                            for m in range(2):
                                r = slice(r0 + 32 * m, r0 + 32 * m + 32)
                                last = nc.tensor.matmul(ps[:, pair + m, 0:nk], qk[r, hh // 2, P * t:P * t + P],
                                                        qk[r, 2 + hh // 2, 0:nk], start=True, stop=True)
                        else:
                            last = nc.tensor.matmul(ps[:, pair, 0:nk], qm[0:HD, hh, P * t:P * t + P],
                                                    km[0:HD, hh, 0:nk], start=True, stop=True)
                        last.then_inc(S("scores_done"), 1)
                    n = s - 2
                    if 0 <= n < len(units):
                        kind, t, hh, nk = units[n]
                        if kind == "da":
                            pe.wait_ge(S("mixed"), before // 2 + sum(1 for x in units[:n + 1] if x[0] == "da"))
                        else:
                            pe.wait_ge(S("exp_done"), before + n + 1)
                        if n >= 2:
                            pe.wait_ge(S("probs_t_ready"), before + n - 1)
                        for k in range(nk // P):
                            last = tr(ps[:, 6 + n % 2, P * k:P * k + P], probs[:, n % 3, 0, P * k:P * k + P])
                        last.then_inc(S("probs_turned"), 1)
                    n = s - 3
                    if 0 <= n < len(units):
                        kind, t, hh, nk = units[n]
                        g = n // DA_H
                        if hh == 0 and g >= 2:
                            pe.wait_ge(S("o_placed"), groups_before + g - 1)
                        pe.wait_ge(S("probs_t_ready"), before + n + 1)
                        v = v_da if kind == "da" else v_ml
                        for k in range(nk // P):
                            last = nc.tensor.matmul(ps[:, g % 2, 64 * hh:64 * hh + 64], probs_t[:, n % 2, k, :],
                                                    v[:, k, 64 * hh:64 * hh + 64], start=(k == 0),
                                                    stop=(k == nk // P - 1))
                        last.then_inc(S("heads_done"), 1)
                    g = head_part(s, LAG_TURN)
                    if g is not None:
                        pe.wait_ge(S("o_ready"), groups_before + g + 1)
                        for m in range(2):
                            last = tr(ps[:, g % 2, 256 + P * m:256 + P * m + P],
                                      o_sb[:, units[DA_H * g][0] == "ml", P * m:P * m + P])
                        last.then_inc(S("o_turned"), 1)

            def out_projection(l):
                c0 = P * FIRST_T[l]
                pe.wait_ge(S("o_placed"), (units0 * l + len(attention_units(l))) // DA_H)
                for n in range(2):
                    w = wait_chunk(("out", l, n, 0)).rearrange("p (k n) -> p k n", n=512)
                    for m in range(4):
                        name = f"mix{l}{4 * n + m}"
                        bank = open_bank(name)
                        for k in range(KT):
                            last = nc.tensor.matmul(bank[:, 0:T - c0], w[:, k, P * m:P * m + P], u[:, k, c0:T],
                                                    start=(k == 0), stop=(k == KT - 1))
                        close_bank(last)
                    free_chunk(("out", l, n, 0), name)

            def router(l):
                c0 = P * FIRST_T[l]
                bank = open_bank(f"logits_t{l}")
                for k in range(KT):
                    pe.wait_ge(S("u_ready"), ready_base[f"{l}ffn"] + (2 if l == 0 else 1) * (k + 1))
                    last = nc.tensor.matmul(bank[0:NE, 0:T - c0], rw[:, k, :], u[:, k, c0:T], start=(k == 0),
                                            stop=(k == KT - 1))
                close_bank(last)
                read_back(f"logits_t{l}")
                bank = open_bank(f"logits{l}")
                for t in range(FIRST_T[l], TT):
                    last = tr(bank[:, NE * t:NE * t + NE], rstd[0:NE, P * t:P * t + P])
                close_bank(last)

            def to_rows(l):
                for t in range(FIRST_T[l], TT):
                    for half in range(2):
                        n = ut_count(l, t, half)
                        if n >= 2:
                            pe.wait_ge(S("ut_taken"), n - 1)
                        for m in range(4):
                            last = tr(ps[:, 2 + half, P * m:P * m + P], u[:, 4 * half + m, P * t:P * t + P])
                        last.then_inc(S("ut_turned"), 1)

            def places(l):
                tiles = range(FIRST_T[l], TT)
                pe.wait_ge(S("chosen_ready"), 2 * l + 2)
                bank = open_bank(f"places{l}")
                chosen = chosen_bf
                for t in tiles:
                    for t2 in range(FIRST_T[l], t):
                        nc.tensor.matmul(bank[:, NE * t:NE * t + NE], ones_bf, chosen[:, t2, :],
                                         start=(t2 == FIRST_T[l]), stop=False)
                    nc.tensor.matmul(bank[:, NE * t:NE * t + NE], tri_bf, chosen[:, t, :],
                                     start=(t == FIRST_T[l]), stop=True)
                for t in tiles:
                    last = nc.tensor.matmul(bank[:, NE * TT:NE * TT + NE], ones_bf, chosen[:, t, :],
                                            start=(t == FIRST_T[l]), stop=(t == TT - 1))
                close_bank(last)

            def experts(l):
                base, tiles = moe_base[l], range(FIRST_T[l], TT)
                nt = len(tiles)
                pe.wait_ge(S("passes_ready"), l + 1)
                n_more = nc.tensor.value_load(passes[0:1, l:l + 1], min_val=0, max_val=TT - 1)
                with pe.Fori(0, n_more + 1) as p:
                    with pe.Fori(0, NE // GROUP) as q:
                        for j in range(GROUP):
                            for i, t in enumerate(tiles):
                                k = j * nt + i
                                pe.wait_ge(S("onehot_ready", l), p * (NE * nt) + q * (GROUP * nt) + (k + 1))
                                last = nc.tensor.matmul(ps[:, 4, 9 * j:9 * j + 9], onehot[:, k, :],
                                                        vals_parts[:, t, bass.ds(q * GROUP + j, 1), :, :].rearrange(
                                                            "p o s c -> p (o s c)"), start=(i == 0),
                                                        stop=(i == nt - 1))
                        last.then_inc(S("lists_summed", l), 1)
                        pe.wait_ge(S("lists_ready", l), p * (NE // GROUP) + q + 1)

                    def wait_slot(q, n, kind):
                        c = chunk_place(kind, n)
                        rounds = 16 * GROUP * PER_EXPERT // RING
                        pe.wait_ge(landed[l][(base + c) % RING], p * (rounds * NE // GROUP) + q * rounds
                                   + landed_count(base + c))
                        return ring[:, (base + c) % RING, :]

                    def turn_x(q, n, half):
                        if half == 0:
                            pe.wait_ge(S(f"gathered{n % GATHERS}", l), p * (16 * NE // GATHERS)
                                       + q * (16 * GROUP // GATHERS) + 16 * (n // GATHERS + 1))
                        else:
                            pe.wait_ge(S("x_t_ready", l), p * (2 * NE) + q * (2 * GROUP) + (2 * n + 1))
                        for m in range(4):
                            k = 4 * half + m
                            last = tr(ps[:, 4, P * m:P * m + P], x_slots[:, n % GATHERS, P * k:P * k + P])
                        last.then_inc(S("x_turned", l), 1)

                    def project_up(q, n, kind):
                        w = wait_slot(q, n, kind).rearrange("p (k n) -> p k n", n=DE)
                        if kind == 0:
                            pe.wait_ge(S("x_t_ready", l), p * (2 * NE) + q * (2 * GROUP) + (2 * n + 2))
                        for k in range(KT):
                            last = nc.tensor.matmul(ps[:, 2 * (n % 2) + kind, :], x_t[:, n % 2, k, :], w[:, k, :],
                                                    start=(k == 0), stop=(k == KT - 1))
                        last.then_inc(S("gate_done" if kind == 0 else "up_done", l), 1)

                    def project_down(q, n):
                        pe.wait_ge(S("hid_t_ready", l), p * NE + q * GROUP + (n + 1))
                        pe.wait_ge(S("y_scaled", l), p * NE + q * GROUP + (n + 1))
                        w = wait_slot(q, n, 2).rearrange("p (f n) -> p f n", n=DM)
                        for b in range(2):
                            for f in range(4):
                                last = nc.tensor.matmul(ps[:, 6 + b, :], hid_t[:, f, :],
                                                        w[:, f, 512 * b:512 * b + 512], start=(f == 0), stop=(f == 3))
                        last.then_inc(S("down_done", l), 1)

                    def turn_hidden(q, n):
                        pe.wait_ge(S("hid_ready", l), p * NE + q * GROUP + (n + 1))
                        for f in range(4):
                            last = tr(ps[:, 5, P * f:P * f + P], hid[:, P * f:P * f + P])
                        last.then_inc(S("hid_turned", l), 1)

                    def step(q, n):
                        project_up(q, n + 1, 0)
                        if n + 2 < NE:
                            turn_x(q, n + 2, 0)
                        project_up(q, n + 1, 1)
                        if n + 2 < NE:
                            turn_x(q, n + 2, 1)
                        project_down(q, n)
                        turn_hidden(q, n + 1)

                    turn_x(0, 0, 0)
                    turn_x(0, 0, 1)
                    project_up(0, 0, 0)
                    turn_x(0, 1, 0)
                    project_up(0, 0, 1)
                    turn_x(0, 1, 1)
                    turn_hidden(0, 0)
                    with pe.Fori(0, STEPS) as q:
                        for n in range(GROUP):
                            step(q, n)
                    for n in range(STEPS * GROUP, NE - 1):
                        step(0, n)
                    project_down(0, NE - 1)

            def add_experts(l):
                for i, t in enumerate(range(FIRST_T[l], TT)):
                    pe.wait_ge(S("y_combined", l), i + 1)
                    for half in range(2):
                        bank = open_bank(f"y{l}{t}{half}")
                        for m in range(4):
                            k = 4 * half + m
                            last = tr(bank[:, P * m:P * m + P], y_tok[:, t, P * k:P * k + P])
                        close_bank(last)

            pe.wait_ge(S("const_landed"), 16 * (1 + n_vec_dmas))
            pe.wait_ge(S("ones_ready"), 2)
            bank = open_bank("vecs")
            for l in range(DEPTH):
                last = tr(bank[:, P * l:P * l + NVECS[l]], vecrows[0:NVECS[l], l, :])
            close_bank(last)
            for t in range(TT):
                pe.wait_ge(S("tokens_landed", t), 16)
                for half in range(2):
                    bank = open_bank(f"h{t}{half}")
                    for m in range(4):
                        last = tr(bank[:, P * m:P * m + P], tok[:, t, 512 * half + P * m:512 * half + P * m + P])
                    close_bank(last)
            for l in range(DEPTH):
                if l == 0:
                    pe.wait_ge(S("cond_ready"), 1)
                    spare(2)
                norm_mean(f"{l}mix", 0)
                if l == 0:
                    spare(3)
                project(l)
                project_qk(l, 0)
                turn_steps(l)
                project_qk(l, 1)
                latents_mean(l)
                project_qk(l, 2)
                project_qk(l, 3)
                scan_start(l)
                latents_up(l)
                scan_states(l)
                rotate(l)
                scan_tiles(l)
                attention(l)
                out_projection(l)
                c0 = P * FIRST_T[l]
                norm_mean(f"{l}ffn", c0)
                router(l)
                to_rows(l)
                places(l)
                experts(l)
                add_experts(l)
            norm_mean("final", NCTX)
            for t in (2, 3):
                for half in range(2):
                    bank = open_bank(f"out{t}{half}")
                    for m in range(4):
                        k = 4 * half + m
                        pe.wait_ge(S("u_ready"), ready_base["final"] + k + 1)
                        last = tr(bank[:, P * m:P * m + P], u[:, k, P * t:P * t + P])
                    close_bank(last)

        @block.vector
        def _(dve):
            step = Tally(S("vector_step"))
            read = Tally(evacuated)

            def link(ins):
                dve.wait_ge(step.sem, step.by(ins))

            def claim(name):
                assert read.n == entry[name], (name, read.n, entry[name])
                dve.wait_ge(filled, read.n + 1)
                return ps[:, read.n % 2, :]

            def emptied(ins):
                read.by(ins)

            def own_read():
                dve.wait_ge(read.sem, read.n)

            v = nc.vector
            tt, ts, stt = v.tensor_tensor, v.tensor_scalar, v.scalar_tensor_tensor

            def modulation(part):
                l, g, kk = part
                group = DEPTH_GROUPS * l + g
                if kk == 3:
                    dve.wait_ge(S("mod_chunk_used"), 4 * group + 4)
                    v.tensor_copy(modrow[:, :], ps[:, MOD_BANK, :]).then_inc(S("modrow_ready"), 1)
                if kk < 4:
                    return
                dve.wait_ge(S("mod_turned"), group + 1)
                tt(mod[:, l, 16 * g:16 * g + 16, :].rearrange("p (j s) c -> p j s c", s=4),
                   ps[:, MOD_BANK, :].rearrange("p (s j r) -> p j s r", s=4, j=4)[:, :, :, 0:2],
                   vec[:, l, 16 * g:16 * g + 16].rearrange("p (j s) -> p j s", s=4).unsqueeze(3)
                   .to_broadcast([P, 4, 4, 2]), ALU.add).then_inc(S("mod_placed"), 1)
                dve.wait_ge(S("mod_placed"), group + 1)
                if g != 1:
                    n, at_v = (0, V_GMIX) if g == 0 else (1, V_GFFN)
                    scale = mod[:, l, 8:16, :] if g == 0 else mod[:, l, 32:40, :]
                    stt(gain[:, l, n, :, :], scale, 1.0,
                        vec[:, l, at_v:at_v + KT].unsqueeze(2).to_broadcast([P, KT, 2]), ALU.add,
                        ALU.mult).then_inc(S("gain_ready"), 1)

            def spare(n):
                for k in range(mod_done[0], min(mod_done[0] + n, len(MOD_PARTS))):
                    modulation(MOD_PARTS[k])
                mod_done[0] += n

            mod_done = [0]

            def add_square(name, c0, k):
                if k == 0:
                    return
                sq = squares_of(name)
                dve.wait_ge(S("squares"), squares_base[name] + k + 1)
                ins = tt(rstd[:, c0:T], sq[:, 0, c0:T] if k == 1 else rstd[:, c0:T], sq[:, k, c0:T], ALU.add)
                if k < KT - 1:
                    link(ins)
                else:
                    ins.then_inc(S("squares_summed"), 1)

            def norm(name, c0):
                bank = claim(f"ms{name}")
                emptied(ts(rstd[:, c0:T], bank[:, 0:T - c0], EPS, None, ALU.add))
                if name == "0mix":
                    spare(5)
                dve.wait_ge(S("rstd_ready"), NORMS.index(name) + 1)
                for k in range(KT):
                    tt(u[:, k, c0:T], h[:, k, c0:T], rstd[:, c0:T], ALU.mult).then_inc(S("u_scaled"), 1)

            def project(l):
                first = FIRST_T[l]
                for m in range(6):
                    c0 = first_column(l, "xbc", m)
                    bank = claim(f"xbc{l}{m}")[:, 0:T - c0].rearrange("p (s t) -> p s t", t=NCTX)
                    acc = xbc[:, m, c0:T].rearrange("p (s t) -> p s t", t=NCTX)
                    w = vec[:, l, V_CONVW + m:V_CONVW + 18:6]
                    dve.wait_ge(S("conv_mid"), 6 * l + m + 1)
                    link(stt(acc[:, :, 1:256], bank[:, :, 0:255], w[:, 0:1], acc[:, :, 1:256], ALU.mult, ALU.add))
                    emptied(stt(acc[:, :, 0:255], bank[:, :, 1:256], w[:, 2:3], acc[:, :, 0:255], ALU.mult, ALU.add))
                for i in range(2):
                    emptied(v.tensor_copy(v_da[:, 2 * i:2 * i + 2, :],
                                          claim(f"v{l}{i}").rearrange("p (t n) -> p t n", n=256)))
                for m in range(3):
                    c0 = first_column(l, "lat", m)
                    emptied(v.tensor_copy(latent[:, m, c0:T], claim(f"lat{l}{m}")[:, 0:T - c0]))
                bank = claim(f"kr{l}")
                v.tensor_copy(rstd[0:16, :], bank[0:16, :])
                emptied(v.tensor_copy(km[NOPE:HD, 0, :], bank[NOPE:HD, :]))

            def take_steps(l):
                bank = claim(f"dt{l}")[:, 0:64].rearrange("p (t d h) -> p d t h", t=TT, d=2)
                emptied(tt(sc[:, 0, :].rearrange("p (d t h) -> p d t h", d=2, t=TT), bank,
                           bcast[:, l, B_DTB:B_DTB + 16].rearrange("p (d h) -> p d h", d=2).unsqueeze(2)
                           .to_broadcast([P, 2, TT, SSD_H]), ALU.add))

            def take_qk(l, m):
                c0 = 0 if m >= 2 or l == 0 else NCTX
                emptied(v.tensor_copy(qk[:, m, c0:T], claim(f"qk{l}{m}")[:, 0:T - c0]))

            def take_z(l, t):
                emptied(v.tensor_copy(z[:, t, :], claim(f"z{l}{t}")))

            def latents_mean(l):
                c0 = P * FIRST_T[l]
                bank = claim(f"cqms{l}")
                emptied(ts(r_lat[:, 0, c0:T], bank[:, 0:T - c0], DM / QR, EPS, ALU.mult, ALU.add))
                bank = claim(f"ckvms{l}")
                emptied(ts(r_lat[:, 1, :], bank, DM / KVR, EPS, ALU.mult, ALU.add))

            def latents_norm(l):
                c0 = P * FIRST_T[l]
                dve.wait_ge(S("r_lat_ready"), 2 * l + 2)
                for m in range(3):
                    g = vec[:, l, V_QG + m:V_QG + m + 1]
                    cc = c0 if m < 2 else 0
                    stt(latent[:, m, cc:T], latent[:, m, cc:T], g, r_lat[:, m // 2, cc:T], ALU.mult,
                        ALU.mult).then_inc(S("latent_normed"), 1)

            def latents_up(l):
                c0 = P * FIRST_T[l]
                for hh in range(DA_H):
                    emptied(v.tensor_copy(qm[0:HD, hh, c0:T], claim(f"qm{l}{hh}")[0:HD, 0:T - c0]))
                for hh in range(DA_H):
                    emptied(v.tensor_copy(km[0:NOPE, hh, :], claim(f"km{l}{hh}")[0:NOPE, :]))
                for i in range(2):
                    emptied(v.tensor_copy(v_ml[:, 2 * i:2 * i + 2, :],
                                          claim(f"vm{l}{i}").rearrange("p (t n) -> p t n", n=256)))

            def rope(dst, bank, cos, sin, r):
                emptied(tt(rope_tmp[r, :], bank[r, 0:NLAT], sin[r, :], ALU.mult))
                link(tt(dst, dst, cos[r, :], ALU.mult))
                own_read()
                link(tt(dst, dst, rope_tmp[r, :], ALU.add))

            def rotate(l):
                cos, sin = cst[:, C_COS:C_COS + NLAT], cst[:, C_SIN:C_SIN + NLAT]
                for m in range(4):
                    if m == 2 and l == 0:
                        take_z(l, TT - 1)
                    rope(qk[:, m, NCTX:T], claim(f"qkrot{l}{m}"), cos, sin, slice(0, P))
                for hh in range(DA_H):
                    rope(qm[0:HD, hh, NCTX:T], claim(f"qmrot{l}{hh}"), cst[:, C_MCOS:C_MCOS + NLAT],
                         cst[:, C_MSIN:C_MSIN + NLAT], slice(0, HD))
                    spare(1)
                rope(km[NOPE:HD, 0, NCTX:T], claim(f"krrot{l}"), cos, sin, slice(NOPE, HD))
                spare(1)
                v.tensor_copy(km[NOPE:HD, 1:4, :], km[NOPE:HD, 0:1, :].to_broadcast([ROPE, 3, T])).then_inc(
                    S("roped"), 1)

            def steps_start(l):
                stt(sc[:, 1, :], sc[:, 0, :], -1.0, sc[:, 0, :], ALU.mult, ALU.max).then_inc(S("dt_abs"), 1)

            def steps_one(l):
                dve.wait_ge(S("dt_exp"), 2 * l + 1)
                ts(sc[:, 3, :], sc[:, 2, :], 1.0, None, ALU.add).then_inc(S("dt_u"), 1)

            def steps_end(l):
                dve.wait_ge(S("dt_u"), l + 1)
                link(ts(sc[:, 4, :], sc[:, 3, :], 1.0, None, ALU.is_equal))
                link(stt(sc[:, 5, :], sc[:, 3, :], -1.0, sc[:, 4, :], ALU.add, ALU.add))
                link(v.reciprocal(sc[:, 5, :], sc[:, 5, :]))
                dve.wait_ge(S("dt_exp"), 2 * l + 2)
                link(tt(sc[:, 5, :], sc[:, 5, :], sc[:, 6, :], ALU.mult))
                link(tt(sc[:, 5, :], sc[:, 5, :], sc[:, 4, :], ALU.add))
                link(tt(sc[:, 5, :], sc[:, 5, :], sc[:, 2, :], ALU.mult))
                link(stt(sc[:, 1, :], sc[:, 0, :], 0.0, sc[:, 5, :], ALU.max, ALU.add))
                link(stt(sc[:, 2, 0:32].rearrange("p (t h) -> p t h", t=TT),
                         sc[:, 1, 0:32].rearrange("p (t h) -> p t h", t=TT), -1.0,
                         sc[:, 7, 0:8].unsqueeze(1).to_broadcast([P, TT, SSD_H]), ALU.mult, ALU.mult))
                stt(sc[:, 2, 32:64].rearrange("p (t h) -> p t h", t=TT),
                    sc[:, 1, 32:64].rearrange("p (t h) -> p t h", t=TT), -1.0,
                    sc[:, 7, 8:16].unsqueeze(1).to_broadcast([P, TT, SSD_H]), ALU.mult,
                    ALU.mult).then_inc(S("da_ready"), 1)

            def scan_start(l):
                for t in range(TT):
                    emptied(v.tensor_copy(xbc[:, 0:4, P * t:P * t + P],
                                          claim(f"xs{l}{t}").rearrange("p (m n) -> p m n", n=P)))
                emptied(v.tensor_copy(b_tok, claim(f"btok{l}").rearrange("p (t n) -> p t n", n=P)))
                bank = claim(f"cum{l}")
                emptied(v.tensor_copy(sc[:, 8:10, :], bank[:, 0:128].rearrange("p (a n) -> p a n", n=64)))
                own_read()
                tt(sc[:, 10, :], sc[:, 9, :], sc[:, 8, :], ALU.subtract).then_inc(S("cum_ready"), 1)

            def scan_states(l):
                dve.wait_ge(S("decays_ready"), l + 1)
                tt(sc[:, 5, :], sc[:, 5, :], sc[:, 1, :], ALU.mult).then_inc(S("to_end_ready"), 1)
                first_of = {0: 0, 1: 1}
                for d in range(2):
                    v.memset(state[:, d, first_of[d], :], 0.0).then_inc(S("state_zeroed", l), 1)
                dve.wait_ge(S("state_zeroed", l), 2)
                for n, (d, t, nxt) in enumerate(state_steps(l)):
                    bank = claim(f"state{l}{n}")
                    for g in range(2):
                        r = slice(64 * g, 64 * g + 64)
                        dec = sc[r, 4, 32 * d + 8 * t + 4 * g:32 * d + 8 * t + 4 * g + 4]
                        last = tt(state[r, d, nxt, :].rearrange("p (h n) -> p h n", n=64),
                                  state[r, d, t, :].rearrange("p (h n) -> p h n", n=64),
                                  dec.unsqueeze(2).to_broadcast([64, 4, 64]), ALU.mult)
                    link(last)
                    emptied(tt(state[:, d, nxt, :], state[:, d, nxt, :], bank[:, 0:256], ALU.add))
                    own_read()
                    if z_after(l, n) is not None:
                        take_z(l, z_after(l, n))
                dve.sem_inc(S("states_done"), 1)

            def scan_tiles(l):
                first = FIRST_T[l]
                for i, t in enumerate(range(first, TT)):
                    if i:
                        dve.wait_ge(S("w_ready", l), 2 * i)
                    for g in range(2):
                        bank = claim(f"cb{l}{t}{g}")
                        for d in range(2):
                            last = tt(gm[:, d, g, :], bank[:, 0:P], tri[d], ALU.mult)
                        emptied(last)
                    for d in range(2):
                        n = 2 * i + d
                        dve.wait_ge(S("rows_cast", l), n + 1)
                        for hh in range(SSD_H):
                            last = ts(ew[:, d, hh, :], ps[:, 2 + hh // 4, P * (hh % 4):P * (hh % 4) + P],
                                      sc[:, 8, 32 * d + 8 * t + hh:32 * d + 8 * t + hh + 1], 0.0, ALU.subtract,
                                      ALU.min)
                        last.then_inc(S("decay_clamped", l), 1)
                        if i and d == 0:
                            y_norm(l, t - 1)
                        spare(2)
                    if i:
                        y_turned(l, t - 1)
                    spare(1)
                    dve.wait_ge(S("y_summed", l), i + 1)
                    for d, dst in ((1, y_two), (0, y_acc)):
                        last = tt(dst.rearrange("p (g h n) -> p g h n", g=2, h=4),
                                  ps[:, 5:7, 256 * d:256 * d + 256].rearrange("p g (h n) -> p g h n", h=4),
                                  sc[:, 3, 32 * d + 8 * t:32 * d + 8 * t + 8].rearrange("p (g h) -> p g h", g=2)
                                  .unsqueeze(3).to_broadcast([P, 2, 4, SSD_P]), ALU.mult)
                    link(last)
                    link(tt(y_acc, y_acc, y_two, ALU.add))
                    tt(y_acc, y_acc, ps[:, 4, :], ALU.add).then_inc(S("y_banks_read", l), 1)
                    dve.wait_ge(S("y_banks_read", l), i + 1)
                    dve.wait_ge(S("skip_ready", l), i + 1)
                    link(tt(y_acc, y_acc, y_skip, ALU.add))
                    dve.wait_ge(S("z_ready"), l + 1)
                    tt(y_acc, y_acc, z[:, t, :], ALU.mult).then_inc(S("y_gated", l), 1)
                y_norm(l, TT - 1)

            def y_norm(l, t):
                i = t - FIRST_T[l]
                dve.wait_ge(S("y_gated", l), i + 1)
                dve.wait_ge(S("y_squared", l), i + 1)
                ts(y_acc, y_acc, small[:, 0:1], None, ALU.mult).then_inc(S("y_normed", l), 1)

            def y_turned(l, t):
                bank = claim(f"yT{l}{t}")
                for m in range(4):
                    last = ts(u[:, 2 + m, P * t:P * t + P], bank[:, P * m:P * m + P],
                              vec[:, l, V_SSDG + m:V_SSDG + m + 1], None, ALU.mult)
                emptied(last)

            def lam(l):
                lv = bcast[:, l, B_LAM:B_LAM + 128].rearrange("p (a b n) -> p a b n", a=2, b=2)
                link(tt(o_sq[:, 0:64].rearrange("p (a n) -> p a n", a=2), lv[:, :, 0, :], lv[:, :, 1, :], ALU.mult))
                v.tensor_reduce(small[:, 4:6], o_sq[:, 0:64].rearrange("p (a n) -> p a n", a=2), AX.X,
                                ALU.add).then_inc(S("lam_sums"), 1)
                dve.wait_ge(S("lam_exp"), l + 1)
                link(tt(small[:, 8:9], small[:, 7:8], small[:, 6:7], ALU.subtract))
                link(ts(small[:, 8:9], small[:, 8:9], lam_init(l), None, ALU.subtract))

            def attention(l):
                units = attention_units(l)
                mx, nb, rs, rr = (stats[:, s] for s in range(4))
                lam(l)
                for s in range(len(units) - DA_H + LAG_PLACE + 1):
                    if s == 2:
                        y_turned(l, TT - 1)
                    if s < len(units):
                        kind, t, hh, nk = units[s]
                        nm = 2 if kind == "da" else 1
                        pair = 2 + 2 * (s % 2)
                        dve.wait_ge(S("scores_done"), units0 * l + s + 1)
                        link(v.tensor_reduce(mx[:, s, 0:nm], ps[:, pair:pair + nm, 0:nk], AX.X, ALU.max))
                        ts(nb[:, s, 0:nm], mx[:, s, 0:nm], -(DA_SCALE if kind == "da" else MLA_SCALE), None,
                           ALU.mult).then_inc(S("max_ready"), 1)
                    n = s - 1
                    if 0 <= n < len(units):
                        kind, t, hh, nk = units[n]
                        dve.wait_ge(S("exp_done"), units0 * l + n + 1)
                        if kind == "da":
                            link(v.reciprocal(rr[:, n, :], rs[:, n, :]))
                            link(tt(rr[:, n, 1:2], rr[:, n, 1:2], small[:, 8:9], ALU.mult))
                            link(ts(probs[:, n % 3, 1, 0:nk], probs[:, n % 3, 1, 0:nk], rr[:, n, 1:2], None, ALU.mult))
                            stt(probs[:, n % 3, 0, 0:nk], probs[:, n % 3, 0, 0:nk], rr[:, n, 0:1],
                                probs[:, n % 3, 1, 0:nk], ALU.mult, ALU.add).then_inc(S("mixed"), 1)
                        else:
                            link(v.reciprocal(rr[:, n, 0:1], rs[:, n, 0:1]))
                    for lag, part in ((LAG_OUT, take_out), (LAG_NORM, norm_out), (LAG_PLACE, place_out)):
                        g = head_part(s, lag)
                        if g is not None and DA_H * g < len(units):
                            part(l, g)

            def take_out(l, g):
                kind = attention_units(l)[DA_H * g][0]
                dve.wait_ge(S("heads_done"), units0 * l + DA_H * (g + 1))
                bank = ps[:, g % 2, 0:256].rearrange("p (h n) -> p h n", n=DA_V)
                ob = o_sb[:, int(kind == "ml"), :].rearrange("p (h n) -> p h n", n=DA_V)
                if kind == "ml":
                    tt(ob, bank, stats[:, 3, DA_H * g:DA_H * g + 4, 0:1].to_broadcast([P, DA_H, DA_V]),
                       ALU.mult).then_inc(S("o_ready"), 1)
                else:
                    link(v.tensor_copy(ob, bank))
                    sq = o_sq.rearrange("p (h n) -> p h n", n=DA_V)
                    link(tt(sq, ob, ob, ALU.mult))
                    v.tensor_reduce(small[:, 12:16], sq, AX.X, ALU.add).then_inc(S("o_squared"), 1)

            def norm_out(l, g):
                kind, t, _, _ = attention_units(l)[DA_H * g]
                if kind == "da":
                    ob = o_sb[:, 0, :].rearrange("p (h n) -> p h n", n=DA_V)
                    dve.wait_ge(S("o_rstd"), units0 // 8 * l + t - FIRST_T[l] + 1)
                    tt(ob, ob, small[:, 12:16].unsqueeze(2).to_broadcast([P, DA_H, DA_V]),
                       ALU.mult).then_inc(S("o_ready"), 1)

            def place_out(l, g):
                kind, t, _, _ = attention_units(l)[DA_H * g]
                dve.wait_ge(S("o_turned"), units0 // DA_H * l + g + 1)
                bank = ps[:, g % 2, 256:512].rearrange("p (m n) -> p m n", n=P)
                if kind == "da":
                    ts(u[:, 0:2, P * t:P * t + P], bank, vec[:, l, V_SUBG:V_SUBG + 1], 1.0 - lam_init(l), ALU.mult,
                       ALU.mult).then_inc(S("o_placed"), 1)
                else:
                    v.tensor_copy(u[:, 6:8, P * t:P * t + P], bank).then_inc(S("o_placed"), 1)

            def add_mixed(l):
                c0 = P * FIRST_T[l]
                for m in range(KT):
                    bank = claim(f"mix{l}{m}")
                    for s in range(c0 // NCTX, 2):
                        a = NCTX * s
                        last = stt(h[:, m, a:a + NCTX], bank[:, a - c0:a - c0 + NCTX],
                                   mod[:, l, V_GATE_MIX + m, s:s + 1], h[:, m, a:a + NCTX], ALU.mult, ALU.add)
                    emptied(last)
                    if m:
                        add_square(f"{l}ffn", c0, m - 1)
                add_square(f"{l}ffn", c0, KT - 1)

            def add_experts(l, norm_name):
                tiles = range(FIRST_T[l], TT)

                def add_squares(i):
                    dve.wait_ge(S("squares"), squares_base[norm_name] + i + 1)
                    cols = slice(P * tiles[i], P * tiles[i] + P)
                    ins = v.tensor_reduce(rstd[:, cols], u[:, :, cols].rearrange("p k t -> p t k"), AX.X, ALU.add)
                    if i == len(tiles) - 1:
                        ins.then_inc(S("squares_summed"), 1)

                for i, t in enumerate(tiles):
                    for half in range(2):
                        bank = claim(f"y{l}{t}{half}")
                        for m in range(4):
                            k = 4 * half + m
                            last = stt(h[:, k, P * t:P * t + P], bank[:, P * m:P * m + P],
                                       mod[:, l, V_GATE_FFN + k, t // 2:t // 2 + 1], h[:, k, P * t:P * t + P],
                                       ALU.mult, ALU.add)
                        emptied(last)
                    if i:
                        add_squares(i - 1)
                add_squares(len(tiles) - 1)

            def router(l):
                f = FIRST_T[l]
                lg, aff, sel, pair, w1, w2, w3, oh1, oh2, sm, key, msk = (rt[:, s, f:TT, :] for s in range(12))
                n = TT - f

                def g4(ap):
                    return ap.rearrange("p t (g e) -> p t g e", g=NG)

                v.tensor_copy(tri_bf, tri[0])
                v.tensor_copy(ones_bf, ones[:, :])
                emptied(v.tensor_copy(rstd[0:NE, P * f:T], claim(f"logits_t{l}")[0:NE, 0:T - P * f]))
                bank = claim(f"logits{l}")[:, 0:TT * NE].rearrange("p (t e) -> p t e", e=NE)[:, f:TT, :]
                emptied(v.tensor_copy(lg, bank))
                dve.wait_ge(S("logits_exp"), l + 1)
                link(ts(aff, aff, 1.0, None, ALU.add))
                link(v.reciprocal(aff, aff))
                link(tt(sel, aff, bcast[:, l, B_RB:B_RB + NE].unsqueeze(1).to_broadcast([P, n, NE]), ALU.add))
                s4 = g4(sel)
                pr = pair.rearrange("p t (g e) -> p t g e", g=NG)
                pr2 = w1.rearrange("p t (g e) -> p t g e", g=NG)
                for t in range(n):
                    tt(pr[:, t, :, 0:3], s4[:, t, :, 0:3], s4[:, t, :, 1:4], ALU.add)
                    tt(pr2[:, t, :, 0:2], s4[:, t, :, 0:2], s4[:, t, :, 2:4], ALU.add)
                    link(tt(pr[:, t, :, 3:4], s4[:, t, :, 0:1], s4[:, t, :, 3:4], ALU.add))
                    link(tt(pr[:, t, :, 0:2], pr[:, t, :, 0:2], pr2[:, t, :, 0:2], ALU.max))
                gs = w2[:, :, 0:4]
                gb = w2[:, :, 4:5]
                gk = w2[:, :, 8:12]
                link(v.tensor_reduce(gs, pr, AX.X, ALU.max))
                link(v.tensor_reduce(gb, gs, AX.X, ALU.max))
                link(tt(gk, gs, gb.to_broadcast([P, n, 4]), ALU.is_equal))
                link(tt(gk, gk, cst[:, C_PG:C_PG + NG].unsqueeze(1).to_broadcast([P, n, 4]), ALU.mult))
                link(v.tensor_reduce(gb, gk, AX.X, ALU.max))
                link(tt(gk, gk, gb.to_broadcast([P, n, 4]), ALU.is_equal))
                for t in range(n):
                    last = v.tensor_copy(g4(msk)[:, t], gk[:, t, :].unsqueeze(2).to_broadcast([P, NG, 4]))
                link(last)
                link(tt(sm, sel, msk, ALU.mult))
                link(ts(msk, msk, -1.0, 1e30, ALU.add, ALU.mult))
                link(tt(sm, sm, msk, ALU.add))
                for oh in (oh1, oh2):
                    link(v.tensor_reduce(w3[:, :, 0:1], sm, AX.X, ALU.max))
                    link(tt(key, sm, w3[:, :, 0:1].to_broadcast([P, n, NE]), ALU.is_equal))
                    link(tt(key, key, cst[:, C_PE:C_PE + NE].unsqueeze(1).to_broadcast([P, n, NE]), ALU.mult))
                    link(v.tensor_reduce(w3[:, :, 0:1], key, AX.X, ALU.max))
                    link(tt(oh, key, w3[:, :, 0:1].to_broadcast([P, n, NE]), ALU.is_equal))
                    if oh is oh1:
                        link(stt(sm, oh, -2e30, sm, ALU.mult, ALU.add))
                tt(chosen_bf[:, f:TT, :], oh1, oh2, ALU.add).then_inc(S("chosen_ready"), 1)
                tt(msk, oh1, oh2, ALU.add).then_inc(S("chosen_ready"), 1)
                dve.wait_ge(S("chosen_ready"), 2 * l + 2)
                link(tt(oh1, msk, aff, ALU.mult))
                link(v.tensor_reduce(w3[:, :, 0:1], oh1, AX.X, ALU.add))
                link(v.reciprocal(w3[:, :, 0:1], w3[:, :, 0:1]))
                tok_id = cst[:, C_TOK + f:C_TOK + TT].unsqueeze(2).to_broadcast([P, n, NE])
                vl = vals[:, f:TT, :, :]
                tt(vl[:, :, :, 2], oh1, w3[:, :, 0:1].to_broadcast([P, n, NE]), ALU.mult)
                ts(vl[:, :, :, 0], tok_id, -float(NOWHERE + P * f), None, ALU.add)
                link(ts(key, oh2, float(T), -float(NOWHERE), ALU.mult, ALU.add))
                link(tt(vl[:, :, :, 1], key, tok_id, ALU.add))
                vp, rest = vals_parts[:, f:TT], vals_rest[:, f:TT]
                link(v.tensor_copy(vp[:, :, :, 0, :], vl))
                link(tt(rest, vl, vp[:, :, :, 0, :], ALU.subtract))
                link(v.tensor_copy(vp[:, :, :, 1, :], rest))
                link(tt(vp[:, :, :, 2, :], rest, vp[:, :, :, 1, :], ALU.subtract))
                bank = claim(f"places{l}")
                ps_pl = bank[:, 0:TT * NE].rearrange("p (t e) -> p t e", e=NE)[:, f:TT, :]
                link(tt(pos[:, f:TT, :], ps_pl, msk, ALU.mult))
                emptied(v.tensor_reduce(small[:, 24:25], bank[:, NE * TT:NE * TT + NE], AX.X, ALU.max))
                link(ts(pos[:, f:TT, :], pos[:, f:TT, :], -1.0, None, ALU.add))
                own_read()
                link(ts(small[:, 25:26], small[:, 24:25], float(P), None, ALU.is_gt))
                for k in range(2, n):
                    link(stt(small[:, 25:26], small[:, 24:25], float(k * P), small[:, 25:26], ALU.is_gt, ALU.add))
                v.tensor_copy(passes[:, l:l + 1], small[:, 25:26]).then_inc(S("passes_ready"), 1)

            def experts(l):
                tiles = range(FIRST_T[l], TT)
                nt = len(tiles)
                iota = cst[:, C_IOTA:C_IOTA + P]
                dve.wait_ge(S("passes_ready"), l + 1)
                dve.sem_inc(S("y_scaled", l), 1)
                n_more = v.value_load(passes[0:1, l:l + 1], min_val=0, max_val=TT - 1)
                with dve.Fori(0, n_more + 1) as p:
                    dve.wait_ge(S("scatters_ended", l), p * (NE + 1) + 1)
                    alone(dve)
                    with dve.Fori(0, NE // GROUP) as q:
                        for j in range(GROUP):
                            for i, t in enumerate(tiles):
                                ts(onehot[:, j * nt + i, :], iota, pos[:, t, bass.ds(q * GROUP + j, 1)], None,
                                   ALU.is_equal).then_inc(S("onehot_ready", l), 1)
                        dve.wait_ge(S("lists_summed", l), p * (NE // GROUP) + q + 1)
                        sums = small[:, 48:48 + 3 * GROUP].rearrange("p (j c) -> p j c", c=3)
                        v.tensor_reduce(sums, ps[:, 4, 0:3 * PARTS * GROUP].rearrange(
                            "p (j s c) -> p j c s", s=PARTS, c=3), AX.X, ALU.add).then_inc(S("parts_summed", l), 1)
                        dve.wait_ge(S("parts_summed", l), p * (NE // GROUP) + q + 1)
                        here = bass.ds(q * GROUP, GROUP)
                        ts(row_in[:, here], sums[:, :, 0], float(NOWHERE), None, ALU.add)
                        ts(row_out[:, here], sums[:, :, 1], float(NOWHERE), None, ALU.add)
                        v.tensor_copy(gate_list[:, here], sums[:, :, 2]).then_inc(S("lists_ready", l), 1)
                    ts(pos[:, FIRST_T[l]:TT, :], pos[:, FIRST_T[l]:TT, :], -float(P), None,
                       ALU.add).then_inc(S("pos_moved", l), 1)
                    dve.wait_ge(S("pos_moved", l), p + 1)

                    def hidden(q, n):
                        dve.wait_ge(S("silu_done", l), p * NE + q * GROUP + (n + 1))
                        dve.wait_ge(S("up_done", l), p * NE + q * GROUP + (n + 1))
                        tt(hid, silu_g, ps[:, 2 * (n % 2) + 1, :], ALU.mult).then_inc(S("hid_ready", l), 1)

                    def scale(q, n):
                        dve.wait_ge(S("down_done", l), p * NE + q * GROUP + (n + 1))
                        dve.wait_ge(S("scatters_ended", l), p * (NE + 1) + q * GROUP + (n + 1))
                        ts(y_slots[:, n % 2, :].rearrange("p (b n) -> p b n", b=2), ps[:, 6:8, :],
                           gate_list[:, bass.ds(q * GROUP + n, 1)], None, ALU.mult).then_inc(S("y_scaled", l), 1)

                    hidden(0, 0)
                    with dve.Fori(0, STEPS) as q:
                        for n in range(GROUP):
                            hidden(q, n + 1)
                            scale(q, n)
                    for n in range(STEPS * GROUP, NE - 1):
                        hidden(0, n + 1)
                        scale(0, n)
                    scale(0, NE - 1)

            v.memset(ones[:, :], 1.0).then_inc(S("ones_ready"), 1)
            v.memset(ones_mean[:, :], 1.0 / DM).then_inc(S("ones_ready"), 1)
            v.memset(small[:, 20:21], EPS)
            link(v.memset(cond[:, :, :], 0.0))
            bank = claim("vecs")
            for l in range(DEPTH):
                last = v.tensor_copy(vec[:, l, 0:NVECS[l]], bank[:, P * l:P * l + NVECS[l]])
            emptied(last)
            own_read()
            dve.wait_ge(S("cond_exp"), 1)
            link(ts(small[:, 32:48], small[:, 32:48], 1.0, None, ALU.add))
            link(v.reciprocal(small[:, 32:48], small[:, 32:48]))
            tt(cond[:, :, 0:2].rearrange("p k c -> p c k"), vec[:, 0, V_CCTX:V_CCTX + 16].rearrange(
                "p (c k) -> p c k", c=2), small[:, 32:48].rearrange("p (c k) -> p c k", c=2),
               ALU.mult).then_inc(S("cond_ready"), 1)
            for t in range(TT):
                for half in range(2):
                    emptied(v.tensor_copy(h[:, 4 * half:4 * half + 4, P * t:P * t + P],
                                          claim(f"h{t}{half}").rearrange("p (m n) -> p m n", n=P)))
            for k in range(KT):
                add_square("0mix", 0, k)
            dve.wait_ge(S("bcast_landed"), 16 * n_bcast_dmas)
            for l in range(DEPTH):
                norm(f"{l}mix", 0)
                project(l)
                take_qk(l, 0)
                take_steps(l)
                own_read()
                steps_start(l)
                steps_one(l)
                take_qk(l, 1)
                steps_end(l)
                latents_mean(l)
                take_qk(l, 2)
                latents_norm(l)
                take_qk(l, 3)
                scan_start(l)
                latents_up(l)
                scan_states(l)
                rotate(l)
                scan_tiles(l)
                attention(l)
                add_mixed(l)
                norm(f"{l}ffn", P * FIRST_T[l])
                router(l)
                own_read()
                experts(l)
                add_experts(l, "1mix" if l == 0 else "final")
            norm("final", NCTX)
            for t in (2, 3):
                for half in range(2):
                    emptied(v.tensor_copy(tok[:, t, 512 * half:512 * half + 512], claim(f"out{t}{half}")))

        @block.scalar
        def _(act):
            a = nc.scalar.activation
            step = Tally(S("scalar_step"))

            def link(ins):
                act.wait_ge(step.sem, step.by(ins))

            def wait_evac(name):
                act.wait_ge(evacuated, entry[name] + 1)

            def rsqrt(dst, src, sem, scale=1.0, bias=0.0):
                link(a(dst, src, ACT.Ln, scale=scale, bias=bias))
                a(dst, dst, ACT.Exp, scale=-0.5).then_inc(sem, 1)

            def norm(name, c0, source, gains, shifts):
                if name in ("1mix", "final"):
                    for t in range(TT if name == "1mix" else NLAT // P):
                        t = t if name == "1mix" else NCTX // P + t
                        wait_evac(f"{source}{t}1")
                        cols = slice(P * t, P * t + P)
                        a(u[:, :, cols], h[:, :, cols], ACT.Square).then_inc(S("squares"), 1)
                for k in range(KT if name not in ("1mix", "final") else 0):
                    wait_evac("h31" if source is None else f"{source}{k}")
                    a(squares_of(name)[:, k, c0:T], h[:, k, c0:T], ACT.Square).then_inc(S("squares"), 1)
                wait_evac(f"ms{name}")
                rsqrt(rstd[:, c0:T], rstd[:, c0:T], S("rstd_ready"))
                if gains is not None:
                    act.wait_ge(S("gain_ready"), gains[0])
                for k in range(KT):
                    act.wait_ge(S("u_scaled"), eights[name] + k + 1)
                    if gains is None:
                        a(u[:, k, c0:T], u[:, k, c0:T], ACT.Identity,
                          scale=vec[:, 0, V_FING + k:V_FING + k + 1]).then_inc(S("u_ready"), 1)
                    else:
                        for s in range(c0 // NCTX, 2):
                            cols = u[:, k, NCTX * s:NCTX * s + NCTX]
                            a(cols, cols, ACT.Identity, scale=gains[1][:, k, s:s + 1],
                              bias=shifts[:, k, s:s + 1]).then_inc(S("u_ready"), 1)

            def project(l):
                for m in range(6):
                    act.wait_ge(filled, entry[f"xbc{l}{m}"] + 1)
                    c0 = first_column(l, "xbc", m)
                    a(xbc[:, m, c0:T], ps[:, entry[f"xbc{l}{m}"] % 2, 0:T - c0], ACT.Identity,
                      scale=vec[:, l, V_CONVW + 6 + m:V_CONVW + 7 + m],
                      bias=vec[:, l, V_CONVB + m:V_CONVB + m + 1]).then_inc(S("conv_mid"), 1)
                for m in range(6):
                    wait_evac(f"xbc{l}{m}")
                    c0 = first_column(l, "xbc", m)
                    a(xbc[:, m, c0:T], xbc[:, m, c0:T], ACT.Silu).then_inc(S("xbc_ready"), 1)
                for m in range(3):
                    wait_evac(f"lat{l}{m}")
                    c0 = first_column(l, "lat", m)
                    a(latent_sq[:, m, c0:T], latent[:, m, c0:T], ACT.Square).then_inc(S("latent_sq"), 1)

            def latents_mean(l):
                c0 = P * FIRST_T[l]
                wait_evac(f"cqms{l}")
                rsqrt(r_lat[:, 0, c0:T], r_lat[:, 0, c0:T], S("r_lat_ready"))
                wait_evac(f"ckvms{l}")
                rsqrt(r_lat[:, 1, :], r_lat[:, 1, :], S("r_lat_ready"))

            def steps(l):
                act.wait_ge(S("dt_abs"), l + 1)
                a(sc[:, 2, :], sc[:, 1, :], ACT.Exp, scale=-1.0).then_inc(S("dt_exp"), 1)
                link(a(sc[:, 7, 0:16], bcast[:, l, B_ALOG:B_ALOG + 16], ACT.Exp))
                act.wait_ge(S("dt_u"), l + 1)
                a(sc[:, 6, :], sc[:, 3, :], ACT.Ln).then_inc(S("dt_exp"), 1)

            def scan(l):
                act.wait_ge(S("cum_ready"), l + 1)
                a(sc[:, 3, :], sc[:, 8, :], ACT.Exp)
                a(sc[:, 4, :], sc[:, 9, :], ACT.Exp)
                a(sc[:, 5, :], sc[:, 10, :], ACT.Exp).then_inc(S("decays_ready"), 1)
                wait_evac(f"z{l}{TT - 1}")
                a(z[:, FIRST_T[l]:TT, :], z[:, FIRST_T[l]:TT, :], ACT.Silu).then_inc(S("z_ready"), 1)
                for i in range(TT - FIRST_T[l]):
                    for d in range(2):
                        act.wait_ge(S("decay_clamped", l), 2 * i + d + 1)
                        a(ew[:, d, :, :], ew[:, d, :, :], ACT.Exp).then_inc(S("decay_exp", l), 1)
                    act.wait_ge(S("y_gated", l), i + 1)
                    link(a(y_two, y_acc, ACT.Square, accum_out=small[:, 1:2]))
                    rsqrt(small[:, 0:1], small[:, 1:2], S("y_squared", l), 1.0 / SSD_INNER, small[:, 20:21])

            def attention(l):
                units = attention_units(l)
                mx, nb, rs, rr = (stats[:, s] for s in range(4))
                act.wait_ge(S("lam_sums"), l + 1)
                a(small[:, 6:8], small[:, 4:6], ACT.Exp).then_inc(S("lam_exp"), 1)
                for s in range(len(units) - DA_H + LAG_OUT + 1):
                    if s < len(units):
                        kind, t, hh, nk = units[s]
                        nm = 2 if kind == "da" else 1
                        act.wait_ge(S("max_ready"), units0 * l + s + 1)
                        if s >= 3:
                            act.wait_ge(S("probs_turned"), units0 * l + s - 2)
                        for m in range(nm):
                            last = a(probs[:, s % 3, m, 0:nk], ps[:, 2 + 2 * (s % 2) + m, 0:nk], ACT.Exp,
                                     scale=DA_SCALE if kind == "da" else MLA_SCALE, bias=nb[:, s, m:m + 1],
                                     accum_out=rs[:, s, m:m + 1])
                        last.then_inc(S("exp_done"), 1)
                    n = s - 2
                    if 0 <= n < len(units):
                        nk = units[n][3]
                        act.wait_ge(S("probs_turned"), units0 * l + n + 1)
                        if n >= 2:
                            act.wait_ge(S("heads_done"), units0 * l + n - 1)
                        nc.scalar.copy(probs_t[:, n % 2, 0:nk // P, :],
                                       ps[:, 6 + n % 2, 0:nk].rearrange("p (k q) -> p k q", q=P)).then_inc(
                            S("probs_t_ready"), 1)
                    g = head_part(s, LAG_OUT)
                    if g is not None and units[DA_H * g][0] == "da":
                        t = units[DA_H * g][1]
                        act.wait_ge(S("o_squared"), units0 // 8 * l + t - FIRST_T[l] + 1)
                        rsqrt(small[:, 12:16], small[:, 12:16], S("o_rstd"), 1.0 / DA_V, small[:, 20:21])

            def experts(l):
                f = FIRST_T[l]
                wait_evac(f"logits{l}")
                lg, aff = rt[:, 0, f:TT, :], rt[:, 1, f:TT, :]
                a(aff, lg, ACT.Exp, scale=-1.0).then_inc(S("logits_exp"), 1)
                for t in range(f, TT):
                    for half in range(2):
                        act.wait_ge(S("ut_turned"), ut_count(l, t, half) + 1)
                        nc.scalar.copy(u_tok[:, t, 512 * half:512 * half + 512],
                                       ps[:, 2 + half, :]).then_inc(S("ut_taken"), 1)
                    if t == TT - 1:
                        break
                    act.wait_ge(S("ut_taken"), ut_count(l, t, 1) + 1)
                    act.dma_start(u_rows[l][P * (t - f):P * (t - f) + P, :], u_tok[:, t, :]).then_inc(
                        S("u_stored", l), 16)
                act.wait_ge(S("passes_ready"), l + 1)
                n_more = nc.scalar.value_load(passes[0:1, l:l + 1], min_val=0, max_val=TT - 1)
                with act.Fori(0, n_more + 1) as p:
                    def copy_x(q, n, half):
                        act.wait_ge(S("x_turned", l), p * (2 * NE) + q * (2 * GROUP) + (2 * n + half + 1))
                        nc.scalar.copy(x_t[:, n % 2, 4 * half:4 * half + 4, :],
                                       ps[:, 4, :].rearrange("p (k s) -> p k s", s=P)).then_inc(S("x_t_ready", l), 1)

                    def silu(q, n):
                        act.wait_ge(S("gate_done", l), p * NE + q * GROUP + (n + 1))
                        a(silu_g, ps[:, 2 * (n % 2), :], ACT.Silu).then_inc(S("silu_done", l), 1)

                    def copy_hidden(q, n):
                        act.wait_ge(S("hid_turned", l), p * NE + q * GROUP + (n + 1))
                        nc.scalar.copy(hid_t, ps[:, 5, :].rearrange("p (f s) -> p f s", s=P)).then_inc(
                            S("hid_t_ready", l), 1)

                    def step(q, n):
                        silu(q, n + 1)
                        if n + 2 < NE:
                            copy_x(q, n + 2, 0)
                            copy_x(q, n + 2, 1)
                        copy_hidden(q, n + 1)

                    copy_x(0, 0, 0)
                    copy_x(0, 0, 1)
                    silu(0, 0)
                    copy_x(0, 1, 0)
                    copy_x(0, 1, 1)
                    copy_hidden(0, 0)
                    with act.Fori(0, STEPS) as q:
                        for n in range(GROUP):
                            step(q, n)
                    for n in range(STEPS * GROUP, NE - 1):
                        step(0, n)
                act.wait_ge(S("all_scattered", l), 1)
                for t in range(f, TT):
                    for k, dst in enumerate((y_tok, y_tok2)):
                        act.dma_start(dst[:, t, :], y_rows[l][T * k + P * t:T * k + P * t + P, :]).then_inc(
                            S(f"y_back{t}", l), 16)

            act.dma_start(cst[:, :], consts).then_inc(S("const_landed"), 16)
            for dst, src in vec_loads:
                act.dma_start(dst, src).then_inc(S("const_landed"), 16)
            def load_up(l):
                act.dma_start(wuq[:, :, :], mla_w_uq[l].rearrange("(k p) n -> p k n", p=P)).then_inc(S("wu_landed"), 16)
                act.dma_start(wukv[:, :], mla_w_ukv[l]).then_inc(S("wu_landed"), 16)

            wait_evac("vecs")
            a(small[:, 32:48], vec[:, 0, V_CCTX:V_CCTX + 16], ACT.Exp, scale=-1.0).then_inc(S("cond_exp"), 1)
            for dst, src in bcast_loads:
                act.dma_start(dst, src).then_inc(S("bcast_landed"), 16)
            act.dma_start(rw[:, :, :], router_w.rearrange("(k p) e -> p k e", p=P)).then_inc(S("bcast_landed"), 16)
            load_up(0)
            gain_count = {(0, 0): 1, (0, 1): 2, (1, 0): 3, (1, 1): 4}
            for l in range(DEPTH):
                norm(f"{l}mix", 0, None if l == 0 else "y0", (gain_count[(l, 0)], gain[:, l, 0]), mod[:, l, 0:8, :])
                project(l)
                steps(l)
                latents_mean(l)
                scan(l)
                attention(l)
                if l == 0:
                    load_up(1)
                norm(f"{l}ffn", P * FIRST_T[l], f"mix{l}", (gain_count[(l, 1)], gain[:, l, 1]), mod[:, l, 24:32, :])
                experts(l)
            norm("final", NCTX, "y1", None, None)

        @block.gpsimd
        def _(pool):
            g = nc.gpsimd

            def hb(ap):
                return ap.unsqueeze(2).to_broadcast([P, SSD_H, SSD_P])

            def xs(t):
                return xbc[:, 0:4, P * t:P * t + P].rearrange("p m (a n) -> p m a n", a=2)

            def xb(ap):
                return ap.rearrange("p (m a) -> p m a", a=2).unsqueeze(3).to_broadcast([P, 4, 2, SSD_P])

            def experts(l):
                pool.sem_inc(S("scatters_ended", l), 1)
                pool.wait_ge(S("ut_taken"), ut_count(l, TT - 1, 1) + 1)
                g.dma_start(u_rows[l][P * (TT - 1 - FIRST_T[l]):P * (TT - FIRST_T[l]), :],
                            u_tok[:, TT - 1, :]).then_inc(S("scattered", l), 16)
                pool.wait_ge(S("passes_ready"), l + 1)
                n_more = g.value_load(passes[0:1, l:l + 1], min_val=0, max_val=TT - 1)
                pool.wait_ge(S("u_stored", l), 16 * (TT - FIRST_T[l] - 1))
                pool.wait_ge(S("scattered", l), 16)
                with pool.Fori(0, n_more + 1) as p:
                    def gather(q, n):
                        pool.wait_ge(S("lists_ready", l), p * (NE // GROUP) + q + (n // GROUP + 1))
                        if n >= GATHERS:
                            pool.wait_ge(S("x_turned", l), p * (2 * NE) + q * (2 * GROUP) + 2 * (n - GATHERS + 1))
                        alone(pool)
                        k = n % GROUP
                        g.tensor_copy(row_in_now[:, k:k + 1], row_in[:, bass.ds(q * GROUP + n, 1)]).then_inc(
                            S("row_in_copied", l), 1)
                        pool.wait_ge(S("row_in_copied", l), p * NE + q * GROUP + (n + 1))
                        alone(pool)
                        g.indirect_dma_start(x_slots[:, n % GATHERS, :], None, u_rows[l],
                                             bass.IndirectOffsetOnAxis(ap=row_in_now[:, k:k + 1], axis=0),
                                             bounds_check=P * (TT - FIRST_T[l]) - 1, oob_is_err=False).then_inc(
                            S(f"gathered{n % GATHERS}", l), 16)

                    def scatter(q, n):
                        pool.wait_ge(S("y_scaled", l), p * NE + q * GROUP + (n + 2))
                        alone(pool)
                        k = n % GROUP
                        g.tensor_copy(row_out_now[:, k:k + 1], row_out[:, bass.ds(q * GROUP + n, 1)]).then_inc(
                            S("row_out_copied", l), 1)
                        pool.wait_ge(S("row_out_copied", l), p * NE + q * GROUP + (n + 1))
                        pool.wait_ge(S("scattered", l), p * (16 * NE) + q * (16 * GROUP) + 16 * (n + 1))
                        pool.sem_inc(S("scatters_ended", l), 1)
                        g.indirect_dma_start(y_rows[l], bass.IndirectOffsetOnAxis(ap=row_out_now[:, k:k + 1], axis=0),
                                             y_slots[:, n % 2, :], None, bounds_check=2 * T - 1,
                                             oob_is_err=False).then_inc(S("scattered", l), 16)

                    for n in range(GATHERS):
                        gather(0, n)
                    with pool.Fori(0, STEPS) as q:
                        for n in range(GROUP):
                            gather(q, n + GATHERS)
                            scatter(q, n)
                    for n in range(STEPS * GROUP, NE):
                        if n + GATHERS < NE:
                            gather(0, n + GATHERS)
                        scatter(0, n)
                    pool.wait_ge(S("scattered", l), p * (16 * NE) + 16 * (NE + 1))
                    pool.sem_inc(S("scatters_ended", l), 1)
                pool.sem_inc(S("all_scattered", l), 1)
                for t in range(FIRST_T[l], TT):
                    pool.wait_ge(S(f"y_back{t}", l), 32)
                    g.tensor_tensor(y_tok[:, t, :], y_tok[:, t, :], y_tok2[:, t, :], ALU.add).then_inc(
                        S("y_combined", l), 1)

            for l in range(DEPTH):
                first = FIRST_T[l]
                pool.wait_ge(S("to_end_ready"), l + 1)
                for n, (d, t, _) in enumerate(state_steps(l)):
                    if n >= 2:
                        pool.wait_ge(filled, entry[f"state{l}{n - 2}"] + 1)
                    g.tensor_tensor(xdt[:, n % 2, :].rearrange("p (m a n) -> p m a n", m=4, a=2), xs(t),
                                    xb(sc[:, 5, 32 * d + 8 * t:32 * d + 8 * t + 8]), ALU.mult).then_inc(
                        S("xde_ready", l), 1)
                for i, t in enumerate(range(first, TT)):
                    for d in range(2):
                        if i:
                            pool.wait_ge(S("y_summed", l), i)
                        g.tensor_tensor(ew[:, d, :, :], tri[d].unsqueeze(1).to_broadcast([P, SSD_H, P]),
                                        sc[:, 2, 32 * d + 8 * t:32 * d + 8 * t + 8].unsqueeze(2).to_broadcast(
                                            [P, SSD_H, P]), ALU.mult).then_inc(S("rows_built", l), 1)
                    for d in range(2):
                        if i == 0:
                            pool.wait_ge(filled, entry[f"state{l}{len(state_steps(l)) - 1}"] + 1)
                        last = g.tensor_tensor(xdt[:, d, :].rearrange("p (m a n) -> p m a n", m=4, a=2), xs(t),
                                               xb(sc[:, 1, 32 * d + 8 * t:32 * d + 8 * t + 8]), ALU.mult)
                    if i:
                        pool.wait_ge(S("y_gated", l), i)
                    g.tensor_tensor(y_skip.rearrange("p (m a n) -> p m a n", m=4, a=2), xs(t),
                                    xb(bcast[:, l, B_D:B_D + 8]), ALU.mult).then_inc(S("skip_ready", l), 1)
                    pool.wait_ge(evacuated, entry[f"cb{l}{t}1"] + 1)
                    for d in range(2):
                        pool.wait_ge(S("decay_exp", l), 2 * i + d + 1)
                        for gg in range(2):
                            part = ew[:, d, 4 * gg:4 * gg + 4, :]
                            last = g.tensor_tensor(part, part, gm[:, d, gg, :].unsqueeze(1).to_broadcast([P, 4, P]),
                                                   ALU.mult)
                        last.then_inc(S("w_ready", l), 1)

                experts(l)

        @block.sync
        def _(sp):
            def chunk_source(key):
                kind, l, n, k = key
                if kind == "mod":
                    return [(2 * 2048, w_mod[l].rearrange("(k p) n -> p k n", p=P)[:, 2 * k:2 * k + 2,
                                                                                 2048 * n:2048 * n + 2048], 0, 2048)]
                w = w_in[l].rearrange("(k p) n -> p k n", p=P)
                if kind == "out":
                    return [(SLOT, w_out[l].rearrange("(k p) n -> p k n", p=P)[:, :, 512 * n:512 * n + 512], 0, 512)]
                if n == "bcv":
                    return [(SLOT, w[:, :, COL_BC:COL_BC + 256], 0, 512), (SLOT, w[:, :, COL_V:COL_V + 256], 256, 512)]
                col, width = IN_COLS[n]
                return [(KT * width, w[:, :, col:col + width], 0, width)]

            def load(i, key):
                if i >= RING:
                    sp.wait_ge(*released[i - RING])
                for total, src, a, row in chunk_source(key):
                    dst = ring[:, i % RING, 0:total].rearrange("p (k n) -> p k n", n=row)[:, :, a:a + src.shape[2]]
                    sp.dma_start(dst, src).then_inc(landed_sem(i), 16)

            def experts(l):
                base = moe_base[l]
                gate = exp_w_gate[l].rearrange("e (k p) n -> p e k n", p=P)
                up = exp_w_up[l].rearrange("e (k p) n -> p e k n", p=P)
                down = exp_w_down[l].rearrange("e (f p) n -> p e f n", p=P)
                readers = [S("gate_done", l), S("up_done", l), S("down_done", l)]

                per = GROUP * PER_EXPERT
                total = NE * PER_EXPERT

                def send(c, q):
                    kind, n = CHUNK_AT[c % total]
                    src, width = ((gate, DE), (up, DE), (down, DM))[kind]
                    slot = (base + c) % RING
                    sp.dma_start(ring[:, slot, :].rearrange("p (o k n) -> p o k n", o=1, n=width),
                                 src[:, bass.ds(q * GROUP + n, 1), :, :]).then_inc(landed[l][slot], 16)

                def wait_reader(c, p, q):
                    kind, n = CHUNK_AT[c - RING]
                    sp.wait_ge(readers[kind], p * NE + q * GROUP + (n + 1))

                for c in range(RING):
                    sp.wait_ge(*released[base + c - RING])
                    send(c, 0)

                def one_pass(p):
                    first = RING + 2
                    for c in range(RING, first):
                        wait_reader(c, p, 0)
                        send(c, 0)
                    with sp.Fori(0, STEPS) as q:
                        for c in range(first, first + per):
                            wait_reader(c, p, q)
                            send(c, q)
                    for c in range(first + STEPS * per, total):
                        wait_reader(c, p, 0)
                        send(c, 0)

                sp.wait_ge(S("passes_ready"), l + 1)
                n_more = nc.sync.value_load(passes[0:1, l:l + 1], min_val=0, max_val=TT - 1)
                with sp.If(n_more > 0):
                    with sp.Fori(0, n_more) as p:
                        one_pass(p)
                        for c in range(total, total + RING):
                            wait_reader(c, p, 0)
                            send(c, 0)
                one_pass(n_more)
                for c in range(total - RING, total):
                    kind, n = CHUNK_AT[c]
                    released[base + c] = (readers[kind], n_more * NE + (n + 1))

            for t in range(TT):
                tokens = (ctx if t < 2 else x).rearrange("b (t p) n -> p (b t) n", p=P)
                sp.dma_start(tok[:, t, :], tokens[:, t % 2, :]).then_inc(S("tokens_landed", t), 16)
            sp.wait_ge(S("const_landed"), 16 * (1 + n_vec_dmas))
            for i, key in enumerate(chunks):
                load(i, key)
            experts(0)
            for i, key in enumerate(after):
                load(second + i, key)
            experts(1)
            for t in (2, 3):
                for half in range(2):
                    sp.wait_ge(evacuated, entry[f"out{t}{half}"] + 1)
                    sp.dma_start(out.rearrange("b (t p) n -> p (b t) n", p=P)[:, t - 2, 512 * half:512 * half + 512],
                                 tok[:, t, 512 * half:512 * half + 512]).then_inc(S("out_stored"), 16)
            sp.wait_ge(S("out_stored"), 64)


_INS = ["x", "c", "ctx", "c_ctx", "norm_mix_g", "norm_ffn_g", "w_mod", "b_mod", "w_in", "w_out", "da_lambda",
        "da_subln_g", "ssd_conv_w", "ssd_conv_b", "ssd_dt_bias", "ssd_a_log", "ssd_d", "ssd_norm_g", "mla_q_norm_g",
        "mla_kv_norm_g", "mla_w_uq", "mla_w_ukv", "router_w", "router_bias", "exp_w_gate", "exp_w_up", "exp_w_down",
        "final_norm_g"]


def kernel(**inputs):
    import concourse.bacc as bacc
    from concourse.bass_utils import run_bass_kernel_spmd as run

    nc = bacc.Bacc("TRN2", target_bir_lowering=False, num_devices=1)
    arrays = {"in_constants": shape_constants()}
    args = [nc.dram_tensor("in_constants", (P, NCONST), F32, kind="ExternalInput").ap()]
    for name in _INS:
        a = np.ascontiguousarray(inputs[name])
        arrays[f"in_{name}"] = a
        args.append(nc.dram_tensor(f"in_{name}", a.shape, mybir.dt.from_np(a.dtype), kind="ExternalInput").ap())
    args.append(nc.dram_tensor("out_0", (1, NLAT, DM), F32, kind="ExternalOutput").ap())
    hybrid_dit_kernel(nc, *args)
    r = run(nc, [arrays], core_ids=[0])
    return r.results[0]["out_0"]
```
